# Optimizing a Trainium2 kernel written in Bass

```python
import jax, jax.numpy as jnp
from jax import lax
import numpy as np
import math

D_MODEL = 1024
BATCH = 1
SEQ = 512
DEPTH = 1

CHUNK = 64
EPS = 1e-6

POOL_WINDOWS = (2, 4, 8, 16)
POOL_WIDTH = D_MODEL
POOL_GROUP = POOL_WIDTH // len(POOL_WINDOWS)

LRU_WIDTH = D_MODEL
LRU_BLOCKS = 16
LRU_BLOCK = LRU_WIDTH // LRU_BLOCKS
CONV_WIDTH = 4
LRU_C = 8.0

SB_HEADS = 8
SB_HEAD_DIM = 128
SB_WIDTH = SB_HEADS * SB_HEAD_DIM
Q_BLOCK = 128

N_BRANCH = 3
IN_COLS = POOL_WIDTH + LRU_WIDTH + 3 * SB_WIDTH + N_BRANCH * D_MODEL
D_FF = ((8 * D_MODEL + 3 * 256 - 1) // (3 * 256)) * 256


def rms_norm(x, g):
    x32 = x.astype(jnp.float32)
    y = x32 * lax.rsqrt(jnp.mean(x32 * x32, axis=-1, keepdims=True) + EPS)
    return (y * g.astype(jnp.float32)).astype(x.dtype)

def pool_mixer(u, w_pool, pool_scale):
    S = u.shape[1]
    u32 = u.astype(jnp.float32)
    pos = jnp.arange(1, S + 1, dtype=jnp.float32)[None, :, None]
    outs = []
    for g, w in enumerate(POOL_WINDOWS):
        ug = u32[..., g * POOL_GROUP:(g + 1) * POOL_GROUP]
        cs = jnp.cumsum(ug, axis=1)
        cs_lag = jnp.pad(cs, ((0, 0), (w, 0), (0, 0)))[:, :S]
        mean = (cs - cs_lag) / jnp.minimum(pos, float(w))
        outs.append(mean - ug)
    p = jnp.stack(outs, axis=2).astype(u.dtype)
    y = jnp.einsum('bsgi,gij->bsgj', p, w_pool)
    return y.reshape(u.shape) * pool_scale

def rglru_mixer(u, conv_w, conv_b, w_rg, b_rg, w_ig, b_ig, lru_lambda):
    B, S, _ = u.shape
    up = jnp.pad(u, ((0, 0), (CONV_WIDTH - 1, 0), (0, 0)))
    xc = conv_b + conv_w[0] * up[:, 0:S]
    for k in range(1, CONV_WIDTH):
        xc = xc + conv_w[k] * up[:, k:k + S]
    xb = xc.reshape(B, S, LRU_BLOCKS, LRU_BLOCK)
    r = jax.nn.sigmoid(jnp.einsum('bshi,hij->bshj', xb, w_rg).reshape(B, S, LRU_WIDTH) + b_rg)
    i = jax.nn.sigmoid(jnp.einsum('bshi,hij->bshj', xb, w_ig).reshape(B, S, LRU_WIDTH) + b_ig)
    log_a = (-LRU_C * r.astype(jnp.float32)) * jax.nn.softplus(-lru_lambda.astype(jnp.float32))
    a = jnp.exp(log_a)
    mult = jnp.sqrt(-jnp.expm1(2.0 * log_a))
    b = mult * (i * xc).astype(jnp.float32)

    def combine(c1, c2):
        a1, b1 = c1
        a2, b2 = c2
        return a1 * a2, a2 * b1 + b2

    _, h = lax.associative_scan(combine, (a, b), axis=1)
    return h.astype(u.dtype)

def stick_breaking_attention(q, k, v):
    B, S, H, Dh = q.shape
    scale = Dh ** -0.5
    outs = []
    for start in range(0, S, Q_BLOCK):
        end = start + Q_BLOCK
        qb = q[:, start:end]
        kb = k[:, :end]
        vb = v[:, :end]
        z = jnp.einsum('bqhd,bkhd->bhqk', qb, kb).astype(jnp.float32) * scale
        qpos = jnp.arange(start, end)[:, None]
        kpos = jnp.arange(end)[None, :]
        causal = kpos < qpos
        log_beta = jax.nn.log_sigmoid(z)
        log_keep = jnp.where(causal, jax.nn.log_sigmoid(-z), 0.0)
        after = lax.cumsum(log_keep, axis=3, reverse=True) - log_keep
        w = jnp.where(causal, jnp.exp(log_beta + after), 0.0)
        outs.append(jnp.einsum('bhqk,bkhd->bqhd', w.astype(v.dtype), vb))
    return jnp.concatenate(outs, axis=1)

def first_inputs(seed: int = 0) -> dict:
    key = jax.random.key(seed)
    ks = jax.random.split(key, 24)
    f32 = jnp.float32
    nrm = lambda k, shape, s: jax.random.normal(k, shape, f32) * s
    u = jax.random.uniform(ks[13], (DEPTH, LRU_WIDTH), f32, minval=0.9, maxval=0.999)
    p = u ** (1.0 / LRU_C)
    lru_lambda = jnp.log(p) - jnp.log1p(-p)
    return {
        "x": nrm(ks[0], (BATCH, SEQ, D_MODEL), 1.0),
        "norm_mix": 1.0 + nrm(ks[1], (DEPTH, D_MODEL), 0.02),
        "w_in": nrm(ks[2], (DEPTH, D_MODEL, IN_COLS), D_MODEL ** -0.5),
        "b_gate": nrm(ks[3], (DEPTH, N_BRANCH * D_MODEL), 0.01),
        "w_pool": nrm(ks[4], (DEPTH, len(POOL_WINDOWS), POOL_GROUP, POOL_GROUP), POOL_GROUP ** -0.5),
        "pool_scale": 1.0 + nrm(ks[5], (DEPTH, POOL_WIDTH), 0.1),
        "conv_w": nrm(ks[6], (DEPTH, CONV_WIDTH, LRU_WIDTH), CONV_WIDTH ** -0.5),
        "conv_b": nrm(ks[7], (DEPTH, LRU_WIDTH), 0.01),
        "w_rg": nrm(ks[8], (DEPTH, LRU_BLOCKS, LRU_BLOCK, LRU_BLOCK), LRU_BLOCK ** -0.5),
        "b_rg": nrm(ks[9], (DEPTH, LRU_WIDTH), 0.01),
        "w_ig": nrm(ks[10], (DEPTH, LRU_BLOCKS, LRU_BLOCK, LRU_BLOCK), LRU_BLOCK ** -0.5),
        "b_ig": nrm(ks[11], (DEPTH, LRU_WIDTH), 0.01),
        "lru_lambda": lru_lambda,
        "q_norm": 1.0 + nrm(ks[14], (DEPTH, SB_HEAD_DIM), 0.02),
        "k_norm": 1.0 + nrm(ks[15], (DEPTH, SB_HEAD_DIM), 0.02),
        "w_branch": nrm(ks[16], (DEPTH, N_BRANCH, D_MODEL, D_MODEL), D_MODEL ** -0.5),
        "w_out": nrm(ks[17], (DEPTH, D_MODEL, D_MODEL), D_MODEL ** -0.5),
        "norm_ffn": 1.0 + nrm(ks[18], (DEPTH, D_MODEL), 0.02),
        "w_ffn_gate": nrm(ks[19], (DEPTH, D_MODEL, D_FF), D_MODEL ** -0.5),
        "w_ffn_up": nrm(ks[20], (DEPTH, D_MODEL, D_FF), D_MODEL ** -0.5),
        "w_ffn_down": nrm(ks[21], (DEPTH, D_FF, D_MODEL), D_FF ** -0.5),
    }

def first_block(x, norm_mix, w_in, b_gate, w_pool, pool_scale, conv_w, conv_b, w_rg, b_rg,
              w_ig, b_ig, lru_lambda, q_norm, k_norm, w_branch, w_out, norm_ffn,
              w_ffn_gate, w_ffn_up, w_ffn_down):
    B, S, _ = x.shape
    splits = np.cumsum([POOL_WIDTH, LRU_WIDTH, SB_WIDTH, SB_WIDTH, SB_WIDTH]).tolist()
    for l in range(DEPTH):
        h = rms_norm(x, norm_mix[l])
        proj = jnp.einsum('bsd,dc->bsc', h, w_in[l])
        u_pool, u_lru, q, k, v, g_logits = jnp.split(proj, splits, axis=-1)
        gates = jax.nn.sigmoid(g_logits + b_gate[l]).reshape(B, S, N_BRANCH, D_MODEL)

        y_pool = pool_mixer(u_pool, w_pool[l], pool_scale[l])
        y_lru = rglru_mixer(u_lru, conv_w[l], conv_b[l], w_rg[l], b_rg[l],
                            w_ig[l], b_ig[l], lru_lambda[l])
        qh = rms_norm(q.reshape(B, S, SB_HEADS, SB_HEAD_DIM), q_norm[l])
        kh = rms_norm(k.reshape(B, S, SB_HEADS, SB_HEAD_DIM), k_norm[l])
        vh = v.reshape(B, S, SB_HEADS, SB_HEAD_DIM)
        y_sb = stick_breaking_attention(qh, kh, vh).reshape(B, S, SB_WIDTH)

        merged = (gates[:, :, 0] * jnp.einsum('bsc,cd->bsd', y_pool, w_branch[l, 0])
                  + gates[:, :, 1] * jnp.einsum('bsc,cd->bsd', y_lru, w_branch[l, 1])
                  + gates[:, :, 2] * jnp.einsum('bsc,cd->bsd', y_sb, w_branch[l, 2]))
        x = x + jnp.einsum('bsd,de->bse', merged, w_out[l])

        h2 = rms_norm(x, norm_ffn[l])
        act = jax.nn.silu(jnp.einsum('bsd,df->bsf', h2, w_ffn_gate[l])) * jnp.einsum('bsd,df->bsf', h2, w_ffn_up[l])
        x = x + jnp.einsum('bsf,fd->bsd', act, w_ffn_down[l])
    return x


DEPTH_2 = 2

HEAD_DIM = 64
MOBA_HEADS = 8
MOBA_BLOCK = 256
MOBA_TOPK = 3
MOBA_QCHUNK = 16
DIFF_HEADS = 4
DIFF_HEAD_DIM = 64
DIL_HEADS = 8
DIL_CONFIGS = ((128, 1), (512, 4), (2048, 16))
DIL_BLOCK = 128
MLA_HEADS = 4
MLA_Q_RANK = 256
MLA_KV_RANK = 128
MLA_NOPE_DIM = 128
MLA_ROPE_DIM = 64
MLA_V_DIM = 128
ROPE_THETA = 10000.0
REL_BUCKETS = 32
REL_MAX_DIST = 1024
N_BIAS_HEADS = MOBA_HEADS + DIFF_HEADS + DIL_HEADS
D_FF_2 = 2816
CONV_WIDTH_2 = 3
NEG = -1e30
N_EVEN = (DEPTH_2 + 1) // 2
N_ODD = DEPTH_2 // 2
MOBA_W = MOBA_HEADS * HEAD_DIM
DIFF_QK_W = DIFF_HEADS * 2 * DIFF_HEAD_DIM
DIFF_V_W = DIFF_HEADS * 2 * DIFF_HEAD_DIM
EVEN_IN_SPLIT = (MOBA_W, MOBA_W, MOBA_W, DIFF_QK_W, DIFF_QK_W, DIFF_V_W)
EVEN_IN = sum(EVEN_IN_SPLIT)
EVEN_MIX = MOBA_W + DIFF_V_W
DIL_W = DIL_HEADS * HEAD_DIM
ODD_IN_SPLIT = (DIL_W, DIL_W, DIL_W, MLA_Q_RANK, MLA_KV_RANK, MLA_ROPE_DIM)
ODD_IN = sum(ODD_IN_SPLIT)
ODD_MIX = DIL_W + MLA_HEADS * MLA_V_DIM


def rmsnorm(x, g):
    xf = x.astype(jnp.float32)
    y = xf * lax.rsqrt(jnp.mean(xf * xf, axis=-1, keepdims=True) + EPS)
    return (y * g.astype(jnp.float32)).astype(x.dtype)

def split_cols(x, sizes):
    outs, off = [], 0
    for s in sizes:
        outs.append(x[..., off:off + s])
        off += s
    return outs

def heads(x, n, d):
    b, s, _ = x.shape
    return x.reshape(b, s, n, d).transpose(0, 2, 1, 3)

def merge_heads(o):
    b, h, s, d = o.shape
    return o.transpose(0, 2, 1, 3).reshape(b, s, h * d)

def rel_bucket(dist):
    max_exact = REL_BUCKETS // 2
    n = jnp.maximum(dist, 0)
    nf = jnp.maximum(n, 1).astype(jnp.float32)
    large = max_exact + (jnp.log(nf / max_exact) / math.log(REL_MAX_DIST / max_exact)
                         * (REL_BUCKETS - max_exact)).astype(jnp.int32)
    large = jnp.minimum(large, REL_BUCKETS - 1)
    return jnp.where(n < max_exact, n, large)

def rope(x, pos):
    half = x.shape[-1] // 2
    freq = ROPE_THETA ** (-jnp.arange(half, dtype=jnp.float32) / half)
    ang = pos.astype(jnp.float32)[:, None] * freq[None, :]
    cos, sin = jnp.cos(ang), jnp.sin(ang)
    xf = x.astype(jnp.float32)
    x1, x2 = xf[..., :half], xf[..., half:]
    return jnp.concatenate([x1 * cos - x2 * sin, x1 * sin + x2 * cos], axis=-1).astype(x.dtype)

def moba_attention(q, k, v, bias_table):
    B, H, S, dh = q.shape
    blk = MOBA_BLOCK
    sp = -(-S // blk) * blk
    if sp != S:
        padw = ((0, 0), (0, 0), (0, sp - S), (0, 0))
        q, k, v = jnp.pad(q, padw), jnp.pad(k, padw), jnp.pad(v, padw)
    nb = sp // blk
    n_sel = min(MOBA_TOPK, nb - 1)
    scale = dh ** -0.5
    kb = k.reshape(B, H, nb, blk, dh)
    vb = v.reshape(B, H, nb, blk, dh)
    qblk = jnp.arange(sp) // blk
    table_t = bias_table.T
    head_ix = jnp.arange(H)[None, :, None, None, None]
    if n_sel > 0:
        kmean = jnp.mean(kb.astype(jnp.float32), axis=3)
        gate = jnp.einsum('bhsd,bhnd->bhsn', q.astype(jnp.float32), kmean)
        fully_past = jnp.arange(nb)[None, :] < qblk[:, None]
        gate = jnp.where(fully_past, gate, -jnp.inf)
        _, sel = lax.top_k(gate, n_sel)
        sel_ok = sel < qblk[:, None]
    gather_blocks = jax.vmap(jax.vmap(lambda xb, ix: xb[ix]))

    def chunk(c):
        start = c * MOBA_QCHUNK
        qc = lax.dynamic_slice_in_dim(q, start, MOBA_QCHUNK, axis=2)
        qpos = start + jnp.arange(MOBA_QCHUNK)
        own = start // blk
        k_own = lax.dynamic_index_in_dim(kb, own, axis=2, keepdims=False)
        v_own = lax.dynamic_index_in_dim(vb, own, axis=2, keepdims=False)
        dist_own = qpos[:, None] - (own * blk + jnp.arange(blk))[None, :]
        b_own = jnp.moveaxis(jnp.take(bias_table, rel_bucket(dist_own), axis=0), -1, 0)
        s_own = jnp.einsum('bhqd,bhkd->bhqk', qc, k_own).astype(jnp.float32) * scale + b_own
        s_own = jnp.where(dist_own >= 0, s_own, NEG)
        if n_sel == 0:
            p = jax.nn.softmax(s_own, axis=-1).astype(v.dtype)
            return jnp.einsum('bhqk,bhkd->bhqd', p, v_own)
        sel_c = lax.dynamic_slice_in_dim(sel, start, MOBA_QCHUNK, axis=2)
        ok_c = lax.dynamic_slice_in_dim(sel_ok, start, MOBA_QCHUNK, axis=2)
        flat = sel_c.reshape(B, H, MOBA_QCHUNK * n_sel)
        k_sel = gather_blocks(kb, flat).reshape(B, H, MOBA_QCHUNK, n_sel, blk, dh)
        v_sel = gather_blocks(vb, flat).reshape(B, H, MOBA_QCHUNK, n_sel, blk, dh)
        s_sel = jnp.einsum('bhqd,bhqnkd->bhqnk', qc, k_sel).astype(jnp.float32) * scale
        dist_sel = qpos[None, None, :, None, None] - (sel_c[..., None] * blk + jnp.arange(blk))
        s_sel = s_sel + table_t[head_ix, rel_bucket(dist_sel)]
        s_sel = jnp.where(ok_c[..., None], s_sel, NEG)
        s = jnp.concatenate([s_own, s_sel.reshape(B, H, MOBA_QCHUNK, n_sel * blk)], axis=-1)
        p = jax.nn.softmax(s, axis=-1).astype(v.dtype)
        p_own = p[..., :blk]
        p_sel = p[..., blk:].reshape(B, H, MOBA_QCHUNK, n_sel, blk)
        return (jnp.einsum('bhqk,bhkd->bhqd', p_own, v_own)
                + jnp.einsum('bhqnk,bhqnkd->bhqd', p_sel, v_sel))

    o = lax.map(chunk, jnp.arange(sp // MOBA_QCHUNK))
    o = jnp.moveaxis(o, 0, 2).reshape(B, H, sp, dh)
    return o[:, :, :S]

def diff_attention(q, k, v, lam, subln_g, lam_init, bias_table):
    B, H, _, S, dh = q.shape
    scale = dh ** -0.5
    kpos = jnp.arange(S)

    def block(i):
        qb = lax.dynamic_slice_in_dim(q, i * Q_BLOCK, Q_BLOCK, axis=3)
        qpos = i * Q_BLOCK + jnp.arange(Q_BLOCK)
        dist = qpos[:, None] - kpos[None, :]
        bias = jnp.moveaxis(jnp.take(bias_table, rel_bucket(dist), axis=0), -1, 0)
        s = jnp.einsum('bhcqd,bhckd->bhcqk', qb, k).astype(jnp.float32) * scale
        s = jnp.where(dist >= 0, s + bias[None, :, None], NEG)
        p = jax.nn.softmax(s, axis=-1)
        a = (p[:, :, 0] - lam * p[:, :, 1]).astype(v.dtype)
        return jnp.einsum('bhqk,bhkd->bhqd', a, v)

    o = lax.map(block, jnp.arange(S // Q_BLOCK))
    o = jnp.moveaxis(o, 0, 2).reshape(B, H, S, 2 * dh)
    return rmsnorm(o, subln_g) * (1.0 - lam_init)

def dilated_attention(q, k, v, bias_table):
    B, H, S, dh = q.shape
    blk = DIL_BLOCK
    scale = dh ** -0.5
    qi = jnp.arange(blk)
    kj = jnp.arange(2 * blk) - blk
    step = qi[:, None] - kj[None, :]
    outs, lses = [], []
    for window, dil in DIL_CONFIGS:
        span = window // dil
        L = S // dil
        lp = -(-L // blk) * blk
        nblk = lp // blk

        def strided(x):
            x = x.reshape(B, H, L, dil, dh).transpose(0, 1, 3, 2, 4)
            x = jnp.pad(x, ((0, 0), (0, 0), (0, 0), (0, lp - L), (0, 0)))
            return x.reshape(B, H, dil, nblk, blk, dh)

        def band(x):
            prev = jnp.pad(x, ((0, 0), (0, 0), (0, 0), (1, 0), (0, 0), (0, 0)))[:, :, :, :-1]
            return jnp.concatenate([prev, x], axis=4)

        qb = strided(q)
        kband = band(strided(k))
        vband = band(strided(v))
        s = jnp.einsum('bhrnqd,bhrnkd->bhrnqk', qb, kband).astype(jnp.float32) * scale
        bias = jnp.moveaxis(jnp.take(bias_table, rel_bucket(step * dil), axis=0), -1, 0)
        key_exists = (jnp.arange(nblk)[:, None] * blk + kj[None, :]) >= 0
        mask = ((step >= 0) & (step <= span))[None] & key_exists[:, None, :]
        s = jnp.where(mask, s + bias[None, :, None, None], NEG)
        m = jnp.max(s, axis=-1, keepdims=True)
        e = jnp.exp(s - m)
        den = jnp.sum(e, axis=-1, keepdims=True)
        o = jnp.einsum('bhrnqk,bhrnkd->bhrnqd', (e / den).astype(v.dtype), vband)
        lse = (m + jnp.log(den))[..., 0]
        o = o.reshape(B, H, dil, lp, dh)[:, :, :, :L].transpose(0, 1, 3, 2, 4).reshape(B, H, S, dh)
        lse = lse.reshape(B, H, dil, lp)[:, :, :, :L].transpose(0, 1, 3, 2).reshape(B, H, S)
        outs.append(o)
        lses.append(lse)
    wts = jax.nn.softmax(jnp.stack(lses, axis=0), axis=0)
    return jnp.einsum('gbhs,gbhsd->bhsd', wts.astype(v.dtype), jnp.stack(outs, axis=0))

def mla_attention(q_nope, q_rope, k_nope, k_rope, v):
    B, H, S, _ = q_nope.shape
    scale = (MLA_NOPE_DIM + MLA_ROPE_DIM) ** -0.5
    kpos = jnp.arange(S)

    def block(i):
        qn = lax.dynamic_slice_in_dim(q_nope, i * Q_BLOCK, Q_BLOCK, axis=2)
        qr = lax.dynamic_slice_in_dim(q_rope, i * Q_BLOCK, Q_BLOCK, axis=2)
        qpos = i * Q_BLOCK + jnp.arange(Q_BLOCK)
        s = (jnp.einsum('bhqd,bhkd->bhqk', qn, k_nope)
             + jnp.einsum('bhqd,bkd->bhqk', qr, k_rope)).astype(jnp.float32) * scale
        s = jnp.where(qpos[:, None] >= kpos[None, :], s, NEG)
        p = jax.nn.softmax(s, axis=-1).astype(v.dtype)
        return jnp.einsum('bhqk,bhkd->bhqd', p, v)

    o = lax.map(block, jnp.arange(S // Q_BLOCK))
    return jnp.moveaxis(o, 0, 2).reshape(B, H, S, MLA_V_DIM)

def even_mixer(h, w_in, lam_params, subln_g, w_out, rel_table, lam_init):
    B, S, _ = h.shape
    qa, ka, va, qd, kd, vd = split_cols(h @ w_in, EVEN_IN_SPLIT)
    o_a = moba_attention(heads(qa, MOBA_HEADS, HEAD_DIM), heads(ka, MOBA_HEADS, HEAD_DIM),
                         heads(va, MOBA_HEADS, HEAD_DIM), rel_table[:, :MOBA_HEADS])
    qd = qd.reshape(B, S, DIFF_HEADS, 2, DIFF_HEAD_DIM).transpose(0, 2, 3, 1, 4)
    kd = kd.reshape(B, S, DIFF_HEADS, 2, DIFF_HEAD_DIM).transpose(0, 2, 3, 1, 4)
    vd = heads(vd, DIFF_HEADS, 2 * DIFF_HEAD_DIM)
    lp = lam_params.astype(jnp.float32)
    lam = jnp.exp(jnp.sum(lp[0] * lp[1])) - jnp.exp(jnp.sum(lp[2] * lp[3])) + lam_init
    o_b = diff_attention(qd, kd, vd, lam, subln_g, lam_init,
                         rel_table[:, MOBA_HEADS:MOBA_HEADS + DIFF_HEADS])
    return jnp.concatenate([merge_heads(o_a), merge_heads(o_b)], axis=-1) @ w_out

def odd_mixer(h, w_in, q_norm, w_uq, kv_norm, w_ukv, w_out, rel_table):
    B, S, _ = h.shape
    qc, kc, vc, cq, ckv, kr = split_cols(h @ w_in, ODD_IN_SPLIT)
    o_c = dilated_attention(heads(qc, DIL_HEADS, HEAD_DIM), heads(kc, DIL_HEADS, HEAD_DIM),
                            heads(vc, DIL_HEADS, HEAD_DIM), rel_table[:, MOBA_HEADS + DIFF_HEADS:])
    pos = jnp.arange(S)
    q = heads(rmsnorm(cq, q_norm) @ w_uq, MLA_HEADS, MLA_NOPE_DIM + MLA_ROPE_DIM)
    q_nope, q_rope = q[..., :MLA_NOPE_DIM], rope(q[..., MLA_NOPE_DIM:], pos)
    kv = heads(rmsnorm(ckv, kv_norm) @ w_ukv, MLA_HEADS, MLA_NOPE_DIM + MLA_V_DIM)
    k_nope, v = kv[..., :MLA_NOPE_DIM], kv[..., MLA_NOPE_DIM:]
    o_d = mla_attention(q_nope, q_rope, k_nope, rope(kr, pos), v)
    return jnp.concatenate([merge_heads(o_c), merge_heads(o_d)], axis=-1) @ w_out

def conv_ffn(h, w_in, conv_w, conv_b, w_out):
    u, g = jnp.split(h @ w_in, 2, axis=-1)
    g = lax.conv_general_dilated(g, conv_w[:, None, :], window_strides=(1,),
                                 padding=[(CONV_WIDTH_2 - 1, 0)],
                                 dimension_numbers=('NWC', 'WIO', 'NWC'),
                                 feature_group_count=D_FF_2) + conv_b
    return (jax.nn.gelu(g, approximate=False) * u) @ w_out

def second_inputs(seed: int = 0) -> dict:
    key = jax.random.key(seed)
    ks = jax.random.split(key, 20)
    f32 = jnp.float32

    def w(k, shape, fan_in):
        return jax.random.normal(k, shape, f32) * (fan_in ** -0.5)

    def gain(k, shape):
        return 1.0 + 0.02 * jax.random.normal(k, shape, f32)

    return {
        'x': jax.random.normal(ks[0], (BATCH, SEQ, D_MODEL), f32),
        'rel_bias': 0.2 * jax.random.normal(ks[1], (REL_BUCKETS, N_BIAS_HEADS), f32),
        'even_norm1': gain(ks[2], (N_EVEN, D_MODEL)),
        'even_w_in': w(ks[3], (N_EVEN, D_MODEL, EVEN_IN), D_MODEL),
        'diff_lambda': 0.1 * jax.random.normal(ks[4], (N_EVEN, 4, DIFF_HEAD_DIM), f32),
        'diff_subln': gain(ks[5], (N_EVEN, 2 * DIFF_HEAD_DIM)),
        'even_w_out': w(ks[6], (N_EVEN, EVEN_MIX, D_MODEL), EVEN_MIX),
        'odd_norm1': gain(ks[7], (N_ODD, D_MODEL)),
        'odd_w_in': w(ks[8], (N_ODD, D_MODEL, ODD_IN), D_MODEL),
        'mla_q_norm': gain(ks[9], (N_ODD, MLA_Q_RANK)),
        'mla_w_uq': w(ks[10], (N_ODD, MLA_Q_RANK, MLA_HEADS * (MLA_NOPE_DIM + MLA_ROPE_DIM)), MLA_Q_RANK),
        'mla_kv_norm': gain(ks[11], (N_ODD, MLA_KV_RANK)),
        'mla_w_ukv': w(ks[12], (N_ODD, MLA_KV_RANK, MLA_HEADS * (MLA_NOPE_DIM + MLA_V_DIM)), MLA_KV_RANK),
        'odd_w_out': w(ks[13], (N_ODD, ODD_MIX, D_MODEL), ODD_MIX),
        'ffn_norm': gain(ks[14], (DEPTH_2, D_MODEL)),
        'ffn_w_in': w(ks[15], (DEPTH_2, D_MODEL, 2 * D_FF_2), D_MODEL),
        'ffn_conv_w': w(ks[16], (DEPTH_2, CONV_WIDTH_2, D_FF_2), CONV_WIDTH_2),
        'ffn_conv_b': 0.02 * jax.random.normal(ks[17], (DEPTH_2, D_FF_2), f32),
        'ffn_w_out': w(ks[18], (DEPTH_2, D_FF_2, D_MODEL), D_FF_2),
        'final_norm': gain(ks[19], (D_MODEL,)),
    }

def second_block(x, rel_bias, even_norm1, even_w_in, diff_lambda, diff_subln, even_w_out,
              odd_norm1, odd_w_in, mla_q_norm, mla_w_uq, mla_kv_norm, mla_w_ukv, odd_w_out,
              ffn_norm, ffn_w_in, ffn_conv_w, ffn_conv_b, ffn_w_out, final_norm):
    h = x
    for layer in range(DEPTH_2):
        i = layer // 2
        if layer % 2 == 0:
            lam_init = 0.8 - 0.6 * math.exp(-0.3 * layer)
            h = h + even_mixer(rmsnorm(h, even_norm1[i]), even_w_in[i], diff_lambda[i],
                               diff_subln[i], even_w_out[i], rel_bias, lam_init)
        else:
            h = h + odd_mixer(rmsnorm(h, odd_norm1[i]), odd_w_in[i], mla_q_norm[i], mla_w_uq[i],
                              mla_kv_norm[i], mla_w_ukv[i], odd_w_out[i], rel_bias)
        h = h + conv_ffn(rmsnorm(h, ffn_norm[layer]), ffn_w_in[layer], ffn_conv_w[layer],
                         ffn_conv_b[layer], ffn_w_out[layer])
    return rmsnorm(h, final_norm)


def setup_inputs(seed=0):
    out = dict(first_inputs(seed))
    for name, value in second_inputs(seed + 1).items():
        if name != "x":
            out[name + "_2"] = value
    return out


def reference(
    x, norm_mix, w_in, b_gate, w_pool, pool_scale, conv_w, conv_b, w_rg, b_rg, w_ig, b_ig,
    lru_lambda, q_norm, k_norm, w_branch, w_out, norm_ffn, w_ffn_gate, w_ffn_up, w_ffn_down,
    rel_bias_2, even_norm1_2, even_w_in_2, diff_lambda_2, diff_subln_2, even_w_out_2,
    odd_norm1_2, odd_w_in_2, mla_q_norm_2, mla_w_uq_2, mla_kv_norm_2, mla_w_ukv_2, odd_w_out_2,
    ffn_norm_2, ffn_w_in_2, ffn_conv_w_2, ffn_conv_b_2, ffn_w_out_2, final_norm_2,
):
    x = first_block(
        x, norm_mix, w_in, b_gate, w_pool, pool_scale, conv_w, conv_b, w_rg, b_rg, w_ig, b_ig,
        lru_lambda, q_norm, k_norm, w_branch, w_out, norm_ffn, w_ffn_gate, w_ffn_up, w_ffn_down,
    )
    return second_block(
        x, rel_bias_2, even_norm1_2, even_w_in_2, diff_lambda_2, diff_subln_2, even_w_out_2,
        odd_norm1_2, odd_w_in_2, mla_q_norm_2, mla_w_uq_2, mla_kv_norm_2, mla_w_ukv_2,
        odd_w_out_2, ffn_norm_2, ffn_w_in_2, ffn_conv_w_2, ffn_conv_b_2, ffn_w_out_2,
        final_norm_2,
    )


_drawn_inputs = setup_inputs


def setup_inputs(seed=0):
    import zlib

    import numpy as np

    out = dict(_drawn_inputs(seed))
    spreads = {}
    factors = {'norm_mix': 3.035,
     'b_gate': 8.0,
     'b_rg': 8.0,
     'b_ig': 8.0,
     'q_norm': 8.0,
     'k_norm': 8.0,
     'norm_ffn': 3.776,
     'even_norm1_2': 4.173,
     'diff_subln_2': 5.131,
     'odd_norm1_2': 8.0,
     'mla_q_norm_2': 8.0,
     'mla_kv_norm_2': 8.0,
     'ffn_norm_2': 3.43,
     'ffn_conv_b_2': 4.972}
    for name, (base, spread) in spreads.items():
        noise = np.random.default_rng([zlib.crc32(name.encode()), seed]).standard_normal(out[name].shape)
        drawn = base * np.exp(spread * noise) if base else spread * noise
        out[name] = __import__('jax').numpy.asarray(drawn.astype(out[name].dtype))
    for name, factor in factors.items():
        out[name] = (out[name] * factor).astype(out[name].dtype)
    return out
```

```python
from contextlib import ExitStack
import math

import numpy as np

import concourse.bass as bass
from concourse import mybir

F32 = mybir.dt.float32
F32R = mybir.dt.float32r
ALU = mybir.AluOpType
ACT = mybir.ActivationFunctionType
AX = mybir.AxisListType

P = 128
S = 512
D = 1024
KT = D // P
NB = S // P
FF = 2816
FT = FF // P
HALF = FT // 2
EPS = 1e-6
CHUNK = KT * 2 * P
DOWN = HALF * P
NEG = -1e30
TW = 640
WINDOWS = (2, 4, 8, 16)
LAM_INIT = 0.8 - 0.6 * math.exp(-0.3 * 0)
MASK_ROW = 20
ROWS = 21

STAGES = [("qk", 8, 0), ("v", 4, 0), ("gate2", 8, 0), ("pool", 4, 0), ("wpool", 2, 0), ("gate0", 8, 0),
          ("lru", 4, 0), ("gate1", 8, 0), ("out", 4, 0), ("ffn0", FT, 0), ("down0", 16, 1),
          ("eqk", 8, 0), ("ev", 4, 0), ("eout", 4, 0), ("ffn1", FT, 0), ("down1", 16, 1),
          ("oqk", 6, 0), ("ov", 2, 0), ("mla", 2, 0), ("oout", 4, 0), ("ffn2", FT, 0), ("down2", 16, 1)]
BASE, WHERE, COUNT = {}, {}, {name: count for name, count, _ in STAGES}
_n, _in = 0, [0, 0]
for _name, _count, _kind in STAGES:
    BASE[_name], WHERE[_name] = _n, _in[_kind]
    _n, _in[_kind] = _n + _count, _in[_kind] + _count
CHUNKS = _n
MAIN, DOWNS = _in

COLS = {}
_at = 0
for _name, _k in [("norm_mix", 8), ("b_gate", 24), ("pool_scale", 8), ("conv_w", 32), ("conv_b", 8), ("b_rg", 8),
                  ("b_ig", 8), ("lru_lambda", 8), ("qk_norm", 16), ("norm_ffn", 8), ("even_norm", 8),
                  ("odd_norm", 8), ("mla_q_norm", 2), ("mla_kv_norm", 1), ("ffn_norm", 16), ("final", 8),
                  ("ffn_b", 2 * FT), ("ffn_w", 6 * FT), ("subln", 8), ("one_scale", 16), ("even_scale", 16),
                  ("odd_scale", 12), ("subln_factor", 8), ("edge", 64)]:
    COLS[_name] = _at
    _at += _k
NCOL = _at


def program(nc, wmain, wdown, xin, cols_in, mats_in, rg_in, rope_in, onehot_in, add_in, rel_in, lam_in, out, table):
    base = nc.sbuf_base + 31 & ~31
    top = [base]

    def place(name, shape, dt=F32, at=None):
        size = int(np.prod(shape[1:])) * 4
        if at is None:
            at = top[0]
            top[0] += size + 31 & ~31
        return nc.alloc_sbuf_tensor_at(name, shape, dt, offset=at)

    raw = place("raw", [P, 2, CHUNK])
    wh = place("w_high", [P, 2, CHUNK], F32R)
    wl = place("w_low", [P, 2, CHUNK], F32R)
    xT = place("x_residual", [P, KT, S])
    xh = place("x_high", [P, KT, S], F32R)
    xl = place("x_low", [P, KT, S], F32R)
    cols = place("columns", [P, NCOL])
    mats = place("matrices", [P, 7, P])
    ones, ident, negtri, negones, negmask, mask01, small_rot = (mats[:, j, :] for j in range(7))
    rstd = place("rstd", [P, S])
    tmpa = place("temp_a", [P, 2, S])
    tmpb = place("temp_b", [P, 2, S])
    small = place("small", [P, 128])
    arena = top[0]
    T = S * 4

    def over(name, shape, tile, dt=F32):
        return place(name, shape, dt, at=arena + int(tile * T))

    ah = over("act_high", [P, FT, S], 0, F32R)
    al = over("act_low", [P, FT, S], FT, F32R)
    qk = over("qk", [P, 16, S], 0)
    vt = over("v_tokens", [P, NB, D], 16)
    yh = over("y_high", [P, KT, S], 8, F32R)
    yl = over("y_low", [P, KT, S], 16, F32R)
    merged = over("merged", [P, KT, S], 24)
    sp = over("softplus", [P, NB, S], 32)
    wz = over("sb_weights", [P, NB, S], 36)
    ks = over("k_stage", [P, S], 40)
    vs = over("v_stage", [P, NB, P], 41)
    pu = over("pool_u", [P, 2, 16 + S], 32)
    pa = over("pool_a", [P, 2, 16 + S], 35)
    rgw = over("rg_blocks", [P, 16, P], 38)
    xc = over("conv_out", [P, 2, S], 0)
    rr = over("r_gate", [P, 2, S], 2)
    ii = over("i_gate", [P, 2, S], 4)
    aa = over("decay", [P, 2, S], 6)
    yt = over("y_tokens", [P, NB, D], 24)
    tq = over("probs", [P, NB, S], 32)
    pts = over("probs_t", [P, 2, S], 36)
    qs = over("q_stage", [P, 2, S], 38)
    bt = over("bias", [P, 2, S], 40)
    rope = over("rope", [P, 2, S], 42)
    ch = over("c_high", [P, 3, S], 32, F32R)
    cl = over("c_low", [P, 3, S], 35, F32R)
    oh = over("onehot", [32, TW], 24)
    ad = over("table_add", [ROWS, TW], 26)
    tt = over("table", [ROWS, TW], 28)
    rb = over("rel_bias", [32, ROWS + 3], 30)
    lamb = over("lambda_rows", [P, 4, 64], 31)
    assert arena + 44 * T <= nc.sbuf_usable_end, (arena + 44 * T, nc.sbuf_usable_end)

    nm = small[:, 0:8].rearrange("p (u q) -> p u q", u=2)
    rs = small[:, 8:16].rearrange("p (u q) -> p u q", u=2)
    rd = small[:, 16:24].rearrange("p (u q) -> p u q", u=2)
    dss = small[:, 24:40].rearrange("p (q h) -> p q h", q=NB)
    nlam = small[:, 40:41]
    decay8 = small[:, 48:56]
    ndecay8 = small[:, 56:64]
    t1, t2, t3, t4 = (small[:, 64 + 8 * j:72 + 8 * j] for j in range(4))
    lam2 = small[:, 96:98]

    with ExitStack() as ctx:
        names = {}

        def sem(name):
            if name not in names:
                names[name] = ctx.enter_context(nc.semaphore(name))
            return names[name]

        bank = [ctx.enter_context(nc.psum_tensor(f"bank{b}", [P, S], F32)) for b in range(8)]

        raw_landed = [sem("raw_landed_0"), sem("raw_landed_1")]
        high_ready, low_ready = sem("high_ready"), sem("low_ready")
        inputs_landed = sem("inputs_landed")
        table_ready, table_stored = sem("table_ready"), sem("table_stored")
        out_stored = sem("out_stored")

        class Steps:

            def __init__(self, eng, semaphore):
                self.eng, self.semaphore, self.n, self.here = eng, semaphore, 0, 0

            def __call__(self, instruction):
                self.here += 1
                self.n = self.n + 1
                instruction.then_inc(self.semaphore, 1)
                self.eng.wait_ge(self.semaphore, self.n)

        def repeat(eng, rounds, steps=None, per=0):
            first = steps.n if steps else 0
            with eng.Fori(0, rounds) as i:
                if steps:
                    steps.n, steps.here = i * per + first, 0
                yield i
                assert not steps or steps.here == per, (steps.here, per)
            if steps:
                steps.n = first + rounds * per

        def col(name, k, n=1):
            if type(k) is int:
                return cols[:, COLS[name] + k:COLS[name] + k + n]
            return cols[:, bass.ds(k + COLS[name], n)]

        def tile(t, k, n=1):
            if type(k) is int:
                return t[:, k, :]
            return t[:, bass.ds(k, 1), :].rearrange("p a s -> p (a s)")

        def cut(k, n):
            return slice(k, k + n) if type(k) is int else bass.ds(k, n)

        block = ctx.enter_context(nc.Block())

        @block.sync
        def _(sp_):
            def stream(name, count, down):
                source, width = (wdown, DOWN) if down else (wmain, CHUNK)
                n0, at = BASE[name], WHERE[name]

                def load(i, c):
                    if n0 + c >= 2:
                        sp_.wait_ge(low_ready, i * 2 + (n0 + c - 1))
                    src = source[cut(i * 2 + (at + c), 1), :, :].rearrange("a p n -> (a p) n")
                    sp_.dma_start(raw[:, c, 0:width], src).then_inc(raw_landed[c], 16)

                rounds = count // 2
                if n0 == 0:
                    load(0, 0)
                    load(0, 1)
                    n0, at, rounds = 2, at + 2, rounds - 1
                for i in repeat(sp_, rounds):
                    for c in range(2):
                        load(i, c)

            sp_.dma_start(xT[:, :, :], xin).then_inc(inputs_landed, 16)
            sp_.dma_start(cols[:, :], cols_in).then_inc(inputs_landed, 16)
            sp_.dma_start(mats[:, :, :], mats_in).then_inc(inputs_landed, 16)
            sp_.dma_start(oh[:, :], onehot_in).then_inc(inputs_landed, 16)
            sp_.dma_start(ad[:, :], add_in).then_inc(inputs_landed, 16)
            sp_.dma_start(rb[:, :], rel_in).then_inc(inputs_landed, 16)
            sp_.dma_start(lamb[:, :, :], lam_in).then_inc(inputs_landed, 16)
            for name, count, down in STAGES:
                stream(name, count, down)
            for t in range(KT):
                sp_.wait_ge(sem("final_ready"), t + 1)
                sp_.dma_start(out[:, t, :], tile(qk, t)).then_inc(out_stored, 16)
            sp_.wait_ge(out_stored, 16 * KT)

        @block.tensor
        def _(pe):
            def products(target, stationary, moving, start=True, stop=True):
                n = len(stationary)
                for k, ((sh, sl), (mh, ml)) in enumerate(zip(stationary, moving)):
                    pe.matmul(target, sh, ml, start=start and k == 0, stop=False)
                    pe.matmul(target, sh, mh, start=False, stop=False)
                    last = pe.matmul(target, sl, mh, start=False, stop=stop and k == n - 1)
                return last

            def weights(c, j, kts=KT, width=2 * P, at=0):
                w = [slice(at + k * width + j * P, at + k * width + (j + 1) * P) for k in range(kts)]
                return [(wh[:, c, s], wl[:, c, s]) for s in w]

            def acts(h, l, first=0, kts=KT):
                return [(h[:, first + k, :], l[:, first + k, :]) for k in range(kts)]

            def chunk(i, n):
                pe.wait_ge(low_ready, i + (n + 1))

            def credit(name, n):
                pe.sem_inc(sem(name), n)

            pe.wait_ge(inputs_landed, 7 * 16)
            for j in range(2):
                last = pe.matmul(bank[j][0:ROWS, 0:TW // 2], rb[:, 0:ROWS], oh[:, j * TW // 2:(j + 1) * TW // 2],
                                 start=True, stop=True)
            last.then_inc(sem("table_mm"), 1)

            def norm_sum(v):
                for t in range(KT):
                    pe.wait_ge(sem("square_ready"), KT * v + t + 1)
                    pe.matmul(bank[7][:, :], ones, tile(tmpb, t % 2), start=t == 0,
                              stop=t == KT - 1).then_inc(sem("square_used"), 1)

            def feature_major(name, chunks, x, ready, read, free_after, kts=KT):
                for s, v in free_after:
                    pe.wait_ge(sem(s), v)
                credit(read, 4)
                n0 = BASE[name]
                for i in repeat(pe, chunks // 2):
                    for c in range(2):
                        chunk(i * 2, n0 + c)
                        for j in range(2):
                            pe.wait_ge(sem(read), i * 4 + (2 * c + j + 1))
                            products(bank[2 * c + j][:, :], weights(c, j), x).then_inc(sem(ready), 1)

            def token_major(name, chunks, x, ready, read, free_after):
                for s, v in free_after:
                    pe.wait_ge(sem(s), v)
                credit(read, 4)
                n0 = BASE[name]
                for i in repeat(pe, chunks // 2):
                    for c in range(2):
                        chunk(i * 2, n0 + c)
                        w = [(wh[:, c, k * 2 * P:(k + 1) * 2 * P], wl[:, c, k * 2 * P:(k + 1) * 2 * P])
                             for k in range(KT)]
                        for j in range(2):
                            pe.wait_ge(sem(read), i * 4 + (2 * c + j + 1))
                            for b in range(2):
                                tokens = slice((2 * j + b) * P, (2 * j + b + 1) * P)
                                last = products(bank[2 * c + j][:, b * 2 * P:(b + 1) * 2 * P],
                                                [(h[:, tokens], l[:, tokens]) for h, l in x], w)
                            last.then_inc(sem(ready), 1)

            def paired(name, chunks, x0, x1, ready, read0, read1, free_after):
                for s, v in free_after:
                    pe.wait_ge(sem(s), v)
                credit(read0, 2)
                credit(read1, 2)
                n0 = BASE[name]
                for i in repeat(pe, chunks // 2):
                    for c, x, read in ((0, x0, read0), (1, x1, read1)):
                        chunk(i * 2, n0 + c)
                        for j in range(2):
                            pe.wait_ge(sem(read), i * 2 + (j + 1))
                            products(bank[2 * c + j][:, :], weights(c, j), x).then_inc(sem(ready), 1)

            def down(name, x, ready, read, free_after):
                for s, v in free_after:
                    pe.wait_ge(sem(s), v)
                credit(read, 2)
                n0 = BASE[name]
                for i in repeat(pe, 4):
                    for j in range(2):
                        pe.wait_ge(sem(read), i * 2 + (j + 1))
                        for c in range(2):
                            chunk(i * 4, n0 + 2 * j + c)
                            products(bank[j][:, :], weights(c, 0, HALF, P), x[c * HALF:(c + 1) * HALF],
                                     start=c == 0, stop=c == 1).then_inc(sem(ready), 1)

            def turn(v, free_after):
                for s, n in free_after:
                    pe.wait_ge(sem(s), n)
                for t in range(KT):
                    if t >= 2:
                        pe.wait_ge(sem("turn_read"), KT * v + t - 1)
                    for b in range(NB):
                        last = pe.transpose(bank[t % 2][:, b * P:(b + 1) * P], yt[:, b, t * P:(t + 1) * P], ident)
                    last.then_inc(sem("turned"), 1)

            def attend(kind, pairs, u0, r0):
                if u0 == 0:
                    credit("s_ready", 4)
                    credit("s_read", 8)
                    credit("pt_even", 1)
                    credit("pt_odd", 1)
                    credit("pv_done", 2)
                    credit("t_ready", 4)
                    credit("y_read", 2)
                for i in repeat(pe, pairs):

                    def scores(u, b):
                        n = (b + 1) * P
                        pe.wait_ge(sem("s_read"), i * 8 + (4 * (u0 + u) + b + 5))
                        half = slice(64 * u, 64 * u + 64)
                        q = slice(b * P, n)
                        if kind == "mla":
                            pe.matmul(bank[b][:, 0:n], qs[:, u, q],
                                      tile(qk, i * 2 + (4 + u))[:, 0:n], start=True, stop=False)
                            last = pe.matmul(bank[b][:, 0:n], tmpa[half, 0, q], qk[half, 11, 0:n],
                                             start=False, stop=True)
                        else:
                            k = {"moba": 4, "diff": 12, "dil": 4}[kind]
                            last = pe.matmul(bank[b][:, 0:n], qs[:, u, q], tile(qk, i + k)[:, 0:n],
                                             start=True, stop=True)
                        last.then_inc(sem("s_ready"), 1)

                    def transposes(u, b):
                        pe.wait_ge(sem("p_ready"), i * 8 + (4 * (u0 + u) + b + 1))
                        pe.wait_ge(sem("pt_odd" if b % 2 else "pt_even"), i * 4 + (2 * (u0 + u) + b // 2 + 1))
                        for k in range(b + 1):
                            last = pe.transpose(bank[4 + b % 2][:, k * P:(k + 1) * P], tq[:, b, k * P:(k + 1) * P],
                                                ident)
                        last.then_inc(sem("t_ready"), 1)

                    def values(u, b):
                        pe.wait_ge(sem("pt_odd" if b % 2 else "pt_even"), i * 4 + (2 * (u0 + u) + b // 2 + 2))
                        if b == 0:
                            pe.wait_ge(sem("y_read"), i * 2 + (u0 + u + 1))
                        dh = 64 if kind in ("moba", "dil") else P
                        if dh == 64:
                            c = i * P + 64 * u
                        elif kind == "diff":
                            c = i * P + 4 * P
                        else:
                            c = i * (2 * P) + (4 + u) * P
                        for k in range(b + 1):
                            last = pe.matmul(bank[6 + u][:, b * dh:(b + 1) * dh],
                                             pts[:, b % 2, k * P:(k + 1) * P], vt[:, k, cut(c, dh)],
                                             start=k == 0, stop=k == b)
                        last.then_inc(sem("pv_done"), 1)

                    pe.wait_ge(sem("q_staged"), i * 2 + 2 * (r0 + 1))
                    for b in range(NB):
                        scores(0, b)
                    for u in range(2):
                        for b in range(NB):
                            transposes(u, b)
                            if u == 0:
                                scores(1, b)
                            if b:
                                values(u, b - 1)
                        values(u, NB - 1)

            norm_sum(0)
            pe.wait_ge(sem("xl_ready"), KT)
            feature_major("qk", 8, acts(xh, xl), "qk_ready", "qk_read", [("table_read", 2)])
            token_major("v", 4, acts(xh, xl), "v_ready", "v_read", [("qk_read", 20)])
            pe.wait_ge(sem("v_read"), 12)
            credit("qk_sum_read", 2)
            credit("qk_sum", 2)
            for i in repeat(pe, 8):
                for c in range(2):
                    pe.wait_ge(sem("qk_square"), i * 2 + (c + 1))
                    pe.wait_ge(sem("qk_sum_read"), i * 2 + (c + 1))
                    pe.matmul(bank[c][:, :], ones, tile(tmpb, c), start=True, stop=True).then_inc(sem("qk_sum"), 1)
            pe.wait_ge(sem("qk_sum_read"), 18)
            pe.wait_ge(sem("qk_normed"), 16)
            credit("w_ready", 4)
            credit("z_done", 1)
            credit("sy_ready", 1)
            credit("sy_read", 1)
            credit("z_ready", 4)
            for h in repeat(pe, 8):
                pe.wait_ge(sem("k_staged"), h + 1)
                for m, kb in enumerate(reversed(range(NB))):
                    pe.wait_ge(sem("w_ready"), h * 4 + (m + 1))
                    pe.matmul(bank[kb][:, 0:S - kb * P], ks[:, kb * P:(kb + 1) * P], tile(qk, h)[:, kb * P:S],
                              start=True, stop=False, skip_group_check=True).then_inc(sem("z_ready"), 1)
                for m, kb in enumerate(reversed(range(NB))):
                    pe.wait_ge(sem("sp_ready"), h * 4 + (m + 1))
                    for jb in range(kb, NB):
                        o = (jb - kb) * P
                        pe.matmul(bank[kb][:, o:S - kb * P], negtri if jb == kb else negones, sp[:, jb, jb * P:S],
                                  start=False, stop=False, skip_group_check=True)
                    pe.matmul(bank[kb][:, 0:P], ident, negmask, start=False, stop=True,
                              skip_group_check=True).then_inc(sem("z_done"), 1)
                pe.wait_ge(sem("v_staged"), h + 1)
                pe.wait_ge(sem("sy_read"), h + 1)
                for m, kb in enumerate(range(NB)):
                    pe.wait_ge(sem("w_ready"), h * 4 + 8)
                    last = pe.matmul(bank[4][:, kb * P:S], vs[:, kb, :], wz[:, kb, kb * P:S], start=kb == 0,
                                     stop=kb == NB - 1)
                last.then_inc(sem("sy_ready"), 1)
            pe.wait_ge(sem("yl0_ready"), 8)
            paired("gate2", 8, acts(xh, xl), acts(yh, yl), "g2_ready", "g2_gate", "g2_prod", [("sy_read", 9)])
            feature_major("pool", 4, acts(xh, xl), "pool_ready", "pool_read", [("g2_gate", 10), ("g2_prod", 10)])
            pe.wait_ge(sem("pool_read"), 12)
            for c in range(2):
                chunk(0, BASE["wpool"] + c)
                for g in range(2):
                    pe.wait_ge(sem("p_low"), 4 * c + 2 * g + 2)
                    for j in range(2):
                        f = 4 * c + 2 * g
                        if c:
                            pe.wait_ge(sem("wpool_low"), 2 * g + j + 1)
                        products(bank[2 * g + j][:, :], weights(c, j, 2, at=g * 2 * 2 * P),
                                 acts(yh, yl, f, 2)).then_inc(sem("wpool_ready"), 1)
            pe.wait_ge(sem("wpool_low"), 8)
            paired("gate0", 8, acts(xh, xl), acts(yh, yl), "g0_ready", "g0_gate", "g0_prod", [])
            pe.wait_ge(sem("g0_gate"), 10)
            pe.wait_ge(sem("g0_prod"), 10)
            pe.wait_ge(sem("rg_landed"), 16)

            def lru_gates(t):
                pe.wait_ge(sem("lru_conv"), 3 * t + 3)
                if t >= 2:
                    pe.wait_ge(sem("lru_sigmoid"), 2 * (t - 2) + 2)
                pe.matmul(bank[4 + 2 * (t % 2)][:, :], rgw[:, t, :], xc[:, t % 2, :], start=True, stop=True)
                pe.matmul(bank[5 + 2 * (t % 2)][:, :], rgw[:, 8 + t, :], xc[:, t % 2, :], start=True,
                          stop=True).then_inc(sem("lru_gate"), 1)

            for t in range(KT):
                if t % 2 == 0:
                    chunk(0, BASE["lru"] + t // 2)
                if t >= 4:
                    pe.wait_ge(sem("lru_conv"), 3 * (t - 4) + 3)
                products(bank[t % 4][:, :], weights(t // 2 % 2, t % 2), acts(xh, xl)).then_inc(sem("lru_ready"), 1)
                if t:
                    lru_gates(t - 1)
            lru_gates(KT - 1)
            pe.wait_ge(sem("lru_low"), 8)
            paired("gate1", 8, acts(xh, xl), acts(yh, yl), "g1_ready", "g1_gate", "g1_prod", [])
            pe.wait_ge(sem("yl1_ready"), 8)
            feature_major("out", 4, acts(yh, yl), "out_ready", "out_read", [("g1_gate", 10), ("g1_prod", 10)])

            def ffn(n, v):
                norm_sum(v)
                pe.wait_ge(sem("xl_ready"), KT * (v + 1))
                paired(f"ffn{n}", FT, acts(xh, xl), acts(xh, xl), f"f{n}_ready", f"f{n}_gate", f"f{n}_prod", [])
                pe.wait_ge(sem(f"f{n}_low"), FT)
                down(f"down{n}", acts(ah, al, 0, FT), f"d{n}_ready", f"d{n}_read", [(f"f{n}_gate", FT + 2)])

            ffn(0, 1)
            norm_sum(2)
            pe.wait_ge(sem("xl_ready"), KT * 3)
            feature_major("eqk", 8, acts(xh, xl), "eqk_ready", "eqk_read", [("d0_read", 10)])
            token_major("ev", 4, acts(xh, xl), "ev_ready", "ev_read", [("eqk_read", 20)])
            pe.wait_ge(sem("ev_read"), 12)
            attend("moba", 4, 0, 0)
            attend("diff", 4, 8, 4)
            turn(0, [("y_token", 1)])
            pe.wait_ge(sem("turn_read"), 8)
            feature_major("eout", 4, acts(xh, xl), "eo_ready", "eo_read", [])
            ffn(1, 3)
            norm_sum(4)
            pe.wait_ge(sem("xl_ready"), KT * 5)
            feature_major("oqk", 6, acts(xh, xl), "oqk_ready", "oqk_read", [("d1_read", 10)])
            token_major("ov", 2, acts(xh, xl), "ov_ready", "ov_read", [("oqk_read", 16)])
            pe.wait_ge(sem("ov_read"), 8)
            attend("dil", 4, 16, 8)
            pe.wait_ge(sem("y_read"), 26)
            for t in range(3):
                pe.wait_ge(sem("c_square"), t + 1)
                pe.matmul(bank[6 + t // 2][:, :], ones, tile(tmpb, t % 2), start=t != 1,
                          stop=t != 0).then_inc(sem("c_sum"), 1)
            pe.wait_ge(sem("cl_ready"), 3)
            chunk(0, BASE["mla"])
            for j in range(6):
                if j >= 4:
                    pe.wait_ge(sem("mla_read"), j - 3)
                products(bank[j % 4][:, :], weights(0, j, 2, 6 * P), acts(ch, cl, 0, 2)).then_inc(sem("mla_ready"), 1)
            chunk(0, BASE["mla"] + 1)
            for j in range(4):
                pe.wait_ge(sem("mla_read"), j + 3)
                products(bank[(6 + j) % 4][:, :], weights(1, j, 1), acts(ch, cl, 2, 1)).then_inc(sem("mla_ready"), 1)
            for b in range(NB):
                pe.wait_ge(sem("mla_read"), b + 7)
                products(bank[(10 + b) % 4][:, :], [(ch[:, 2, b * P:(b + 1) * P], cl[:, 2, b * P:(b + 1) * P])],
                         [(wh[:, 1, 4 * P:8 * P], wl[:, 1, 4 * P:8 * P])]).then_inc(sem("mla_ready"), 1)
            pe.wait_ge(sem("mla_read"), 14)
            for n, t in enumerate((12, 13, 11)):
                pe.matmul(bank[4 + n][:, :], small_rot, tile(qk, t), start=True, stop=True)\
                  .then_inc(sem("rotated"), 1)
            pe.wait_ge(sem("roped"), 3)
            attend("mla", 2, 24, 12)
            turn(1, [("y_token", 2)])
            pe.wait_ge(sem("turn_read"), 16)
            feature_major("oout", 4, acts(xh, xl), "oo_ready", "oo_read", [])
            ffn(2, 5)
            norm_sum(6)

        @block.gpsimd
        def _(pool):
            def low(i, n, c):
                pool.wait_ge(high_ready, i + (n + 1))
                pool.tensor_tensor(wl[:, c, :], raw[:, c, :], wh[:, c, :].bitcast(F32),
                                   ALU.subtract).then_inc(low_ready, 1)

            def stage(name, count):
                n0 = BASE[name] + 2
                rounds = count // 2 - (1 if n0 + count > CHUNKS else 0)
                for i in repeat(pool, rounds):
                    for c in range(2):
                        low(i * 2, n0 + c, c)

            def attend(kind, pairs, u0, r0):
                if kind in ("moba", "dil"):
                    pool.wait_ge(low_ready, BASE["eout" if kind == "moba" else "mla"] + 2)
                    pool.wait_ge(sem("d0_read" if kind == "moba" else "d1_read"), 10)
                    for u in range(2):
                        pool.memset(qs[64 - 64 * u:P - 64 * u, u, :], 0.0).then_inc(sem("qs_zero"), 1)
                        pool.wait_ge(sem("qs_zero"), (1 if kind == "moba" else 3) + u)
                for i in repeat(pool, pairs):
                    pool.wait_ge(sem("s_ready"), i * 8 + (4 * u0 + 4))
                    if kind == "mla":
                        pool.tensor_copy(qs[:, :, :], qk[:, bass.ds(i * 2, 2), :]).then_inc(sem("q_staged"), 1)
                        pool.tensor_copy(tmpa[:, 0:1, :], qk[:, bass.ds(i + 12, 1), :])\
                            .then_inc(sem("q_staged"), 1)
                    else:
                        first = {"moba": 0, "diff": 8, "dil": 0}[kind]
                        for u in range(2):
                            half = slice(64 * u, 64 * u + 64)
                            pool.tensor_copy(qs[half, u:u + 1, :], qk[half, bass.ds(i + first, 1), :])\
                                .then_inc(sem("q_staged"), 1)
                            pool.wait_ge(sem("q_staged"), i * 2 + (2 * r0 + u + 1))
                    for u in range(2):
                        pool.wait_ge(sem("s_read"), i * 8 + (4 * (u0 + u) + 4))
                        row = {"moba": i * 2 + u, "diff": i + 8, "dil": i * 2 + (12 + u), "mla": MASK_ROW}[kind]
                        pool.sem_inc(sem("bias_begun"), 1)
                        one = table[cut(row, 1), 0:S]
                        src = bass.AP(tensor=one.tensor, offset=one.offset, ap=[[1, P], [1, S]])
                        pool.dma_start(bt[:, u, :], src).then_inc(sem(f"bias_landed_{u}"), 16)

            for n in range(2):
                low(0, n, n)
            pool.wait_ge(table_ready, 1)
            pool.dma_start(table[:, :], tt[:, :]).then_inc(table_stored, 16)
            pool.wait_ge(table_stored, 16)
            stage("qk", 8)
            stage("v", 4)
            pool.wait_ge(sem("qk_normed"), 16)
            for h in repeat(pool, 8):
                pool.wait_ge(sem("z_ready"), h * 4 + 4)
                pool.tensor_copy(ks[:, :], tile(qk, h + 8)).then_inc(sem("k_staged"), 1)
                pool.wait_ge(sem("sy_ready"), h + 1)
                pool.tensor_copy(vs[:, :, :], vt[:, :, cut(h * P, P)]).then_inc(sem("v_staged"), 1)
            pool.wait_ge(sem("sy_read"), 9)
            pool.dma_start(rgw[:, :, :], rg_in).then_inc(sem("rg_landed"), 16)
            stage("gate2", 8)
            for name in ("pool", "wpool", "gate0", "lru", "gate1", "out", "ffn0"):
                stage(name, COUNT[name])
            stage("down0", 16)
            stage("eqk", 8)
            stage("ev", 4)
            attend("moba", 4, 0, 0)
            attend("diff", 4, 8, 4)
            stage("eout", 4)
            stage("ffn1", FT)
            stage("down1", 16)
            pool.wait_ge(sem("d1_read"), 10)
            pool.dma_start(rope[:, :, :], rope_in).then_inc(sem("rope_landed"), 16)
            stage("oqk", 6)
            stage("ov", 2)
            attend("dil", 4, 16, 8)
            stage("mla", 2)
            pool.wait_ge(sem("roped"), 3)
            attend("mla", 2, 24, 12)
            stage("oout", 4)
            stage("ffn2", FT)
            stage("down2", 16)

        @block.scalar
        def _(act):
            step = Steps(act, sem("act_step"))

            def refill(c, n, i=0):
                if type(i) is not int:
                    act.wait_ge(raw_landed[c], i * 8 + 16 * (n // 2 + 1))
                else:
                    act.wait_ge(raw_landed[c], 16 * ((i + n) // 2 + 1))
                act.activation(wh[:, c, :], raw[:, c, :], ACT.Copy).then_inc(high_ready, 1)

            def norm(v, after):
                for s_, n in after:
                    act.wait_ge(sem(s_), n)
                for t in range(KT):
                    if KT * v + t >= 2:
                        act.wait_ge(sem("square_used"), KT * v + t - 1)
                    act.activation(tmpb[:, t % 2, :], xT[:, t, :], ACT.Square).then_inc(sem("square_ready"), 1)
                act.wait_ge(sem("var_ready"), v + 1)
                act.activation(rstd[:, :], rstd[:, :], ACT.Sqrt).then_inc(sem("std_ready"), 1)
                if v < 6:
                    for t in range(KT):
                        act.wait_ge(sem("nx_ready"), KT * v + t + 1)
                        act.activation(xh[:, t, :], tmpa[:, t % 2, :], ACT.Copy).then_inc(sem("xh_ready"), 1)

            def copies(name, chunks, ready, read, scale):
                n0 = BASE[name] + 2
                for i in repeat(act, chunks // 2):
                    for c in range(2):
                        for j in range(2):
                            act.wait_ge(sem(ready), i * 4 + (2 * c + j + 1))
                            act.activation(tile(qk, i * 4 + (2 * c + j)), bank[2 * c + j][:, :], ACT.Copy,
                                           scale=col(scale, i * 4 + (2 * c + j))).then_inc(sem(read), 1)
                        refill(c, n0 + c, i * 2)

            def value_copies(name, chunks, ready, read):
                n0 = BASE[name] + 2
                for i in repeat(act, chunks // 2):
                    for c in range(2):
                        for j in range(2):
                            act.wait_ge(sem(ready), i * 4 + (2 * c + j + 1))
                            act.activation(vt[:, 2 * j:2 * j + 2, cut(i * S + c * 2 * P, 2 * P)],
                                           bank[2 * c + j][:, :].rearrange("p (b n) -> p b n", b=2),
                                           ACT.Copy).then_inc(sem(read), 1)
                        refill(c, n0 + c, i * 2)

            def gates(b, name, ready, gate, prod):
                n0 = BASE[name] + 2
                for i in repeat(act, 4):
                    for j in range(2):
                        act.wait_ge(sem(ready), i * 4 + (j + 1))
                        act.wait_ge(sem(prod), i * 2 + (j + 1))
                        act.activation(tmpa[:, j, :], bank[j][:, :], ACT.Sigmoid,
                                       bias=col("b_gate", i * 2 + (8 * b + j))).then_inc(sem(gate), 1)
                    refill(0, n0, i * 2)
                    act.wait_ge(sem(ready), i * 4 + 4)
                    refill(1, n0 + 1, i * 2)

            def refills(name, chunks, ready, per, last=False):
                n0 = BASE[name] + 2
                for i in repeat(act, chunks // 2 - last):
                    for c in range(2):
                        act.wait_ge(sem(ready), i * (2 * per) + per * (c + 1))
                        refill(c, n0 + c, i * 2)

            def split(high, source, source_ready):
                for t in range(KT):
                    act.wait_ge(sem(source_ready[0]), source_ready[1] + t)
                    act.activation(yh[:, t, :], source[:, t, :], ACT.Copy).then_inc(sem(high), 1)

            def ffn(n, v, after):
                norm(v, after)
                name, ready, n0 = f"ffn{n}", f"f{n}_ready", BASE[f"ffn{n}"] + 2
                for i in repeat(act, FT // 2):
                    for j in range(2):
                        act.wait_ge(sem(ready), i * 4 + (j + 1))
                        if n == 0:
                            act.activation(tmpa[:, j, :], bank[j][:, :], ACT.Silu).then_inc(sem("f0_gate"), 1)
                        else:
                            k = (n - 1) * FT
                            act.activation(tmpa[:, j, :], bank[j][:, :], ACT.Identity,
                                           bias=col("ffn_b", i * 2 + (k + j)),
                                           scale=col("ffn_w", i * 2 + (3 * k + 2 * FT + j)))\
                               .then_inc(sem(f"f{n}_conv0"), 1)
                    refill(0, n0, i * 2)
                    if n:
                        for j in range(2):
                            act.wait_ge(sem(f"f{n}_gate"), i * 2 + (j + 3))
                            act.activation(tmpa[:, j, :], tmpa[:, j, :], ACT.Gelu).then_inc(sem(f"f{n}_gelu"), 1)
                    for j in range(2):
                        act.wait_ge(sem(f"f{n}_prod"), i * 2 + (j + 3))
                        act.activation(tile(ah, i * 2 + j), tmpb[:, j, :], ACT.Copy).then_inc(sem(f"f{n}_high"), 1)
                    refill(1, n0 + 1, i * 2)
                refills(f"down{n}", 16, f"d{n}_ready", 1, last=n == 2)

            def attend(kind, pairs, u0):
                for i in repeat(act, pairs):
                    def exponent(u, b):
                        q = 4 * (u0 + u) + b
                        n = (b + 1) * P
                        act.wait_ge(sem("s_read"), i * 8 + (q + 9))
                        act.activation(tq[:, b, 0:n], tq[:, b, 0:n], ACT.Exp, bias=nm[:, u, b:b + 1], scale=-1.0,
                                       accum_out=rs[:, u, b:b + 1]).then_inc(sem("p_ready"), 1)

                    def copy_even(u, b):
                        q = 4 * (u0 + u) + b
                        act.wait_ge(sem("t_ready"), i * 8 + (q + 5))
                        act.wait_ge(sem("pv_done"), i * 8 + (q + 1))
                        act.activation(pts[:, 0, 0:(b + 1) * P], bank[4][:, 0:(b + 1) * P], ACT.Copy)\
                           .then_inc(sem("pt_even"), 1)

                    for u in range(2):
                        exponent(u, 0)
                        exponent(u, 1)
                        copy_even(u, 0)
                        exponent(u, 2)
                        exponent(u, 3)
                        copy_even(u, 2)

            def turn(v):
                for t in range(KT):
                    act.wait_ge(sem("turned"), KT * v + t + 1)
                    act.activation(xh[:, t, :], bank[t % 2][:, :], ACT.Copy,
                                   scale=col("one_scale" if v else "subln", t)).then_inc(sem("turn_high"), 1)

            act.wait_ge(raw_landed[0], 16)
            act.activation(wh[:, 0, :], raw[:, 0, :], ACT.Copy).then_inc(high_ready, 1)
            act.wait_ge(raw_landed[1], 16)
            act.activation(wh[:, 1, :], raw[:, 1, :], ACT.Copy).then_inc(high_ready, 1)
            act.wait_ge(sem("lambda_sums"), 2)
            act.activation(t1, col("lru_lambda", 0, 8), ACT.Abs).then_inc(sem("lambda_abs"), 1)
            act.wait_ge(sem("lambda_abs"), 1)
            act.activation(t1, t1, ACT.Exp, scale=-1.0).then_inc(sem("lambda_exp"), 1)
            act.activation(lam2, lam2, ACT.Exp).then_inc(sem("lambda_exp"), 1)
            norm(0, [("inputs_landed", 7 * 16)])
            copies("qk", 8, "qk_ready", "qk_read", "one_scale")
            value_copies("v", 4, "v_ready", "v_read")
            act.wait_ge(sem("qk_read"), 20)
            for i in repeat(act, 8):
                for c in range(2):
                    act.wait_ge(sem("qk_sum"), i * 2 + (c + 1))
                    act.activation(tmpb[:, c, :], tile(qk, i * 2 + c), ACT.Square).then_inc(sem("qk_square"), 1)
                for c in range(2):
                    act.wait_ge(sem("qk_sum_read"), i * 2 + (c + 3))
                    act.activation(tmpa[:, c, :], tmpa[:, c, :], ACT.Sqrt).then_inc(sem("qk_std"), 1)
            for h in repeat(act, 8, step, 8):
                for m, kb in enumerate(reversed(range(NB))):
                    w = sp[:, kb, kb * P:S]
                    act.wait_ge(sem("z_ready"), h * 4 + (m + 5))
                    act.wait_ge(sem("z_done"), h * 4 + 1)
                    step(act.activation(w, bank[kb][:, 0:S - kb * P], ACT.Abs))
                    step(act.activation(w, w, ACT.Exp, scale=-1.0))
                    act.activation(w, w, ACT.Ln, bias=1.0).then_inc(sem("ln_ready"), 1)
                for m, kb in enumerate(reversed(range(NB))):
                    act.wait_ge(sem("z_done"), h * 4 + (m + 2))
                    act.wait_ge(sem("sy_ready"), h + 1)
                    act.activation(wz[:, kb, kb * P:S], bank[kb][:, 0:S - kb * P], ACT.Exp).then_inc(sem("w_ready"), 1)
                act.wait_ge(sem("sy_ready"), h + 2)
                act.activation(tile(qk, h), bank[4][:, :], ACT.Copy).then_inc(sem("sy_read"), 1)
            act.wait_ge(sem("sy_read"), 9)
            for t in range(KT):
                act.activation(yh[:, t, :], qk[:, t, :], ACT.Copy).then_inc(sem("yh0_ready"), 1)
            gates(2, "gate2", "g2_ready", "g2_gate", "g2_prod")
            for t in range(KT + 1):
                if t < KT:
                    act.wait_ge(sem("pool_ready"), t + 1)
                    if t >= 2:
                        act.wait_ge(sem("p_low"), t - 1)
                    else:
                        act.wait_ge(sem("pads_ready"), 4)
                    act.activation(pu[:, t % 2, 16:16 + S], bank[t % 4][:, :], ACT.Copy).then_inc(sem("pool_read"), 1)
                if t:
                    act.wait_ge(sem("p_ready_value"), t)
                    act.activation(yh[:, t - 1, :], tmpb[:, (t - 1) % 2, :], ACT.Copy).then_inc(sem("p_high"), 1)
                if t < KT and t % 2:
                    refill(t // 2 % 2, BASE["pool"] + t // 2 + 2)
            for c in range(2):
                for g in range(2):
                    for j in range(2):
                        f = 4 * c + 2 * g
                        act.wait_ge(sem("wpool_ready"), f + 2)
                        act.activation(yh[:, f + j, :], bank[2 * g + j][:, :], ACT.Copy,
                                       scale=col("pool_scale", f + j)).then_inc(sem("wpool_high"), 1)
                refill(c, BASE["wpool"] + c + 2)
            gates(0, "gate0", "g0_ready", "g0_gate", "g0_prod")
            for t in range(KT + 1):
                if t < KT:
                    act.wait_ge(sem("lru_ready"), t + 1)
                    if t >= 2:
                        act.wait_ge(sem("lru_low"), t - 1)
                    act.activation(xc[:, t % 2, :], bank[t % 4][:, :], ACT.Identity, bias=col("conv_b", t),
                                   scale=col("conv_w", 24 + t)).then_inc(sem("lru_base"), 1)
                    if t % 2:
                        refill(t // 2 % 2, BASE["lru"] + t // 2 + 2)
                if t:
                    u, c = t - 1, (t - 1) % 2
                    act.wait_ge(sem("lru_gate"), u + 1)
                    act.activation(rr[:, c, :], bank[4 + 2 * c][:, :], ACT.Sigmoid, bias=col("b_rg", u))\
                       .then_inc(sem("lru_sigmoid"), 1)
                    act.activation(ii[:, c, :], bank[5 + 2 * c][:, :], ACT.Sigmoid, bias=col("b_ig", u))\
                       .then_inc(sem("lru_sigmoid"), 1)
                    act.wait_ge(sem("lru_sigmoid"), 2 * u + 2)
                    act.activation(tmpb[:, c, :], rr[:, c, :], ACT.Tanh, scale=decay8[:, u:u + 1])\
                       .then_inc(sem("lru_tanh"), 1)
                    act.activation(aa[:, c, :], rr[:, c, :], ACT.Exp, scale=ndecay8[:, u:u + 1])\
                       .then_inc(sem("lru_a"), 1)
                    act.wait_ge(sem("lru_m2"), 2 * u + 2)
                    act.activation(tmpa[:, c, :], tmpa[:, c, :], ACT.Sqrt).then_inc(sem("lru_mult"), 1)
                    act.wait_ge(sem("lru_h"), 3 * u + 3)
                    act.activation(yh[:, u, :], xc[:, c, :], ACT.Copy).then_inc(sem("lru_high"), 1)
            gates(1, "gate1", "g1_ready", "g1_gate", "g1_prod")
            for t in range(KT):
                act.wait_ge(sem("merged_ready"), t + 1)
                act.wait_ge(sem("g1_ready"), 16)
                act.activation(yh[:, t, :], merged[:, t, :], ACT.Copy).then_inc(sem("yh1_ready"), 1)
            refills("out", 4, "out_ready", 2)
            ffn(0, 1, [("out_read", 12)])
            norm(2, [("d0_read", 10)])
            copies("eqk", 8, "eqk_ready", "eqk_read", "even_scale")
            value_copies("ev", 4, "ev_ready", "ev_read")
            attend("moba", 4, 0)
            attend("diff", 4, 8)
            act.wait_ge(sem("diff_var"), 1)
            act.activation(dss, dss, ACT.Sqrt).then_inc(sem("diff_std"), 1)
            turn(0)
            refills("eout", 4, "eo_ready", 2)
            ffn(1, 3, [("eo_read", 12)])
            norm(4, [("d1_read", 10)])
            copies("oqk", 6, "oqk_ready", "oqk_read", "odd_scale")
            value_copies("ov", 2, "ov_ready", "ov_read")
            attend("dil", 4, 16)
            act.wait_ge(sem("oqk_read"), 16)
            for t in range(3):
                if t == 2:
                    act.wait_ge(sem("c_sum"), 1)
                act.activation(tmpb[:, t % 2, :], qk[:, 8 + t, :], ACT.Square).then_inc(sem("c_square"), 1)
            for t in range(2):
                act.wait_ge(sem("c_var"), t + 1)
                act.activation(tmpa[:, t, :], tmpa[:, t, :], ACT.Sqrt).then_inc(sem("c_std"), 1)
            for t in range(3):
                act.wait_ge(sem("c_normed"), t + 1)
                act.activation(ch[:, t, :], qk[:, 8 + t, :], ACT.Copy).then_inc(sem("ch_ready"), 1)
            for j in range(14):
                act.wait_ge(sem("mla_ready"), j + 1)
                if j < 6:
                    act.activation(qk[:, j if j < 4 else j + 8, :], bank[j % 4][:, :], ACT.Copy,
                                   scale=192 ** -0.5).then_inc(sem("mla_read"), 1)
                elif j < 10:
                    act.activation(qk[:, j - 2, :], bank[j % 4][:, :], ACT.Copy).then_inc(sem("mla_read"), 1)
                else:
                    act.activation(vt[:, j - 10, S:2 * S], bank[j % 4][:, :], ACT.Copy).then_inc(sem("mla_read"), 1)
                if j in (5, 13):
                    refill(j // 6 % 2 if j == 5 else 1, BASE["mla"] + 2 + (j == 13))
            attend("mla", 2, 24)
            turn(1)
            refills("oout", 4, "oo_ready", 2)
            ffn(2, 5, [("oo_read", 12)])
            norm(6, [("d2_read", 10)])

        @block.vector
        def _(dve):
            step = Steps(dve, sem("dve_step"))

            def norm(v, gain, g0):
                dve.wait_ge(sem("square_used"), KT * (v + 1))
                dve.tensor_scalar(rstd[:, :], bank[7][:, :], 1.0 / D, EPS, ALU.mult, ALU.add)\
                   .then_inc(sem("var_ready"), 1)
                dve.wait_ge(sem("std_ready"), v + 1)
                step(dve.reciprocal(rstd[:, :], rstd[:, :]))
                for t in range(KT + 1):
                    if t < KT:
                        target = qk[:, t, :] if v == 6 else tmpa[:, t % 2, :]
                        if t >= 2 and v < 6:
                            dve.wait_ge(sem("xl_ready"), KT * v + t - 1)
                        dve.scalar_tensor_tensor(target, xT[:, t, :], col(gain, g0 + t), rstd[:, :], ALU.mult,
                                                 ALU.mult).then_inc(sem("final_ready" if v == 6 else "nx_ready"), 1)
                    if t and v < 6:
                        dve.wait_ge(sem("xh_ready"), KT * v + t)
                        dve.tensor_tensor(xl[:, t - 1, :], tmpa[:, (t - 1) % 2, :], xh[:, t - 1, :].bitcast(F32),
                                          ALU.subtract).then_inc(sem("xl_ready"), 1)

            def products(name, first, ready, gate, prod):
                for i in repeat(dve, 4, step, 0 if first else 2):
                    for j in range(2):
                        dve.wait_ge(sem(gate), i * 2 + (j + 3))
                        dve.wait_ge(sem(ready), i * 4 + (j + 3))
                        if first:
                            dve.tensor_tensor(tile(merged, i * 2 + j), bank[2 + j][:, :], tmpa[:, j, :], ALU.mult)\
                               .then_inc(sem(prod), 1)
                        else:
                            dve.tensor_tensor(tmpb[:, j, :], bank[2 + j][:, :], tmpa[:, j, :], ALU.mult)\
                               .then_inc(sem(prod), 1)
                            dve.wait_ge(sem(prod), i * 2 + (j + 3))
                            step(dve.tensor_tensor(tile(merged, i * 2 + j), tile(merged, i * 2 + j), tmpb[:, j, :],
                                                   ALU.add))

            def residual(chunks, ready, read, per):
                rounds, tiles = (chunks // 2, 4) if per == 1 else (4, 2)
                for i in repeat(dve, rounds):
                    for j in range(tiles):
                        dve.wait_ge(sem(ready), i * (tiles * per) + per * (j + 1))
                        t = i * tiles + j
                        dve.tensor_tensor(tile(xT, t), tile(xT, t), bank[j][:, :], ALU.add).then_inc(sem(read), 1)

            def ffn(n, v, gain, g0):
                norm(v, gain, g0)
                for i in repeat(dve, FT // 2, step, 2 if n else 0):
                    if n:
                        for j in range(2):
                            k = 3 * (n - 1) * FT
                            dve.wait_ge(sem(f"f{n}_conv0"), i * 2 + (j + 1))
                            a = tmpa[:, j, :]
                            step(dve.scalar_tensor_tensor(a[:, 1:S], bank[j][:, 0:S - 1],
                                                          col("ffn_w", i * 2 + (k + FT + j)), a[:, 1:S],
                                                          ALU.mult, ALU.add))
                            dve.scalar_tensor_tensor(a[:, 2:S], bank[j][:, 0:S - 2], col("ffn_w", i * 2 + (k + j)),
                                                     a[:, 2:S], ALU.mult, ALU.add).then_inc(sem(f"f{n}_gate"), 1)
                    for j in range(2):
                        dve.wait_ge(sem(f"f{n}_ready"), i * 4 + (j + 3))
                        dve.wait_ge(sem(f"f{n}_gelu" if n else "f0_gate"), i * 2 + (j + (1 if n else 3)))
                        dve.tensor_tensor(tmpb[:, j, :], tmpa[:, j, :], bank[2 + j][:, :], ALU.mult)\
                           .then_inc(sem(f"f{n}_prod"), 1)
                    for j in range(2):
                        dve.wait_ge(sem(f"f{n}_high"), i * 2 + (j + 1))
                        dve.tensor_tensor(tile(al, i * 2 + j), tmpb[:, j, :], tile(ah, i * 2 + j).bitcast(F32),
                                          ALU.subtract).then_inc(sem(f"f{n}_low"), 1)
                    dve.wait_ge(sem(f"f{n}_low"), i * 2 + 2)
                residual(16, f"d{n}_ready", f"d{n}_read", 2)

            def attend(kind, pairs, u0, r0):
                for i in repeat(dve, pairs, step, 3 if kind == "diff" else 2):
                    def shifted(u, b):
                        q = 4 * (u0 + u) + b
                        n = (b + 1) * P
                        dve.wait_ge(sem(f"bias_landed_{u}"), i * 16 + 16 * (r0 + 1))
                        dve.wait_ge(sem("s_ready"), i * 8 + (q + 5))
                        dve.wait_ge(sem("t_ready"), i * 8 + (q + 1))
                        dve.sem_inc(sem("shift_begun"), 1)
                        dve.tensor_tensor_reduce(tq[:, b, 0:n], bank[b][:, 0:n], bt[:, u, 0:n][:, ::-1], -1.0,
                                                 3.0e38, ALU.add, ALU.min, nm[:, u, b:b + 1])\
                           .then_inc(sem("s_read"), 1)

                    def copy_odd(u, b):
                        q = 4 * (u0 + u) + b
                        dve.wait_ge(sem("t_ready"), i * 8 + (q + 5))
                        dve.wait_ge(sem("pv_done"), i * 8 + (q + 1))
                        dve.tensor_copy(pts[:, 1, 0:(b + 1) * P], bank[5][:, 0:(b + 1) * P])\
                           .then_inc(sem("pt_odd"), 1)

                    def normalised(u):
                        dve.wait_ge(sem("pv_done"), i * 8 + (4 * (u0 + u) + 6))
                        step(dve.reciprocal(rd[:, u, :], rs[:, u, :]))
                        dh, c = 64, i * P + 64 * u
                        if kind == "mla":
                            dh, c = P, i * (2 * P) + (4 + u) * P
                        dve.tensor_tensor(yt[:, :, cut(c, dh)],
                                          bank[6 + u][:, 0:NB * dh].rearrange("p (b n) -> p b n", b=NB),
                                          rd[:, u, :].unsqueeze(2).to_broadcast([P, NB, dh]), ALU.mult)\
                           .then_inc(sem("y_read"), 1)

                    for b in range(NB):
                        shifted(0, b)
                    shifted(1, 0)
                    copy_odd(0, 1)
                    shifted(1, 1)
                    shifted(1, 2)
                    copy_odd(0, 3)
                    shifted(1, 3)
                    if kind != "diff":
                        normalised(0)
                    copy_odd(1, 1)
                    copy_odd(1, 3)
                    if kind != "diff":
                        normalised(1)
                    else:
                        dve.wait_ge(sem("pv_done"), i * 8 + (4 * (u0 + 1) + 6))
                        step(dve.reciprocal(rd[:, :, :], rs[:, :, :]))
                        step(dve.tensor_scalar(rd[:, 1, :], rd[:, 1, :], nlam, None, ALU.mult))
                        for u in range(2):
                            dve.tensor_tensor((tmpa, tmpb)[u][:, 0, :].rearrange("p (b n) -> p b n", b=NB),
                                              bank[6 + u][:, :].rearrange("p (b n) -> p b n", b=NB),
                                              rd[:, u, :].unsqueeze(2).to_broadcast([P, NB, P]), ALU.mult)\
                               .then_inc(sem("y_read"), 1)
                        dve.wait_ge(sem("y_read"), i * 2 + (u0 + 4))
                        step(dve.tensor_tensor(yt[:, :, cut(i * P + 4 * P, P)],
                                               tmpa[:, 0, :].rearrange("p (b n) -> p b n", b=NB),
                                               tmpb[:, 0, :].rearrange("p (b n) -> p b n", b=NB), ALU.add))

            def turn(v):
                for t in range(KT):
                    dve.wait_ge(sem("turn_high"), KT * v + t + 1)
                    dve.scalar_tensor_tensor(xl[:, t, :], bank[t % 2][:, :], col("one_scale" if v else "subln", t),
                                             xh[:, t, :].bitcast(F32), ALU.mult, ALU.subtract)\
                       .then_inc(sem("turn_read"), 1)

            dve.wait_ge(inputs_landed, 7 * 16)
            dve.wait_ge(sem("table_mm"), 1)
            for j in range(2):
                c = slice(j * TW // 2, (j + 1) * TW // 2)
                dve.tensor_tensor(tt[:, c], bank[j][0:ROWS, 0:TW // 2], ad[:, c], ALU.add)\
                   .then_inc(sem("table_read"), 1)
            dve.wait_ge(sem("table_read"), 2)
            lam_col = col("lru_lambda", 0, 8)
            dve.sem_inc(table_ready, 1)
            for k in range(2):
                step(dve.tensor_tensor(tmpa[:, 0, 0:64], lamb[:, 2 * k, :], lamb[:, 2 * k + 1, :], ALU.mult))
                dve.tensor_reduce(lam2[:, k:k + 1], tmpa[:, 0, 0:64], AX.X, ALU.add).then_inc(sem("lambda_sums"), 1)
                dve.wait_ge(sem("lambda_sums"), k + 1)
            step(dve.tensor_scalar(col("qk_norm", 0, 8), col("qk_norm", 0, 8), 128 ** -0.5, None, ALU.mult))
            step(dve.tensor_tensor(col("subln", 0, 8), col("subln", 0, 8), col("subln_factor", 0, 8), ALU.mult))
            dve.wait_ge(sem("lambda_exp"), 2)
            step(dve.tensor_scalar(t2, t1, 2.0, None, ALU.add))
            step(dve.reciprocal(t2, t2))
            step(dve.tensor_tensor(t1, t1, t2, ALU.mult))
            step(dve.tensor_tensor(t2, t1, t1, ALU.mult))
            step(dve.tensor_scalar(t3, t2, 1.0 / 15, None, ALU.mult))
            for k in (13, 11, 9, 7, 5, 3):
                step(dve.scalar_tensor_tensor(t3, t3, 1.0 / k, t2, ALU.add, ALU.mult))
            step(dve.scalar_tensor_tensor(t3, t3, 1.0, t1, ALU.add, ALU.mult))
            step(dve.tensor_scalar(t4, lam_col, -1.0, 0.0, ALU.mult, ALU.max))
            step(dve.scalar_tensor_tensor(t3, t3, 2.0, t4, ALU.mult, ALU.add))
            step(dve.tensor_scalar(decay8, t3, 8.0, None, ALU.mult))
            step(dve.tensor_scalar(ndecay8, t3, -8.0, None, ALU.mult))
            step(dve.tensor_tensor(nlam, lam2[:, 1:2], lam2[:, 0:1], ALU.subtract))
            step(dve.tensor_scalar(nlam, nlam, -LAM_INIT, None, ALU.add))
            norm(0, "norm_mix", 0)
            for i in repeat(dve, 8, step, 2):
                for c in range(2):
                    dve.wait_ge(sem("qk_sum"), i * 2 + (c + 3))
                    dve.tensor_scalar(tmpa[:, c, :], bank[c][:, :], 1.0 / P, EPS, ALU.mult, ALU.add)\
                       .then_inc(sem("qk_sum_read"), 1)
                for c in range(2):
                    dve.wait_ge(sem("qk_std"), i * 2 + (c + 1))
                    step(dve.reciprocal(tmpa[:, c, :], tmpa[:, c, :]))
                    t = tile(qk, i * 2 + c)
                    dve.scalar_tensor_tensor(t, t, col("qk_norm", i * 2 + c), tmpa[:, c, :], ALU.mult, ALU.mult)\
                       .then_inc(sem("qk_normed"), 1)
                dve.wait_ge(sem("qk_normed"), i * 2 + 2)
            for h in repeat(dve, 8, step, 4):
                for m, kb in enumerate(reversed(range(NB))):
                    w, z = sp[:, kb, kb * P:S], bank[kb][:, 0:S - kb * P]
                    dve.wait_ge(sem("ln_ready"), h * 4 + (m + 1))
                    step(dve.scalar_tensor_tensor(w, z, 0.0, w, ALU.max, ALU.add))
                    d = sp[:, kb, kb * P:(kb + 1) * P]
                    dve.tensor_tensor(d, d, mask01, ALU.mult).then_inc(sem("sp_ready"), 1)
            for t in range(KT):
                dve.wait_ge(sem("yh0_ready"), t + 1)
                dve.tensor_tensor(yl[:, t, :], qk[:, t, :], yh[:, t, :].bitcast(F32), ALU.subtract)\
                   .then_inc(sem("yl0_ready"), 1)
            products("gate2", True, "g2_ready", "g2_gate", "g2_prod")
            for b in range(2):
                for t in (pu, pa):
                    dve.memset(t[:, b, 0:16], 0.0).then_inc(sem("pads_ready"), 1)
            dve.wait_ge(sem("pads_ready"), 4)
            for t in range(KT):
                g, b = t // 2, t % 2
                w = WINDOWS[g]
                dve.wait_ge(sem("pool_read"), t + 5)
                src, dst, shift = pu[:, b, :], pa[:, 0, :], 1
                for n in range(g + 1):
                    step(dve.tensor_tensor(dst[:, 16:16 + S], src[:, 16:16 + S], src[:, 16 - shift:16 + S - shift],
                                           ALU.add))
                    src, dst, shift = dst, pa[:, 1 - n % 2, :], shift * 2
                step(dve.tensor_tensor(src[:, 16:32], src[:, 16:32], col("edge", 16 * g, 16), ALU.mult))
                dve.scalar_tensor_tensor(tmpb[:, b, :], src[:, 16:16 + S], 1.0 / w, pu[:, b, 16:16 + S], ALU.mult,
                                         ALU.subtract).then_inc(sem("p_ready_value"), 1)
                dve.wait_ge(sem("p_high"), t + 1)
                dve.tensor_tensor(yl[:, t, :], tmpb[:, b, :], yh[:, t, :].bitcast(F32), ALU.subtract)\
                   .then_inc(sem("p_low"), 1)
            for t in range(KT):
                dve.wait_ge(sem("wpool_high"), t + 1)
                dve.scalar_tensor_tensor(yl[:, t, :], bank[t % 4][:, :], col("pool_scale", t),
                                         yh[:, t, :].bitcast(F32), ALU.mult, ALU.subtract)\
                   .then_inc(sem("wpool_low"), 1)
            dve.wait_ge(sem("g2_prod"), 10)
            products("gate0", False, "g0_ready", "g0_gate", "g0_prod")
            for t in range(KT + 1):
                if t < KT:
                    x = xc[:, t % 2, :]
                    dve.wait_ge(sem("lru_base"), t + 1)
                    for k in (1, 2, 3):
                        dve.scalar_tensor_tensor(x[:, k:S], bank[t % 4][:, 0:S - k], col("conv_w", 8 * (3 - k) + t),
                                                 x[:, k:S], ALU.mult, ALU.add).then_inc(sem("lru_conv"), 1)
                        dve.wait_ge(sem("lru_conv"), 3 * t + k)
                if t:
                    u, c = t - 1, (t - 1) % 2
                    dve.wait_ge(sem("lru_a"), u + 1)
                    dve.tensor_tensor(tmpa[:, c, :], aa[:, c, :], aa[:, c, :], ALU.mult).then_inc(sem("lru_m2"), 1)
                    dve.wait_ge(sem("lru_m2"), 2 * u + 1)
                    dve.scalar_tensor_tensor(tmpa[:, c, :], tmpa[:, c, :], 1.0, tmpb[:, c, :], ALU.add, ALU.mult)\
                       .then_inc(sem("lru_m2"), 1)
                    i_ = ii[:, c, :]
                    dve.tensor_tensor(i_, i_, xc[:, c, :], ALU.mult).then_inc(sem("lru_h"), 1)
                    dve.wait_ge(sem("lru_mult"), u + 1)
                    dve.wait_ge(sem("lru_h"), 3 * u + 1)
                    dve.tensor_tensor(i_, i_, tmpa[:, c, :], ALU.mult).then_inc(sem("lru_h"), 1)
                    dve.wait_ge(sem("lru_h"), 3 * u + 2)
                    dve.tensor_tensor_scan(xc[:, c, :], aa[:, c, :], i_, 0.0, ALU.mult, ALU.add)\
                       .then_inc(sem("lru_h"), 1)
                    dve.wait_ge(sem("lru_high"), u + 1)
                    dve.tensor_tensor(yl[:, u, :], xc[:, c, :], yh[:, u, :].bitcast(F32), ALU.subtract)\
                       .then_inc(sem("lru_low"), 1)
            products("gate1", False, "g1_ready", "g1_gate", "g1_prod")
            for t in range(KT):
                dve.sem_inc(sem("merged_ready"), 1)
            for t in range(KT):
                dve.wait_ge(sem("yh1_ready"), t + 1)
                dve.tensor_tensor(yl[:, t, :], merged[:, t, :], yh[:, t, :].bitcast(F32), ALU.subtract)\
                   .then_inc(sem("yl1_ready"), 1)
            residual(4, "out_ready", "out_read", 1)
            ffn(0, 1, "norm_ffn", 0)
            norm(2, "even_norm", 0)
            attend("moba", 4, 0, 0)
            attend("diff", 4, 8, 4)
            for h in range(4):
                y = yt[:, :, (4 + h) * P:(5 + h) * P]
                w = tmpa[:, 0, :].rearrange("p (b n) -> p b n", b=NB)
                step(dve.tensor_tensor(w, y, y, ALU.mult))
                step(dve.tensor_reduce(dss[:, :, h:h + 1], w, AX.X, ALU.add))
            dve.tensor_scalar(dss, dss, 1.0 / P, EPS, ALU.mult, ALU.add).then_inc(sem("diff_var"), 1)
            dve.wait_ge(sem("diff_std"), 1)
            step(dve.reciprocal(dss, dss))
            for h in range(4):
                y = yt[:, :, (4 + h) * P:(5 + h) * P]
                last = dve.tensor_tensor(y, y, dss[:, :, h:h + 1].to_broadcast([P, NB, P]), ALU.mult)
            last.then_inc(sem("y_token"), 1)
            turn(0)
            residual(4, "eo_ready", "eo_read", 1)
            ffn(1, 3, "ffn_norm", 0)
            norm(4, "odd_norm", 0)
            attend("dil", 4, 16, 8)
            dve.wait_ge(sem("c_sum"), 3)
            for t in range(2):
                dve.tensor_scalar(tmpa[:, t, :], bank[6 + t][:, :], 1.0 / (2 * P, P)[t], EPS, ALU.mult, ALU.add)\
                   .then_inc(sem("c_var"), 1)
            for t in range(2):
                dve.wait_ge(sem("c_std"), t + 1)
                step(dve.reciprocal(tmpa[:, t, :], tmpa[:, t, :]))
            for t in range(3):
                c = qk[:, 8 + t, :]
                gain = col("mla_q_norm", t) if t < 2 else col("mla_kv_norm", 0)
                dve.scalar_tensor_tensor(c, c, gain, tmpa[:, t // 2, :], ALU.mult, ALU.mult)\
                   .then_inc(sem("c_normed"), 1)
            for t in range(3):
                dve.wait_ge(sem("ch_ready"), t + 1)
                dve.tensor_tensor(cl[:, t, :], qk[:, 8 + t, :], ch[:, t, :].bitcast(F32), ALU.subtract)\
                   .then_inc(sem("cl_ready"), 1)
            dve.wait_ge(sem("rope_landed"), 16)
            for n, t in enumerate((12, 13, 11)):
                x = qk[:, t, :]
                dve.wait_ge(sem("rotated"), n + 1)
                step(dve.tensor_tensor(tmpb[:, 0, :], bank[4 + n][:, :], rope[:, 1, :], ALU.mult))
                step(dve.tensor_tensor(x, x, rope[:, 0, :], ALU.mult))
                dve.tensor_tensor(x, x, tmpb[:, 0, :], ALU.add).then_inc(sem("roped"), 1)
                dve.wait_ge(sem("roped"), n + 1)
            attend("mla", 2, 24, 12)
            dve.drain().then_inc(sem("y_token"), 1)
            turn(1)
            residual(4, "oo_ready", "oo_read", 1)
            ffn(2, 5, "ffn_norm", 8)
            norm(6, "final", 0)


def _chunk(w):
    k = w.shape[0] // P
    out = np.zeros((P, CHUNK), w.dtype)
    out[:, 0:k * w.shape[1]] = w.reshape(k, P, w.shape[1]).transpose(1, 0, 2).reshape(P, -1)
    return out


def _chunks(w):
    return [_chunk(w[:, c:c + 2 * P]) for c in range(0, w.shape[1], 2 * P)]


def _pairs(a, b):
    return [c for pair in zip(_chunks(a), _chunks(b)) for c in pair]


def _downs(w):
    return [w[h * DOWN:(h + 1) * DOWN, t * P:(t + 1) * P].reshape(HALF, P, P).transpose(1, 0, 2).reshape(P, DOWN)
            for t in range(KT) for h in range(2)]


def _columns(v):
    return np.asarray(v).reshape(-1, P).T


def _bucket(distance):
    n = np.maximum(distance, 0)
    f = np.maximum(n, 1).astype(np.float32)
    large = 16 + (np.log(f / np.float32(16)) / np.float32(math.log(1024 / 16)) * np.float32(16)).astype(np.int32)
    return np.where(n < 16, n, np.minimum(large, 31))


def _constants():
    p = np.arange(P)
    upper = (p[None, :] > p[:, None]).astype(np.float32)
    rot = np.zeros((P, P), np.float32)
    for h in (0, 64):
        for j in range(32):
            rot[h + 32 + j, h + j] = -1.0
            rot[h + j, h + 32 + j] = 1.0
    mats = np.stack([np.ones((P, P)), np.eye(P), -(p[:, None] >= p[None, :]).astype(np.float32),
                     -np.ones((P, P)), np.where(upper > 0, 0.0, NEG), upper, rot], axis=1).astype(np.float32)
    freq = (np.float32(10000.0) ** (-np.arange(32, dtype=np.float32) / np.float32(32))).astype(np.float32)
    angle = (np.arange(S, dtype=np.float32)[None, :] * freq[:, None]).astype(np.float32)
    rope = np.stack([np.tile(np.cos(angle), (4, 1)), np.tile(np.sin(angle), (4, 1))], axis=1).astype(np.float32)
    distance = np.arange(TW) - (P - 1)
    onehot = ((_bucket(distance)[None, :] == np.arange(32)[:, None]) & (distance >= 0)).astype(np.float32)
    causal = np.where(distance >= 0, 0.0, NEG)
    count = (distance <= 128).astype(int) + (distance % 4 == 0) + (distance % 16 == 0)
    dilated = np.where((distance >= 0) & (count > 0), np.log(np.maximum(count, 1)), NEG)
    add = np.stack([causal] * 12 + [dilated] * 8 + [causal]).astype(np.float32)
    edge = np.ones((P, 64), np.float32)
    for g, w in enumerate(WINDOWS):
        edge[:, 16 * g:16 * g + 16] = w / np.minimum(np.arange(1, 17), w)
    return mats, rope, onehot, add, edge


def _layout(x, norm_mix, w_in, b_gate, w_pool, pool_scale, conv_w, conv_b, w_rg, b_rg, w_ig, b_ig, lru_lambda,
            q_norm, k_norm, w_branch, w_out, norm_ffn, w_ffn_gate, w_ffn_up, w_ffn_down, rel_bias_2, even_norm1_2,
            even_w_in_2, diff_lambda_2, diff_subln_2, even_w_out_2, odd_norm1_2, odd_w_in_2, mla_q_norm_2,
            mla_w_uq_2, mla_kv_norm_2, mla_w_ukv_2, odd_w_out_2, ffn_norm_2, ffn_w_in_2, ffn_conv_w_2,
            ffn_conv_b_2, ffn_w_out_2, final_norm_2):
    wi, wb = w_in[0], w_branch[0]
    ev, od = even_w_in_2[0], odd_w_in_2[0]
    gate = [wi[:, 5 * D + b * D:5 * D + (b + 1) * D] for b in range(3)]
    ffn = lambda l: _pairs(ffn_w_in_2[l][:, FF:], ffn_w_in_2[l][:, :FF])
    uq = mla_w_uq_2[0].reshape(2 * P, 4, 192)
    uq = np.concatenate([uq[:, :, :P].reshape(2 * P, -1), uq[:, :, P:].reshape(2 * P, -1)], axis=1)
    ukv = mla_w_ukv_2[0].reshape(P, 4, 2 * P)
    ukv = np.concatenate([ukv[:, :, :P].reshape(P, -1), ukv[:, :, P:].reshape(P, -1)], axis=1)
    wp = w_pool[0].reshape(4, 2, P, 2 * P).transpose(2, 0, 1, 3).reshape(P, 2, CHUNK // 2)
    wpool = [np.concatenate([wp[:, c], np.zeros_like(wp[:, c])], axis=1) for c in range(2)]
    ckv = np.concatenate([od[:, 1792:1920], od[:, 1920:1984], od[:, 1920:1984]], axis=1)
    main = (_chunks(wi[:, 2 * D:4 * D]) + _chunks(wi[:, 4 * D:5 * D]) + _pairs(gate[2], wb[2])
            + _chunks(wi[:, 0:D]) + wpool + _pairs(gate[0], wb[0]) + _chunks(wi[:, D:2 * D]) + _pairs(gate[1], wb[1])
            + _chunks(w_out[0]) + _pairs(w_ffn_gate[0], w_ffn_up[0])
            + _chunks(ev[:, 0:1024]) + _chunks(ev[:, 1536:2560])
            + _chunks(ev[:, 1024:1536]) + _chunks(ev[:, 2560:3072]) + _chunks(even_w_out_2[0]) + ffn(0)
            + _chunks(od[:, 0:1024]) + _chunks(od[:, 1536:1792]) + _chunks(ckv) + _chunks(od[:, 1024:1536])
            + [_chunk(uq), _chunk(ukv)] + _chunks(odd_w_out_2[0]) + ffn(1))
    assert len(main) == MAIN, (len(main), MAIN)
    downs = _downs(w_ffn_down[0]) + _downs(ffn_w_out_2[0]) + _downs(ffn_w_out_2[1])
    mats, rope, onehot, add, edge = _constants()
    one = np.ones((P, 1), np.float32)
    eighth = 0.125 * one
    cols = [_columns(v) for v in (norm_mix, b_gate, pool_scale, conv_w, conv_b, b_rg, b_ig, lru_lambda)]
    cols += [_columns(q_norm)] * 8 + [_columns(k_norm)] * 8
    cols += [_columns(v) for v in (norm_ffn, even_norm1_2, odd_norm1_2, mla_q_norm_2, mla_kv_norm_2, ffn_norm_2,
                                   final_norm_2, ffn_conv_b_2, ffn_conv_w_2)]
    cols += [one] * 4 + [_columns(diff_subln_2)] * 4
    cols += [one] * 16 + ([eighth] * 4 + [one] * 4) * 2 + [eighth] * 4 + [one] * 8
    cols += [one] * 4 + [(1.0 - LAM_INIT) * one] * 4 + [edge]
    cols = np.ascontiguousarray(np.concatenate(cols, axis=1), dtype=np.float32)
    assert cols.shape == (P, NCOL), (cols.shape, NCOL)
    rg = np.zeros((P, 16, P), np.float32)
    for k, w in enumerate((w_rg[0], w_ig[0])):
        for t in range(KT):
            rg[0:64, 8 * k + t, 0:64] = w[2 * t]
            rg[64:P, 8 * k + t, 64:P] = w[2 * t + 1]
    rel = np.zeros((32, ROWS + 3), np.float32)
    rel[:, 0:20] = rel_bias_2
    return {
        "wmain": np.stack(main), "wdown": np.stack(downs),
        "x": np.ascontiguousarray(x[0].T.reshape(KT, P, S).transpose(1, 0, 2)),
        "cols": cols, "mats": np.ascontiguousarray(mats), "rg": rg, "rope": np.ascontiguousarray(rope),
        "onehot": onehot, "add": add, "rel": rel,
        "lam": np.ascontiguousarray(np.broadcast_to(diff_lambda_2[0][None], (P, 4, 64))),
    }


def kernel(**inputs):
    import concourse.bacc as bacc
    from concourse.bass_utils import run_bass_kernel_spmd

    arrays = _layout(**{k: np.asarray(v) for k, v in inputs.items()})
    nc = bacc.Bacc("TRN2", target_bir_lowering=False, num_devices=1)
    args = [nc.dram_tensor(n, a.shape, F32, kind="ExternalInput").ap() for n, a in arrays.items()]
    out = nc.dram_tensor("out", (P, KT, S), F32, kind="ExternalOutput").ap()
    table = nc.dram_tensor("distance_table", (ROWS, TW), F32, kind="Internal").ap()
    program(nc, *args, out, table)
    r = run_bass_kernel_spmd(nc, [arrays], core_ids=[0])
    y = r.results[0]["out"]
    return np.ascontiguousarray(y.transpose(1, 0, 2).reshape(D, S).T)[None]
```

```python
from contextlib import ExitStack
import math

import numpy as np

import concourse.bass as bass
from concourse import mybir

F32 = mybir.dt.float32
F32R = mybir.dt.float32r
ALU = mybir.AluOpType
ACT = mybir.ActivationFunctionType
AX = mybir.AxisListType

P = 128
S = 512
D = 1024
KT = D // P
NB = S // P
FF = 2816
FT = FF // P
HALF = FT // 2
EPS = 1e-6
CHUNK = KT * 2 * P
DOWN = HALF * P
NEG = -1e30
TW = 640
WINDOWS = (2, 4, 8, 16)
LAM_INIT = 0.8 - 0.6 * math.exp(-0.3 * 0)
MASK_ROW = 20
ROWS = 21

STAGES = [("qk", 8, 0), ("v", 4, 0), ("gate2", 8, 0), ("pool", 4, 0), ("wpool", 2, 0), ("gate0", 8, 0),
          ("lru", 4, 0), ("gate1", 8, 0), ("out", 4, 0), ("ffn0", FT, 0), ("down0", 16, 1),
          ("eqk", 8, 0), ("ev", 4, 0), ("eout", 4, 0), ("ffn1", FT, 0), ("down1", 16, 1),
          ("oqk", 6, 0), ("ov", 2, 0), ("mla", 2, 0), ("oout", 4, 0), ("ffn2", FT, 0), ("down2", 16, 1)]
BASE, WHERE, COUNT = {}, {}, {name: count for name, count, _ in STAGES}
_n, _in = 0, [0, 0]
for _name, _count, _kind in STAGES:
    BASE[_name], WHERE[_name] = _n, _in[_kind]
    _n, _in[_kind] = _n + _count, _in[_kind] + _count
CHUNKS = _n
MAIN, DOWNS = _in

COLS = {}
_at = 0
for _name, _k in [("norm_mix", 8), ("b_gate", 24), ("pool_scale", 8), ("conv_w", 32), ("conv_b", 8), ("b_rg", 8),
                  ("b_ig", 8), ("lru_lambda", 8), ("qk_norm", 16), ("norm_ffn", 8), ("even_norm", 8),
                  ("odd_norm", 8), ("mla_q_norm", 2), ("mla_kv_norm", 1), ("ffn_norm", 16), ("final", 8),
                  ("ffn_b", 2 * FT), ("ffn_w", 6 * FT), ("subln", 8), ("one_scale", 16), ("even_scale", 16),
                  ("odd_scale", 12), ("subln_factor", 8), ("edge", 64)]:
    COLS[_name] = _at
    _at += _k
NCOL = _at


def program(nc, wmain, wdown, xin, cols_in, mats_in, rg_in, rope_in, onehot_in, add_in, rel_in, lam_in, out, table):
    base = nc.sbuf_base + 31 & ~31
    top = [base]

    def place(name, shape, dt=F32, at=None):
        size = int(np.prod(shape[1:])) * 4
        if at is None:
            at = top[0]
            top[0] += size + 31 & ~31
        return nc.alloc_sbuf_tensor_at(name, shape, dt, offset=at)

    raw = place("raw", [P, 2, CHUNK])
    wh = place("w_high", [P, 2, CHUNK], F32R)
    wl = place("w_low", [P, 2, CHUNK], F32R)
    xT = place("x_residual", [P, KT, S])
    xh = place("x_high", [P, KT, S], F32R)
    xl = place("x_low", [P, KT, S], F32R)
    cols = place("columns", [P, NCOL])
    mats = place("matrices", [P, 8, P])
    ones, ident, negtri, negones, negmask, mask01, small_rot, pick = (mats[:, j, :] for j in range(8))
    rstd = place("rstd_diagonals", [P, S])
    tmpa = place("temp_a", [P, 2, S])
    tmpb = place("temp_b", [P, 2, S])
    small = place("small", [P, 128])
    arena = top[0]
    T = S * 4

    def over(name, shape, tile, dt=F32):
        return place(name, shape, dt, at=arena + int(tile * T))

    ah = over("act_high", [P, FT, S], 0, F32R)
    al = over("act_low", [P, FT, S], FT, F32R)
    qk = over("qk", [P, 16, S], 0)
    vt = over("v_tokens", [P, NB, D], 16)
    yh = over("y_high", [P, KT, S], 8, F32R)
    yl = over("y_low", [P, KT, S], 16, F32R)
    merged = over("merged", [P, KT, S], 24)
    sq = over("squares", [P, 16, S], 24)
    sp = over("softplus", [P, 2, 3, S], 32)
    wz = over("sb_weights", [P, 3, S], 38)
    ks = over("k_stage", [P, S], 41)
    vs = over("v_stage", [P, NB, P], 42)
    pu = over("pool_u", [P, 2, 16 + S], 32)
    pa = over("pool_a", [P, 2, 16 + S], 35)
    rgw = over("rg_blocks", [P, 16, P], 38)
    xc = over("conv_out", [P, 2, S], 0)
    rr = over("r_gate", [P, 2, S], 2)
    ii = over("i_gate", [P, 2, S], 4)
    aa = over("decay", [P, 2, S], 6)
    yt = over("y_tokens", [P, NB, D], 24)
    tq = over("probs", [P, NB, S], 32)
    pts = over("probs_t", [P, 2, S], 36)
    qs = over("q_stage", [P, 2, S], 38)
    bt = over("bias", [P, 2, S], 40)
    rope = over("rope", [P, 2, S], 42)
    ch = over("c_high", [P, 3, S], 32, F32R)
    cl = over("c_low", [P, 3, S], 35, F32R)
    oh = over("onehot", [32, TW], 16)
    ad = over("table_add", [ROWS, TW], 18)
    tt = over("table", [ROWS, TW], 20)
    rb = over("rel_bias", [32, ROWS + 3], 22)
    lamb = over("lambda_rows", [P, 4, 64], 23)
    assert arena + 44 * T <= nc.sbuf_usable_end, (arena + 44 * T, nc.sbuf_usable_end)

    SPAN = ((0, 0), (1, 0), (2, 0), (1, 3 * P))

    nm = small[:, 0:8].rearrange("p (u q) -> p u q", u=2)
    rs = small[:, 8:16].rearrange("p (u q) -> p u q", u=2)
    rd = small[:, 16:24].rearrange("p (u q) -> p u q", u=2)
    dss = small[:, 24:40].rearrange("p (q h) -> p q h", q=NB)
    nlam = small[:, 40:41]
    decay8 = small[:, 48:56]
    ndecay8 = small[:, 56:64]
    t1, t2, t3, t4 = (small[:, 64 + 8 * j:72 + 8 * j] for j in range(4))
    lam2 = small[:, 96:98]
    token_rstd = small[:, 98:102]

    with ExitStack() as ctx:
        names = {}

        def sem(name):
            if name not in names:
                names[name] = ctx.enter_context(nc.semaphore(name))
            return names[name]

        bank = [ctx.enter_context(nc.psum_tensor(f"bank{b}", [P, S], F32)) for b in range(8)]

        raw_landed = [sem("raw_landed_0"), sem("raw_landed_1")]
        high_ready, low_ready = sem("high_ready"), sem("low_ready")
        x_landed, inputs_landed = sem("x_landed"), sem("inputs_landed")
        table_ready, table_stored = sem("table_ready"), sem("table_stored")
        out_stored = sem("out_stored")

        class Steps:

            def __init__(self, eng, semaphore):
                self.eng, self.semaphore, self.n, self.here = eng, semaphore, 0, 0

            def __call__(self, instruction):
                self.here += 1
                self.n = self.n + 1
                instruction.then_inc(self.semaphore, 1)
                self.eng.wait_ge(self.semaphore, self.n)

        def repeat(eng, rounds, steps=None, per=0):
            if rounds == 1:
                yield 0
                return
            first = steps.n if steps else 0
            with eng.Fori(0, rounds) as i:
                if steps:
                    steps.n, steps.here = i * per + first, 0
                yield i
                assert not steps or steps.here == per, (steps.here, per)
            if steps:
                steps.n = first + rounds * per

        def col(name, k, n=1):
            if type(k) is int:
                return cols[:, COLS[name] + k:COLS[name] + k + n]
            return cols[:, bass.ds(k + COLS[name], n)]

        def tile(t, k, n=1):
            if type(k) is int:
                return t[:, k, :]
            return t[:, bass.ds(k, 1), :].rearrange("p a s -> p (a s)")

        def in_pairs(eng, kinds, body, steps=None, per=()):
            for n, (kind, pairs, u0) in enumerate(kinds):
                for i in repeat(eng, pairs - 1, steps, per[n] if per else 0):
                    body((kind, u0, i, 0), (kind, u0, i, 1))
                    body((kind, u0, i, 1), (kind, u0, i + 1, 0))
                last = pairs - 1
                after = kinds[n + 1] if n + 1 < len(kinds) else None
                body((kind, u0, last, 0), (kind, u0, last, 1))
                body((kind, u0, last, 1), after and (after[0], after[2], 0, 0))

        def cut(k, n):
            return slice(k, k + n) if type(k) is int else bass.ds(k, n)

        block = ctx.enter_context(nc.Block())

        @block.sync
        def _(sp_):
            def stream(name, count, down):
                source, width = (wdown, DOWN) if down else (wmain, CHUNK)
                n0, at = BASE[name], WHERE[name]

                def load(i, c):
                    if n0 + c >= 2:
                        sp_.wait_ge(low_ready, i * 2 + (n0 + c - 1))
                    src = source[cut(i * 2 + (at + c), 1), :, :].rearrange("a p n -> (a p) n")
                    sp_.dma_start(raw[:, c, 0:width], src).then_inc(raw_landed[c], 16)

                rounds = count // 2
                if n0 == 0:
                    load(0, 0)
                    load(0, 1)
                    n0, at, rounds = 2, at + 2, rounds - 1
                for i in repeat(sp_, rounds):
                    for c in range(2):
                        load(i, c)

            sp_.dma_start(xT[:, :, :], xin).then_inc(x_landed, 16)
            sp_.dma_start(cols[:, :], cols_in).then_inc(x_landed, 16)
            sp_.dma_start(mats[:, :, :], mats_in).then_inc(x_landed, 16)
            sp_.dma_start(oh[:, :], onehot_in).then_inc(inputs_landed, 16)
            sp_.dma_start(ad[:, :], add_in).then_inc(inputs_landed, 16)
            sp_.dma_start(rb[:, :], rel_in).then_inc(inputs_landed, 16)
            sp_.dma_start(lamb[:, :, :], lam_in).then_inc(inputs_landed, 16)
            for name, count, down in STAGES:
                stream(name, count, down)
            for t in range(KT):
                sp_.wait_ge(sem("final_ready"), t + 1)
                sp_.dma_start(out[:, t, :], tile(qk, t)).then_inc(out_stored, 16)
            sp_.wait_ge(out_stored, 16 * KT)

        @block.tensor
        def _(pe):
            def products(target, stationary, moving, start=True, stop=True):
                n = len(stationary)
                for k, ((sh, sl), (mh, ml)) in enumerate(zip(stationary, moving)):
                    pe.matmul(target, sh, ml, start=start and k == 0, stop=False)
                    pe.matmul(target, sh, mh, start=False, stop=False)
                    last = pe.matmul(target, sl, mh, start=False, stop=stop and k == n - 1)
                return last

            def weights(c, j, kts=KT, width=2 * P, at=0):
                w = [slice(at + k * width + j * P, at + k * width + (j + 1) * P) for k in range(kts)]
                return [(wh[:, c, s], wl[:, c, s]) for s in w]

            def acts(h, l, first=0, kts=KT):
                return [(h[:, first + k, :], l[:, first + k, :]) for k in range(kts)]

            def chunk(i, n):
                pe.wait_ge(low_ready, i + (n + 1))

            def credit(name, n):
                pe.sem_inc(sem(name), n)

            def norm_sum(v):
                pe.wait_ge(sem("squares_ready"), v + 1)
                for b in range(NB):
                    last = pe.matmul(bank[7][:, b:b + 1], tmpb[:, 0, b * P:(b + 1) * P], ones[:, 0:1],
                                     start=True, stop=True)
                last.then_inc(sem("token_sums"), 1)
                pe.wait_ge(sem("diagonals_ready"), v + 1)
                pe.matmul(bank[7][:, :], ones, rstd[:, :], start=True, stop=True).then_inc(sem("rstd_ready"), 1)

            def both_columns(c, x, read, target, ready, x_ready):
                for j in range(2):
                    pe.wait_ge(sem(read), j + 1)
                for k in range(KT):
                    pe.wait_ge(sem(x_ready[0]), x_ready[1] + k + 1)
                    for j in range(2):
                        last = products(bank[target + j][:, :], weights(c, j)[k:k + 1], x[k:k + 1],
                                        start=k == 0, stop=k == KT - 1)
                        if k == KT - 1:
                            last.then_inc(sem(ready), 1)

            def feature_major(name, chunks, x, ready, read, free_after, x_ready):
                for s, v in free_after:
                    pe.wait_ge(sem(s), v)
                credit(read, 4)
                n0 = BASE[name]

                def tiles(i, n, c, j):
                    pe.wait_ge(sem(read), i * 4 + (2 * n + j + 1))
                    products(bank[2 * c + j][:, :], weights(c, j), x).then_inc(sem(ready), 1)

                chunk(0, n0)
                both_columns(0, x, read, 0, ready, x_ready)
                chunk(0, n0 + 1)
                tiles(0, 1, 1, 0)
                tiles(0, 1, 1, 1)
                for i in repeat(pe, chunks // 2 - 1):
                    for c in range(2):
                        chunk(i * 2, n0 + 2 + c)
                        for j in range(2):
                            tiles(i, 2 + c, c, j)

            def token_major(name, chunks, x, ready, read, free_after):
                for s, v in free_after:
                    pe.wait_ge(sem(s), v)
                credit(read, 4)
                n0 = BASE[name]
                for i in repeat(pe, chunks // 2):
                    for c in range(2):
                        chunk(i * 2, n0 + c)
                        w = [(wh[:, c, k * 2 * P:(k + 1) * 2 * P], wl[:, c, k * 2 * P:(k + 1) * 2 * P])
                             for k in range(KT)]
                        for j in range(2):
                            pe.wait_ge(sem(read), i * 4 + (2 * c + j + 1))
                            for b in range(2):
                                tokens = slice((2 * j + b) * P, (2 * j + b + 1) * P)
                                last = products(bank[2 * c + j][:, b * 2 * P:(b + 1) * 2 * P],
                                                [(h[:, tokens], l[:, tokens]) for h, l in x], w)
                            last.then_inc(sem(ready), 1)

            def paired(name, chunks, x0, x1, ready, read0, read1, free_after, x0_ready=None, x1_ready=None):
                for s, v in free_after:
                    pe.wait_ge(sem(s), v)
                credit(read0, 2)
                credit(read1, 2)
                n0 = BASE[name]

                def part(i, n, c, x, read, x_ready=None):
                    chunk(i * 2, n0 + 2 * n + c)
                    if x_ready:
                        both_columns(c, x, read, 2 * c, ready, x_ready)
                        return
                    for j in range(2):
                        pe.wait_ge(sem(read), i * 2 + (2 * n + j + 1))
                        products(bank[2 * c + j][:, :], weights(c, j), x).then_inc(sem(ready), 1)

                part(0, 0, 0, x0, read0, x0_ready)
                part(0, 0, 1, x1, read1, x1_ready)
                for i in repeat(pe, chunks // 2 - 1):
                    part(i, 1, 0, x0, read0)
                    part(i, 1, 1, x1, read1)

            def down(name, x, ready, read, free_after, x_ready):
                for s, v in free_after:
                    pe.wait_ge(sem(s), v)
                credit(read, 2)
                n0 = BASE[name]
                for i in repeat(pe, 4):
                    for j in range(2):
                        pe.wait_ge(sem(read), i * 2 + (j + 1))
                        for c in range(2):
                            chunk(i * 4, n0 + 2 * j + c)
                            pe.wait_ge(sem(x_ready), (c + 1) * HALF)
                            products(bank[j][:, :], weights(c, 0, HALF, P), x[c * HALF:(c + 1) * HALF],
                                     start=c == 0, stop=c == 1).then_inc(sem(ready), 1)

            def turn(v, free_after):
                for s, n in free_after:
                    pe.wait_ge(sem(s), n)
                for t in range(KT):
                    if t >= 2:
                        pe.wait_ge(sem("turn_read"), KT * v + t - 1)
                    for b in range(NB):
                        last = pe.transpose(bank[4 + t % 2][:, b * P:(b + 1) * P], yt[:, b, t * P:(t + 1) * P], ident)
                    last.then_inc(sem("turned"), 1)

            def attend(*kinds):
                if kinds[0][0] == "moba":
                    for name, n in (("s_ready", 8), ("s_read", 8), ("pt_even", 1), ("pt_odd", 1), ("pv_done", 2),
                                    ("t_ready", 4), ("y_read", 2)):
                        credit(name, n)

                def scores(unit, b):
                    kind, u0, i, u = unit
                    n = (b + 1) * P
                    q = slice(b * P, n)
                    if b == 0:
                        pe.wait_ge(sem("q_staged"), i * 2 + (u0 + u + 1))
                    pe.wait_ge(sem("s_read"), i * 8 + (4 * (u0 + u) + b + 5))
                    if kind == "mla":
                        half = slice(64 * u, 64 * u + 64)
                        pe.matmul(bank[b][:, 0:n], qs[:, u, q], qk[:, i * 2 + (4 + u), 0:n], start=True, stop=False)
                        last = pe.matmul(bank[b][:, 0:n], tmpa[half, i, q], qk[half, 11, 0:n],
                                         start=False, stop=True)
                    else:
                        k = {"moba": 4, "diff": 12, "dil": 4}[kind]
                        last = pe.matmul(bank[b][:, 0:n], qs[:, u, q], tile(qk, i + k)[:, 0:n],
                                         start=True, stop=True)
                    last.then_inc(sem("s_ready"), 1)

                def transposes(unit, b):
                    kind, u0, i, u = unit
                    pe.wait_ge(sem("p_ready"), i * 8 + (4 * (u0 + u) + b + 1))
                    pe.wait_ge(sem("pt_odd" if b % 2 else "pt_even"), i * 4 + (2 * (u0 + u) + b // 2 + 1))
                    for k in range(b + 1):
                        last = pe.transpose(bank[4 + b % 2][:, k * P:(k + 1) * P], tq[:, b, k * P:(k + 1) * P],
                                            ident)
                    last.then_inc(sem("t_ready"), 1)

                def values(unit, b):
                    kind, u0, i, u = unit
                    pe.wait_ge(sem("pt_odd" if b % 2 else "pt_even"), i * 4 + (2 * (u0 + u) + b // 2 + 2))
                    if b == 0:
                        pe.wait_ge(sem("y_read"), i * 2 + (u0 + u + 1))
                    dh, c = {"moba": (64, i * P + 64 * u), "dil": (64, i * P + 64 * u), "diff": (P, i * P + 4 * P),
                             "mla": (P, i * (2 * P) + (4 + u) * P)}[kind]
                    for k in range(b + 1):
                        last = pe.matmul(bank[6 + u][:, b * dh:(b + 1) * dh],
                                         pts[:, b % 2, k * P:(k + 1) * P], vt[:, k, cut(c, dh)],
                                         start=k == 0, stop=k == b)
                    last.then_inc(sem("pv_done"), 1)

                def body(unit, following):
                    for b in range(NB):
                        transposes(unit, b)
                        if following:
                            scores(following, b)
                        if b:
                            values(unit, b - 1)
                    values(unit, NB - 1)

                for b in range(NB):
                    scores((kinds[0][0], kinds[0][2], 0, 0), b)
                in_pairs(pe, kinds, body)

            norm_sum(0)
            feature_major("qk", 8, acts(xh, xl), "qk_ready", "qk_read", [], ("xl_ready", 0))
            pe.wait_ge(inputs_landed, 4 * 16)
            for j in range(2):
                last = pe.matmul(bank[5 + j][0:ROWS, 0:TW // 2], rb[:, 0:ROWS], oh[:, j * TW // 2:(j + 1) * TW // 2],
                                 start=True, stop=True)
            last.then_inc(sem("table_mm"), 1)
            for t in range(16):
                pe.wait_ge(sem("qk_read"), t + 5)
                last = pe.matmul(bank[4][0:16, :], pick[:, 15 - t:31 - t], sq[:, t, :], start=t == 0, stop=t == 15)
            last.then_inc(sem("qk_sum"), 1)
            token_major("v", 4, acts(xh, xl), "v_ready", "v_read", [])
            pe.wait_ge(sem("v_read"), 12)
            pe.wait_ge(sem("qk_rstd"), 1)
            for t in range(16):
                if t >= 4:
                    pe.wait_ge(sem("qk_normed"), t - 3)
                pe.matmul(bank[t % 4][:, :], ident[0:16, t:t + 1].to_broadcast([16, P]), rstd[0:16, :],
                          start=True, stop=True).then_inc(sem("qk_spread"), 1)
            pe.wait_ge(sem("qk_normed"), 16)
            pe.sem_inc(sem("sy_read"), 2)

            def span(kb, jb):
                at = SPAN[kb][1]
                return slice(at + (jb - kb) * P, at + S - kb * P)

            def sb_scores(i, h):
                c = h % 2
                pe.wait_ge(sem("k_staged"), i + (h + 1))
                if h >= 2:
                    pe.wait_ge(sem("w_ready"), i * 3 + 3 * (h - 1))
                for j, kbs in enumerate(((0,), (1, 3), (2,))):
                    for kb in kbs:
                        last = pe.matmul(bank[3 * c + j][:, span(kb, kb)], ks[:, kb * P:(kb + 1) * P],
                                         tile(qk, i + h)[:, kb * P:S], start=kb < 3, stop=False,
                                         skip_group_check=True)
                    last.then_inc(sem("z_ready"), 1)

            def sb_sums(i, h):
                c = h % 2
                pe.wait_ge(sem("sp_ready"), i * 2 + 2 * (h + 1))
                for j, kbs in enumerate(((0,), (1, 3), (2,))):
                    for kb in kbs:
                        for jb in range(kb, NB):
                            pe.matmul(bank[3 * c + j][:, span(kb, jb)], negtri if jb == kb else negones,
                                      sp[:, c, SPAN[jb][0], span(jb, jb)], start=False, stop=False,
                                      skip_group_check=True)
                        at = SPAN[kb][1]
                        last = pe.matmul(bank[3 * c + j][:, at:at + P], ident, negmask, start=False, stop=True,
                                         skip_group_check=True)
                    last.then_inc(sem("z_done"), 1)

            def sb_values(i, h):
                pe.wait_ge(sem("v_staged"), i + (h + 1))
                pe.wait_ge(sem("w_ready"), i * 3 + 3 * (h + 1))
                pe.wait_ge(sem("sy_read"), i + (h + 1))
                for kb in range(NB):
                    last = pe.matmul(bank[6 + h % 2][:, kb * P:S], vs[:, kb, :], wz[:, SPAN[kb][0], span(kb, kb)],
                                     start=kb == 0, stop=kb == NB - 1)
                last.then_inc(sem("sy_ready"), 1)

            sb_scores(0, 0)
            sb_scores(0, 1)
            sb_sums(0, 0)
            for i in repeat(pe, 3):
                for h in (1, 2):
                    sb_scores(i * 2, h + 1)
                    sb_values(i * 2, h - 1)
                    sb_sums(i * 2, h)
            sb_values(0, 6)
            sb_sums(0, 7)
            sb_values(0, 7)
            paired("gate2", 8, acts(xh, xl), acts(yh, yl), "g2_ready", "g2_gate", "g2_prod", [("sy_read", 10)],
                   x1_ready=("yl0_ready", 0))
            feature_major("pool", 4, acts(xh, xl), "pool_ready", "pool_read", [("g2_gate", 10), ("g2_prod", 10)],
                          ("xl_ready", 0))
            pe.wait_ge(sem("pool_read"), 12)
            for c in range(2):
                chunk(0, BASE["wpool"] + c)
                for g in range(2):
                    pe.wait_ge(sem("p_low"), 4 * c + 2 * g + 2)
                    for j in range(2):
                        f = 4 * c + 2 * g
                        if c:
                            pe.wait_ge(sem("wpool_low"), 2 * g + j + 1)
                        products(bank[2 * g + j][:, :], weights(c, j, 2, at=g * 2 * 2 * P),
                                 acts(yh, yl, f, 2)).then_inc(sem("wpool_ready"), 1)
            pe.wait_ge(sem("wpool_low"), 8)
            paired("gate0", 8, acts(xh, xl), acts(yh, yl), "g0_ready", "g0_gate", "g0_prod", [])
            pe.wait_ge(sem("g0_gate"), 10)
            pe.wait_ge(sem("g0_prod"), 10)
            pe.wait_ge(sem("rg_landed"), 16)

            def lru_gates(t):
                pe.wait_ge(sem("lru_conv"), 3 * t + 3)
                if t >= 2:
                    pe.wait_ge(sem("lru_sigmoid"), 2 * (t - 2) + 2)
                pe.matmul(bank[4 + 2 * (t % 2)][:, :], rgw[:, t, :], xc[:, t % 2, :], start=True, stop=True)
                pe.matmul(bank[5 + 2 * (t % 2)][:, :], rgw[:, 8 + t, :], xc[:, t % 2, :], start=True,
                          stop=True).then_inc(sem("lru_gate"), 1)

            for t in range(KT):
                if t % 2 == 0:
                    chunk(0, BASE["lru"] + t // 2)
                if t >= 4:
                    pe.wait_ge(sem("lru_conv"), 3 * (t - 4) + 3)
                products(bank[t % 4][:, :], weights(t // 2 % 2, t % 2), acts(xh, xl)).then_inc(sem("lru_ready"), 1)
                if t:
                    lru_gates(t - 1)
            lru_gates(KT - 1)
            paired("gate1", 8, acts(xh, xl), acts(yh, yl), "g1_ready", "g1_gate", "g1_prod", [("lru_conv", 24)],
                   x1_ready=("lru_low", 0))
            feature_major("out", 4, acts(yh, yl), "out_ready", "out_read", [("g1_gate", 10), ("g1_prod", 10)],
                          ("yl1_ready", 0))

            def ffn(n, v):
                norm_sum(v)
                paired(f"ffn{n}", FT, acts(xh, xl), acts(xh, xl), f"f{n}_ready", f"f{n}_gate", f"f{n}_prod", [],
                       x0_ready=("xl_ready", KT * v))
                down(f"down{n}", acts(ah, al, 0, FT), f"d{n}_ready", f"d{n}_read", [(f"f{n}_gate", FT + 2)],
                     f"f{n}_low")

            ffn(0, 1)
            norm_sum(2)
            feature_major("eqk", 8, acts(xh, xl), "eqk_ready", "eqk_read", [("d0_read", 10)],
                          ("xl_ready", KT * 2))
            token_major("ev", 4, acts(xh, xl), "ev_ready", "ev_read", [("eqk_read", 20)])
            pe.wait_ge(sem("ev_read"), 12)
            attend(("moba", 4, 0), ("diff", 4, 8))
            turn(0, [("y_token", 1)])
            feature_major("eout", 4, acts(xh, xl), "eo_ready", "eo_read", [], ("turn_read", 0))
            ffn(1, 3)
            norm_sum(4)
            feature_major("oqk", 6, acts(xh, xl), "oqk_ready", "oqk_read", [("d1_read", 10)],
                          ("xl_ready", KT * 4))
            token_major("ov", 2, acts(xh, xl), "ov_ready", "ov_read", [("oqk_read", 16)])
            pe.wait_ge(sem("ov_read"), 8)
            attend(("dil", 4, 16),)
            pe.wait_ge(sem("y_read"), 26)
            for t in range(3):
                pe.wait_ge(sem("c_square"), t + 1)
                pe.matmul(bank[6 + t // 2][:, :], ones, tile(tmpb, t % 2), start=t != 1,
                          stop=t != 0).then_inc(sem("c_sum"), 1)
            pe.wait_ge(sem("cl_ready"), 3)
            chunk(0, BASE["mla"])
            for j in range(6):
                if j >= 4:
                    pe.wait_ge(sem("mla_read"), j - 3)
                products(bank[j % 4][:, :], weights(0, j, 2, 6 * P), acts(ch, cl, 0, 2)).then_inc(sem("mla_ready"), 1)
            chunk(0, BASE["mla"] + 1)
            for j in range(4):
                pe.wait_ge(sem("mla_read"), j + 3)
                products(bank[(6 + j) % 4][:, :], weights(1, j, 1), acts(ch, cl, 2, 1)).then_inc(sem("mla_ready"), 1)
            for b in range(NB):
                pe.wait_ge(sem("mla_read"), b + 7)
                products(bank[(10 + b) % 4][:, :], [(ch[:, 2, b * P:(b + 1) * P], cl[:, 2, b * P:(b + 1) * P])],
                         [(wh[:, 1, 4 * P:8 * P], wl[:, 1, 4 * P:8 * P])]).then_inc(sem("mla_ready"), 1)
            pe.wait_ge(sem("mla_read"), 14)
            for n, t in enumerate((12, 13, 11)):
                pe.matmul(bank[4 + n][:, :], small_rot, tile(qk, t), start=True, stop=True)\
                  .then_inc(sem("rotated"), 1)
            pe.wait_ge(sem("roped"), 3)
            attend(("mla", 2, 24),)
            turn(1, [("y_token", 2)])
            feature_major("oout", 4, acts(xh, xl), "oo_ready", "oo_read", [], ("turn_read", KT))
            ffn(2, 5)
            norm_sum(6)

        @block.gpsimd
        def _(pool):
            def low(i, n, c):
                pool.wait_ge(high_ready, i + (n + 1))
                pool.tensor_tensor(wl[:, c, :], raw[:, c, :], wh[:, c, :].bitcast(F32),
                                   ALU.subtract).then_inc(low_ready, 1)

            def stage(name, count):
                n0 = BASE[name] + 2
                rounds = count // 2 - (1 if n0 + count > CHUNKS else 0)
                for i in repeat(pool, rounds):
                    for c in range(2):
                        low(i * 2, n0 + c, c)

            def attend(*kinds):
                if kinds[0][0] != "mla":
                    first = kinds[0][0] == "moba"
                    pool.wait_ge(low_ready, BASE["eout" if first else "mla"] + 2)
                    pool.wait_ge(sem("d0_read" if first else "d1_read"), 10)
                    for u in range(2):
                        pool.memset(qs[64 - 64 * u:P - 64 * u, u, :], 0.0).then_inc(sem("qs_zero"), 1)
                        pool.wait_ge(sem("qs_zero"), (1 if first else 3) + u)
                for kind, pairs, u0 in kinds:
                    for i in (range(2) if kind == "mla" else repeat(pool, pairs)):
                        for u in range(2):
                            pool.wait_ge(sem("s_ready"), i * 8 + (4 * (u0 + u) + 4))
                            if kind == "mla":
                                if u == 0:
                                    pool.tensor_copy(tmpa[:, i, :], qk[:, i + 12, :])
                                pool.tensor_copy(qs[:, u, :], qk[:, i * 2 + u, :]).then_inc(sem("q_staged"), 1)
                            else:
                                first = {"moba": 0, "diff": 8, "dil": 0}[kind]
                                half = slice(64 * u, 64 * u + 64)
                                pool.tensor_copy(qs[half, u:u + 1, :], qk[half, bass.ds(i + first, 1), :])\
                                    .then_inc(sem("q_staged"), 1)
                            pool.wait_ge(sem("q_staged"), i * 2 + (u0 + u + 1))
                            pool.wait_ge(sem("s_read"), i * 8 + (4 * (u0 + u) + 4))
                            row = {"moba": i * 2 + u, "diff": i + 8, "dil": i * 2 + (12 + u), "mla": MASK_ROW}[kind]
                            pool.sem_inc(sem("bias_begun"), 1)
                            one = table[cut(row, 1), 0:S]
                            src = bass.AP(tensor=one.tensor, offset=one.offset, ap=[[1, P], [1, S]])
                            pool.dma_start(bt[:, u, :], src).then_inc(sem(f"bias_landed_{u}"), 16)

            for n in range(2):
                low(0, n, n)
            stage("qk", 8)
            pool.wait_ge(table_ready, 1)
            pool.dma_start(table[:, :], tt[:, :]).then_inc(table_stored, 16)
            pool.wait_ge(table_stored, 16)
            stage("v", 4)
            pool.wait_ge(sem("qk_normed"), 16)
            pool.wait_ge(sem("v_read"), 12)

            def stage_keys(i, h):
                if h:
                    pool.wait_ge(sem("z_ready"), i * 3 + 3 * h)
                pool.tensor_copy(ks[:, :], tile(qk, i + (h + 8))).then_inc(sem("k_staged"), 1)

            def stage_values(i, h):
                if h:
                    pool.wait_ge(sem("sy_ready"), i + h)
                pool.tensor_copy(vs[:, :, :], vt[:, :, cut(i * P + h * P, P)]).then_inc(sem("v_staged"), 1)

            stage_keys(0, 0)
            stage_values(0, 0)
            stage_keys(0, 1)
            for i in repeat(pool, 6):
                stage_keys(i, 2)
                stage_values(i, 1)
            stage_values(0, 7)
            pool.wait_ge(sem("sy_read"), 10)
            pool.dma_start(rgw[:, :, :], rg_in).then_inc(sem("rg_landed"), 16)
            stage("gate2", 8)
            for name in ("pool", "wpool", "gate0", "lru", "gate1", "out", "ffn0"):
                stage(name, COUNT[name])
            stage("down0", 16)
            stage("eqk", 8)
            stage("ev", 4)
            attend(("moba", 4, 0), ("diff", 4, 8))
            stage("eout", 4)
            stage("ffn1", FT)
            stage("down1", 16)
            pool.wait_ge(sem("d1_read"), 10)
            pool.dma_start(rope[:, :, :], rope_in).then_inc(sem("rope_landed"), 16)
            stage("oqk", 6)
            stage("ov", 2)
            attend(("dil", 4, 16),)
            stage("mla", 2)
            pool.wait_ge(sem("roped"), 3)
            attend(("mla", 2, 24),)
            stage("oout", 4)
            stage("ffn2", FT)
            stage("down2", 16)

        @block.scalar
        def _(act):
            step = Steps(act, sem("act_step"))

            def refill(c, n, i=0):
                if type(i) is not int:
                    act.wait_ge(raw_landed[c], i * 8 + 16 * (n // 2 + 1))
                else:
                    act.wait_ge(raw_landed[c], 16 * ((i + n) // 2 + 1))
                act.activation(wh[:, c, :], raw[:, c, :], ACT.Copy).then_inc(high_ready, 1)

            def norm(v):
                act.preload_act_table(ACT.Sqrt)
                act.wait_ge(sem("var_ready"), v + 1)
                act.activation(token_rstd, token_rstd, ACT.Sqrt).then_inc(sem("std_ready"), 1)
                if v < 6:
                    for t in range(KT):
                        act.wait_ge(sem("nx_ready"), KT * v + t + 1)
                        act.activation(xh[:, t, :], tmpa[:, t % 2, :], ACT.Copy).then_inc(sem("xh_ready"), 1)

            def copies(name, chunks, ready, read, scale, squares=False):
                n0 = BASE[name] + 2
                for i in repeat(act, chunks // 2):
                    for c in range(2):
                        for j in range(2):
                            act.wait_ge(sem(ready), i * 4 + (2 * c + j + 1))
                            if squares:
                                act.activation(tile(sq, i * 4 + (2 * c + j)), bank[2 * c + j][:, :], ACT.Square)
                            act.activation(tile(qk, i * 4 + (2 * c + j)), bank[2 * c + j][:, :], ACT.Copy,
                                           scale=col(scale, i * 4 + (2 * c + j))).then_inc(sem(read), 1)
                        refill(c, n0 + c, i * 2)

            def value_copies(name, chunks, ready, read):
                n0 = BASE[name] + 2
                for i in repeat(act, chunks // 2):
                    for c in range(2):
                        for j in range(2):
                            act.wait_ge(sem(ready), i * 4 + (2 * c + j + 1))
                            act.activation(vt[:, 2 * j:2 * j + 2, cut(i * S + c * 2 * P, 2 * P)],
                                           bank[2 * c + j][:, :].rearrange("p (b n) -> p b n", b=2),
                                           ACT.Copy).then_inc(sem(read), 1)
                        refill(c, n0 + c, i * 2)

            def gates(b, name, ready, gate, prod):
                n0 = BASE[name] + 2
                for i in repeat(act, 4):
                    for j in range(2):
                        act.wait_ge(sem(ready), i * 4 + (j + 1))
                        act.wait_ge(sem(prod), i * 2 + (j + 1))
                        act.activation(tmpa[:, j, :], bank[j][:, :], ACT.Sigmoid,
                                       bias=col("b_gate", i * 2 + (8 * b + j))).then_inc(sem(gate), 1)
                    refill(0, n0, i * 2)
                    act.wait_ge(sem(ready), i * 4 + 4)
                    refill(1, n0 + 1, i * 2)

            def refills(name, chunks, ready, per, last=False):
                n0 = BASE[name] + 2
                for i in repeat(act, chunks // 2 - last):
                    for c in range(2):
                        act.wait_ge(sem(ready), i * (2 * per) + per * (c + 1))
                        refill(c, n0 + c, i * 2)

            def split(high, source, source_ready):
                for t in range(KT):
                    act.wait_ge(sem(source_ready[0]), source_ready[1] + t)
                    act.activation(yh[:, t, :], source[:, t, :], ACT.Copy).then_inc(sem(high), 1)

            def ffn(n, v):
                norm(v)
                name, ready, n0 = f"ffn{n}", f"f{n}_ready", BASE[f"ffn{n}"] + 2
                for i in repeat(act, FT // 2):
                    for j in range(2):
                        act.wait_ge(sem(ready), i * 4 + (j + 1))
                        if n == 0:
                            act.activation(tmpa[:, j, :], bank[j][:, :], ACT.Silu).then_inc(sem("f0_gate"), 1)
                        else:
                            k = (n - 1) * FT
                            act.activation(tmpa[:, j, :], bank[j][:, :], ACT.Identity,
                                           bias=col("ffn_b", i * 2 + (k + j)),
                                           scale=col("ffn_w", i * 2 + (3 * k + 2 * FT + j)))\
                               .then_inc(sem(f"f{n}_conv0"), 1)
                    refill(0, n0, i * 2)
                    if n:
                        for j in range(2):
                            act.wait_ge(sem(f"f{n}_gate"), i * 2 + (j + 3))
                            act.activation(tmpa[:, j, :], tmpa[:, j, :], ACT.Gelu).then_inc(sem(f"f{n}_gelu"), 1)
                    for j in range(2):
                        act.wait_ge(sem(f"f{n}_prod"), i * 2 + (j + 3))
                        act.activation(tile(ah, i * 2 + j), tmpb[:, j, :], ACT.Copy).then_inc(sem(f"f{n}_high"), 1)
                    refill(1, n0 + 1, i * 2)
                refills(f"down{n}", 16, f"d{n}_ready", 1, last=n == 2)

            def attend(*kinds):
                def exponent(unit, b):
                    _, u0, i, u = unit
                    n = (b + 1) * P
                    act.wait_ge(sem("s_read"), i * 8 + (4 * (u0 + u) + b + 9))
                    act.activation(tq[:, b, 0:n], tq[:, b, 0:n], ACT.Exp, bias=nm[:, u, b:b + 1], scale=-1.0,
                                   accum_out=rs[:, u, b:b + 1]).then_inc(sem("p_ready"), 1)

                def copy_even(unit, b):
                    _, u0, i, u = unit
                    q = 4 * (u0 + u) + b
                    act.wait_ge(sem("t_ready"), i * 8 + (q + 5))
                    act.wait_ge(sem("pv_done"), i * 8 + (q + 1))
                    act.activation(pts[:, 0, 0:(b + 1) * P], bank[4][:, 0:(b + 1) * P], ACT.Copy)\
                       .then_inc(sem("pt_even"), 1)

                def body(unit, following):
                    for b in (0, 2):
                        copy_even(unit, b)
                        if following:
                            exponent(following, b)
                            exponent(following, b + 1)

                for b in range(NB):
                    exponent((kinds[0][0], kinds[0][2], 0, 0), b)
                in_pairs(act, kinds, body)

            def turn(v):
                for t in range(KT):
                    act.wait_ge(sem("turned"), KT * v + t + 1)
                    act.activation(xh[:, t, :], bank[4 + t % 2][:, :], ACT.Copy,
                                   scale=col("one_scale" if v else "subln", t)).then_inc(sem("turn_high"), 1)

            act.wait_ge(raw_landed[0], 16)
            act.activation(wh[:, 0, :], raw[:, 0, :], ACT.Copy).then_inc(high_ready, 1)
            act.wait_ge(raw_landed[1], 16)
            act.activation(wh[:, 1, :], raw[:, 1, :], ACT.Copy).then_inc(high_ready, 1)
            act.wait_ge(x_landed, 3 * 16)
            for t in range(KT):
                act.activation(qk[:, t, :], xT[:, t, :], ACT.Square).then_inc(sem("x_square"), 1)
            norm(0)
            copies("qk", 8, "qk_ready", "qk_read", "one_scale", squares=True)
            act.wait_ge(sem("qk_var"), 1)
            act.activation(rstd[0:16, :], rstd[0:16, :], ACT.Sqrt).then_inc(sem("qk_std"), 1)
            act.wait_ge(sem("lambda_sums"), 2)
            act.activation(t1, col("lru_lambda", 0, 8), ACT.Abs).then_inc(sem("lambda_abs"), 1)
            act.wait_ge(sem("lambda_abs"), 1)
            act.activation(t1, t1, ACT.Exp, scale=-1.0).then_inc(sem("lambda_exp"), 1)
            act.activation(lam2, lam2, ACT.Exp).then_inc(sem("lambda_exp"), 1)
            act.wait_ge(table_stored, 16)
            value_copies("v", 4, "v_ready", "v_read")

            def softplus(i, h):
                c, at = h % 2, i * 6 + 6 * h
                tiles = [(sp[:, c, j, 0:w], bank[3 * c + j][:, 0:w]) for j, w in enumerate((S, S, 2 * P))]
                for j, (w, z) in enumerate(tiles):
                    act.wait_ge(sem("z_ready"), i * 3 + (3 * h + j + 1))
                    act.activation(w, z, ACT.Abs).then_inc(sem("sp_chain"), 1)
                for j, (w, z) in enumerate(tiles):
                    act.wait_ge(sem("sp_chain"), at + (j + 1))
                    act.activation(w, w, ACT.Exp, scale=-1.0).then_inc(sem("sp_chain"), 1)
                for j, (w, z) in enumerate(tiles):
                    act.wait_ge(sem("sp_chain"), at + (j + 4))
                    act.activation(w, w, ACT.Ln, bias=1.0).then_inc(sem("ln_ready"), 1)

            def sb_weights(i, h):
                for j, w in enumerate((S, S, 2 * P)):
                    act.wait_ge(sem("z_done"), i * 3 + (3 * h + j + 1))
                    act.activation(wz[:, j, 0:w], bank[3 * (h % 2) + j][:, 0:w], ACT.Exp)\
                       .then_inc(sem("w_ready"), 1)

            def sb_output(i, h):
                act.wait_ge(sem("sy_ready"), i + (h + 1))
                act.activation(tile(qk, i + h), bank[6 + h % 2][:, :], ACT.Copy).then_inc(sem("sy_read"), 1)

            act.preload_act_table_set("natural_log_exp_and_others")
            softplus(0, 0)
            softplus(0, 1)
            sb_weights(0, 0)
            for i in repeat(act, 3):
                for h in (1, 2):
                    softplus(i * 2, h + 1)
                    sb_output(i * 2, h - 1)
                    sb_weights(i * 2, h)
            sb_output(0, 6)
            sb_weights(0, 7)
            sb_output(0, 7)
            act.wait_ge(sem("sy_read"), 10)
            for t in range(KT):
                act.activation(yh[:, t, :], qk[:, t, :], ACT.Copy).then_inc(sem("yh0_ready"), 1)
            gates(2, "gate2", "g2_ready", "g2_gate", "g2_prod")
            for t in range(KT + 1):
                if t < KT:
                    act.wait_ge(sem("pool_ready"), t + 1)
                    if t >= 2:
                        act.wait_ge(sem("p_low"), t - 1)
                    else:
                        act.wait_ge(sem("pads_ready"), 4)
                    act.activation(pu[:, t % 2, 16:16 + S], bank[t % 4][:, :], ACT.Copy).then_inc(sem("pool_read"), 1)
                if t:
                    act.wait_ge(sem("p_ready_value"), t)
                    act.activation(yh[:, t - 1, :], tmpb[:, (t - 1) % 2, :], ACT.Copy).then_inc(sem("p_high"), 1)
                if t < KT and t % 2:
                    refill(t // 2 % 2, BASE["pool"] + t // 2 + 2)
            for c in range(2):
                for g in range(2):
                    for j in range(2):
                        f = 4 * c + 2 * g
                        act.wait_ge(sem("wpool_ready"), f + 2)
                        act.activation(yh[:, f + j, :], bank[2 * g + j][:, :], ACT.Copy,
                                       scale=col("pool_scale", f + j)).then_inc(sem("wpool_high"), 1)
                refill(c, BASE["wpool"] + c + 2)
            gates(0, "gate0", "g0_ready", "g0_gate", "g0_prod")
            for t in range(KT + 1):
                if t < KT:
                    act.wait_ge(sem("lru_ready"), t + 1)
                    if t >= 2:
                        act.wait_ge(sem("lru_low"), t - 1)
                    act.activation(xc[:, t % 2, :], bank[t % 4][:, :], ACT.Identity, bias=col("conv_b", t),
                                   scale=col("conv_w", 24 + t)).then_inc(sem("lru_base"), 1)
                    if t % 2:
                        refill(t // 2 % 2, BASE["lru"] + t // 2 + 2)
                if t:
                    u, c = t - 1, (t - 1) % 2
                    act.wait_ge(sem("lru_gate"), u + 1)
                    act.activation(rr[:, c, :], bank[4 + 2 * c][:, :], ACT.Sigmoid, bias=col("b_rg", u))\
                       .then_inc(sem("lru_sigmoid"), 1)
                    act.activation(ii[:, c, :], bank[5 + 2 * c][:, :], ACT.Sigmoid, bias=col("b_ig", u))\
                       .then_inc(sem("lru_sigmoid"), 1)
                    act.wait_ge(sem("lru_sigmoid"), 2 * u + 2)
                    act.activation(tmpb[:, c, :], rr[:, c, :], ACT.Tanh, scale=decay8[:, u:u + 1])\
                       .then_inc(sem("lru_tanh"), 1)
                    act.activation(aa[:, c, :], rr[:, c, :], ACT.Exp, scale=ndecay8[:, u:u + 1])\
                       .then_inc(sem("lru_a"), 1)
                    act.wait_ge(sem("lru_m2"), 2 * u + 2)
                    act.activation(tmpa[:, c, :], tmpa[:, c, :], ACT.Sqrt).then_inc(sem("lru_mult"), 1)
                    act.wait_ge(sem("lru_h"), 3 * u + 3)
                    act.activation(yh[:, u, :], xc[:, c, :], ACT.Copy).then_inc(sem("lru_high"), 1)
            gates(1, "gate1", "g1_ready", "g1_gate", "g1_prod")
            for t in range(KT):
                act.wait_ge(sem("merged_ready"), t + 1)
                act.wait_ge(sem("g1_ready"), 16)
                act.activation(yh[:, t, :], merged[:, t, :], ACT.Copy).then_inc(sem("yh1_ready"), 1)
            refills("out", 4, "out_ready", 2)
            ffn(0, 1)
            norm(2)
            copies("eqk", 8, "eqk_ready", "eqk_read", "even_scale")
            value_copies("ev", 4, "ev_ready", "ev_read")
            attend(("moba", 4, 0), ("diff", 4, 8))
            act.wait_ge(sem("diff_var"), 1)
            act.activation(dss, dss, ACT.Sqrt).then_inc(sem("diff_std"), 1)
            turn(0)
            refills("eout", 4, "eo_ready", 2)
            ffn(1, 3)
            norm(4)
            copies("oqk", 6, "oqk_ready", "oqk_read", "odd_scale")
            value_copies("ov", 2, "ov_ready", "ov_read")
            attend(("dil", 4, 16),)
            act.wait_ge(sem("oqk_read"), 16)
            for t in range(3):
                if t == 2:
                    act.wait_ge(sem("c_sum"), 1)
                act.activation(tmpb[:, t % 2, :], qk[:, 8 + t, :], ACT.Square).then_inc(sem("c_square"), 1)
            for t in range(2):
                act.wait_ge(sem("c_var"), t + 1)
                act.activation(tmpa[:, t, :], tmpa[:, t, :], ACT.Sqrt).then_inc(sem("c_std"), 1)
            for t in range(3):
                act.wait_ge(sem("c_normed"), t + 1)
                act.activation(ch[:, t, :], qk[:, 8 + t, :], ACT.Copy).then_inc(sem("ch_ready"), 1)
            for j in range(14):
                act.wait_ge(sem("mla_ready"), j + 1)
                if j < 6:
                    act.activation(qk[:, j if j < 4 else j + 8, :], bank[j % 4][:, :], ACT.Copy,
                                   scale=192 ** -0.5).then_inc(sem("mla_read"), 1)
                elif j < 10:
                    act.activation(qk[:, j - 2, :], bank[j % 4][:, :], ACT.Copy).then_inc(sem("mla_read"), 1)
                else:
                    act.activation(vt[:, j - 10, S:2 * S], bank[j % 4][:, :], ACT.Copy).then_inc(sem("mla_read"), 1)
                if j in (5, 13):
                    refill(j // 6 % 2 if j == 5 else 1, BASE["mla"] + 2 + (j == 13))
            attend(("mla", 2, 24),)
            turn(1)
            refills("oout", 4, "oo_ready", 2)
            ffn(2, 5)
            norm(6)

        @block.vector
        def _(dve):
            step = Steps(dve, sem("dve_step"))

            def norm(v, gain, g0):
                dve.wait_ge(sem("token_sums"), v + 1)
                dve.tensor_scalar(token_rstd, bank[7][:, 0:NB], 1.0 / D, EPS, ALU.mult, ALU.add)\
                   .then_inc(sem("var_ready"), 1)
                dve.wait_ge(sem("std_ready"), v + 1)
                step(dve.reciprocal(token_rstd, token_rstd))
                dve.tensor_tensor(rstd[:, :].rearrange("p (b n) -> p b n", b=NB),
                                  ident.unsqueeze(1).to_broadcast([P, NB, P]),
                                  token_rstd.unsqueeze(2).to_broadcast([P, NB, P]), ALU.mult)\
                   .then_inc(sem("diagonals_ready"), 1)
                dve.wait_ge(sem("rstd_ready"), v + 1)
                for t in range(KT + 1):
                    if t < KT:
                        target = qk[:, t, :] if v == 6 else tmpa[:, t % 2, :]
                        if t >= 2 and v < 6:
                            dve.wait_ge(sem("xl_ready"), KT * v + t - 1)
                        dve.scalar_tensor_tensor(target, xT[:, t, :], col(gain, g0 + t), bank[7][:, :], ALU.mult,
                                                 ALU.mult).then_inc(sem("final_ready" if v == 6 else "nx_ready"), 1)
                    if t and v < 6:
                        dve.wait_ge(sem("xh_ready"), KT * v + t)
                        dve.tensor_tensor(xl[:, t - 1, :], tmpa[:, (t - 1) % 2, :], xh[:, t - 1, :].bitcast(F32),
                                          ALU.subtract).then_inc(sem("xl_ready"), 1)

            def products(name, first, ready, gate, prod):
                for i in repeat(dve, 4, step, 0 if first else 2):
                    for j in range(2):
                        dve.wait_ge(sem(gate), i * 2 + (j + 3))
                        dve.wait_ge(sem(ready), i * 4 + (j + 3))
                        if first:
                            dve.tensor_tensor(tile(merged, i * 2 + j), bank[2 + j][:, :], tmpa[:, j, :], ALU.mult)\
                               .then_inc(sem(prod), 1)
                        else:
                            dve.tensor_tensor(tmpb[:, j, :], bank[2 + j][:, :], tmpa[:, j, :], ALU.mult)\
                               .then_inc(sem(prod), 1)
                            dve.wait_ge(sem(prod), i * 2 + (j + 3))
                            step(dve.tensor_tensor(tile(merged, i * 2 + j), tile(merged, i * 2 + j), tmpb[:, j, :],
                                                   ALU.add))

            def residual(chunks, ready, read, per):
                rounds, tiles = (chunks // 2, 4) if per == 1 else (4, 2)
                step(dve.memset(tmpb[:, 0, :], 0.0))
                for i in repeat(dve, rounds, step, 2 * tiles):
                    for j in range(tiles):
                        dve.wait_ge(sem(ready), i * (tiles * per) + per * (j + 1))
                        t = i * tiles + j
                        dve.tensor_tensor(tile(xT, t), tile(xT, t), bank[j][:, :], ALU.add).then_inc(sem(read), 1)
                        dve.wait_ge(sem(read), i * tiles + (j + 1 + (4 if per == 1 else 2)))
                        step(dve.tensor_tensor(tmpb[:, 1, :], tile(xT, t), tile(xT, t), ALU.mult))
                        step(dve.tensor_tensor(tmpb[:, 0, :], tmpb[:, 0, :], tmpb[:, 1, :], ALU.add))
                dve.sem_inc(sem("squares_ready"), 1)

            def ffn(n, v, gain, g0):
                norm(v, gain, g0)
                for i in repeat(dve, FT // 2, step, 2 if n else 0):
                    if n:
                        for j in range(2):
                            k = 3 * (n - 1) * FT
                            dve.wait_ge(sem(f"f{n}_conv0"), i * 2 + (j + 1))
                            a = tmpa[:, j, :]
                            step(dve.scalar_tensor_tensor(a[:, 1:S], bank[j][:, 0:S - 1],
                                                          col("ffn_w", i * 2 + (k + FT + j)), a[:, 1:S],
                                                          ALU.mult, ALU.add))
                            dve.scalar_tensor_tensor(a[:, 2:S], bank[j][:, 0:S - 2], col("ffn_w", i * 2 + (k + j)),
                                                     a[:, 2:S], ALU.mult, ALU.add).then_inc(sem(f"f{n}_gate"), 1)
                    for j in range(2):
                        dve.wait_ge(sem(f"f{n}_ready"), i * 4 + (j + 3))
                        dve.wait_ge(sem(f"f{n}_gelu" if n else "f0_gate"), i * 2 + (j + (1 if n else 3)))
                        dve.tensor_tensor(tmpb[:, j, :], tmpa[:, j, :], bank[2 + j][:, :], ALU.mult)\
                           .then_inc(sem(f"f{n}_prod"), 1)
                    for j in range(2):
                        dve.wait_ge(sem(f"f{n}_high"), i * 2 + (j + 1))
                        dve.tensor_tensor(tile(al, i * 2 + j), tmpb[:, j, :], tile(ah, i * 2 + j).bitcast(F32),
                                          ALU.subtract).then_inc(sem(f"f{n}_low"), 1)
                    dve.wait_ge(sem(f"f{n}_low"), i * 2 + 2)
                residual(16, f"d{n}_ready", f"d{n}_read", 2)

            def attend(*kinds):
                def shifted(unit, b):
                    _, u0, i, u = unit
                    q = 4 * (u0 + u) + b
                    n = (b + 1) * P
                    dve.wait_ge(sem(f"bias_landed_{u}"), i * 16 + 16 * (u0 // 2 + 1))
                    dve.wait_ge(sem("s_ready"), i * 8 + (q + 9))
                    dve.wait_ge(sem("t_ready"), i * 8 + (q + 1))
                    dve.sem_inc(sem("shift_begun"), 1)
                    dve.tensor_tensor_reduce(tq[:, b, 0:n], bank[b][:, 0:n], bt[:, u, 0:n][:, ::-1], -1.0,
                                             3.0e38, ALU.add, ALU.min, nm[:, u, b:b + 1])\
                       .then_inc(sem("s_read"), 1)

                def copy_odd(unit, b):
                    _, u0, i, u = unit
                    q = 4 * (u0 + u) + b
                    dve.wait_ge(sem("t_ready"), i * 8 + (q + 5))
                    dve.wait_ge(sem("pv_done"), i * 8 + (q + 1))
                    dve.tensor_copy(pts[:, 1, 0:(b + 1) * P], bank[5][:, 0:(b + 1) * P])\
                       .then_inc(sem("pt_odd"), 1)

                def normalised(unit):
                    kind, u0, i, u = unit
                    dve.wait_ge(sem("pv_done"), i * 8 + (4 * (u0 + u) + 6))
                    step(dve.reciprocal(rd[:, u, :], rs[:, u, :]))
                    if kind != "diff":
                        dh, c = (P, i * (2 * P) + (4 + u) * P) if kind == "mla" else (64, i * P + 64 * u)
                        dve.tensor_tensor(yt[:, :, cut(c, dh)],
                                          bank[6 + u][:, 0:NB * dh].rearrange("p (b n) -> p b n", b=NB),
                                          rd[:, u, :].unsqueeze(2).to_broadcast([P, NB, dh]), ALU.mult)\
                           .then_inc(sem("y_read"), 1)
                    elif u == 1:
                        step(dve.tensor_scalar(rd[:, 1, :], rd[:, 1, :], nlam, None, ALU.mult))
                        for k in range(2):
                            dve.tensor_tensor((tmpa, tmpb)[k][:, 0, :].rearrange("p (b n) -> p b n", b=NB),
                                              bank[6 + k][:, :].rearrange("p (b n) -> p b n", b=NB),
                                              rd[:, k, :].unsqueeze(2).to_broadcast([P, NB, P]), ALU.mult)\
                               .then_inc(sem("y_read"), 1)
                        dve.wait_ge(sem("y_read"), i * 2 + (u0 + 4))
                        step(dve.tensor_tensor(yt[:, :, cut(i * P + 4 * P, P)],
                                               tmpa[:, 0, :].rearrange("p (b n) -> p b n", b=NB),
                                               tmpb[:, 0, :].rearrange("p (b n) -> p b n", b=NB), ALU.add))

                def body(unit, following):
                    if following:
                        shifted(following, 0)
                    copy_odd(unit, 1)
                    if following:
                        shifted(following, 1)
                        shifted(following, 2)
                    copy_odd(unit, 3)
                    if following:
                        shifted(following, 3)
                    normalised(unit)

                for b in range(NB):
                    shifted((kinds[0][0], kinds[0][2], 0, 0), b)
                in_pairs(dve, kinds, body, step, [4 if kind == "diff" else 2 for kind, _, _ in kinds])

            def turn(v):
                for t in range(KT):
                    dve.wait_ge(sem("turn_high"), KT * v + t + 1)
                    dve.scalar_tensor_tensor(xl[:, t, :], bank[4 + t % 2][:, :], col("one_scale" if v else "subln", t),
                                             xh[:, t, :].bitcast(F32), ALU.mult, ALU.subtract)\
                       .then_inc(sem("turn_read"), 1)

            for t in range(1, KT):
                dve.wait_ge(sem("x_square"), t + 1)
                step(dve.tensor_tensor(tmpb[:, 0, :], tmpb[:, 0, :] if t > 1 else qk[:, 0, :], qk[:, t, :], ALU.add))
            dve.sem_inc(sem("squares_ready"), 1)
            norm(0, "norm_mix", 0)
            dve.wait_ge(sem("table_mm"), 1)
            for j in range(2):
                c = slice(j * TW // 2, (j + 1) * TW // 2)
                dve.tensor_tensor(tt[:, c], bank[5 + j][0:ROWS, 0:TW // 2], ad[:, c], ALU.add)\
                   .then_inc(sem("table_read"), 1)
            dve.wait_ge(sem("table_read"), 2)
            dve.sem_inc(table_ready, 1)
            dve.wait_ge(sem("qk_sum"), 1)
            dve.tensor_scalar(rstd[0:16, :], bank[4][0:16, :], 1.0 / P, EPS, ALU.mult, ALU.add)\
               .then_inc(sem("qk_var"), 1)
            dve.wait_ge(sem("qk_std"), 1)
            dve.reciprocal(rstd[0:16, :], rstd[0:16, :]).then_inc(sem("qk_rstd"), 1)
            lam_col = col("lru_lambda", 0, 8)
            for k in range(2):
                step(dve.tensor_tensor(tmpa[:, 0, 0:64], lamb[:, 2 * k, :], lamb[:, 2 * k + 1, :], ALU.mult))
                dve.tensor_reduce(lam2[:, k:k + 1], tmpa[:, 0, 0:64], AX.X, ALU.add).then_inc(sem("lambda_sums"), 1)
                dve.wait_ge(sem("lambda_sums"), k + 1)
            step(dve.tensor_scalar(col("qk_norm", 0, 8), col("qk_norm", 0, 8), 128 ** -0.5, None, ALU.mult))
            step(dve.tensor_tensor(col("subln", 0, 8), col("subln", 0, 8), col("subln_factor", 0, 8), ALU.mult))
            dve.wait_ge(sem("lambda_exp"), 2)
            step(dve.tensor_scalar(t2, t1, 2.0, None, ALU.add))
            step(dve.reciprocal(t2, t2))
            step(dve.tensor_tensor(t1, t1, t2, ALU.mult))
            step(dve.tensor_tensor(t2, t1, t1, ALU.mult))
            step(dve.tensor_scalar(t3, t2, 1.0 / 15, None, ALU.mult))
            for k in (13, 11, 9, 7, 5, 3):
                step(dve.scalar_tensor_tensor(t3, t3, 1.0 / k, t2, ALU.add, ALU.mult))
            step(dve.scalar_tensor_tensor(t3, t3, 1.0, t1, ALU.add, ALU.mult))
            step(dve.tensor_scalar(t4, lam_col, -1.0, 0.0, ALU.mult, ALU.max))
            step(dve.scalar_tensor_tensor(t3, t3, 2.0, t4, ALU.mult, ALU.add))
            step(dve.tensor_scalar(decay8, t3, 8.0, None, ALU.mult))
            step(dve.tensor_scalar(ndecay8, t3, -8.0, None, ALU.mult))
            step(dve.tensor_tensor(nlam, lam2[:, 1:2], lam2[:, 0:1], ALU.subtract))
            step(dve.tensor_scalar(nlam, nlam, -LAM_INIT, None, ALU.add))
            for t in range(16):
                dve.wait_ge(sem("qk_spread"), t + 1)
                dve.scalar_tensor_tensor(qk[:, t, :], qk[:, t, :], col("qk_norm", t), bank[t % 4][:, :], ALU.mult,
                                         ALU.mult).then_inc(sem("qk_normed"), 1)
            for i in repeat(dve, 4, step, 2):
                for c in range(2):
                    for j, w in enumerate((S, S, 2 * P)):
                        dve.wait_ge(sem("ln_ready"), i * 6 + (3 * c + j + 1))
                        last = dve.scalar_tensor_tensor(sp[:, c, j, 0:w], bank[3 * c + j][:, 0:w], 0.0,
                                                        sp[:, c, j, 0:w], ALU.max, ALU.add)
                    step(last)
                    for d in (sp[:, c, :, 0:P], sp[:, c, 1:2, 3 * P:S]):
                        dve.tensor_tensor(d, d, mask01.unsqueeze(1).to_broadcast([P, d.shape[1], P]), ALU.mult)\
                           .then_inc(sem("sp_ready"), 1)
            for t in range(KT):
                dve.wait_ge(sem("yh0_ready"), t + 1)
                dve.tensor_tensor(yl[:, t, :], qk[:, t, :], yh[:, t, :].bitcast(F32), ALU.subtract)\
                   .then_inc(sem("yl0_ready"), 1)
            products("gate2", True, "g2_ready", "g2_gate", "g2_prod")
            for b in range(2):
                for t in (pu, pa):
                    dve.memset(t[:, b, 0:16], 0.0).then_inc(sem("pads_ready"), 1)
            dve.wait_ge(sem("pads_ready"), 4)
            for t in range(KT):
                g, b = t // 2, t % 2
                w = WINDOWS[g]
                dve.wait_ge(sem("pool_read"), t + 5)
                src, dst, shift = pu[:, b, :], pa[:, 0, :], 1
                for n in range(g + 1):
                    step(dve.tensor_tensor(dst[:, 16:16 + S], src[:, 16:16 + S], src[:, 16 - shift:16 + S - shift],
                                           ALU.add))
                    src, dst, shift = dst, pa[:, 1 - n % 2, :], shift * 2
                step(dve.tensor_tensor(src[:, 16:32], src[:, 16:32], col("edge", 16 * g, 16), ALU.mult))
                dve.scalar_tensor_tensor(tmpb[:, b, :], src[:, 16:16 + S], 1.0 / w, pu[:, b, 16:16 + S], ALU.mult,
                                         ALU.subtract).then_inc(sem("p_ready_value"), 1)
                dve.wait_ge(sem("p_high"), t + 1)
                dve.tensor_tensor(yl[:, t, :], tmpb[:, b, :], yh[:, t, :].bitcast(F32), ALU.subtract)\
                   .then_inc(sem("p_low"), 1)
            for t in range(KT):
                dve.wait_ge(sem("wpool_high"), t + 1)
                dve.scalar_tensor_tensor(yl[:, t, :], bank[t % 4][:, :], col("pool_scale", t),
                                         yh[:, t, :].bitcast(F32), ALU.mult, ALU.subtract)\
                   .then_inc(sem("wpool_low"), 1)
            dve.wait_ge(sem("g2_prod"), 10)
            products("gate0", False, "g0_ready", "g0_gate", "g0_prod")
            for t in range(KT + 1):
                if t < KT:
                    x = xc[:, t % 2, :]
                    dve.wait_ge(sem("lru_base"), t + 1)
                    for k in (1, 2, 3):
                        dve.scalar_tensor_tensor(x[:, k:S], bank[t % 4][:, 0:S - k], col("conv_w", 8 * (3 - k) + t),
                                                 x[:, k:S], ALU.mult, ALU.add).then_inc(sem("lru_conv"), 1)
                        dve.wait_ge(sem("lru_conv"), 3 * t + k)
                if t:
                    u, c = t - 1, (t - 1) % 2
                    dve.wait_ge(sem("lru_a"), u + 1)
                    dve.tensor_tensor(tmpa[:, c, :], aa[:, c, :], aa[:, c, :], ALU.mult).then_inc(sem("lru_m2"), 1)
                    dve.wait_ge(sem("lru_m2"), 2 * u + 1)
                    dve.scalar_tensor_tensor(tmpa[:, c, :], tmpa[:, c, :], 1.0, tmpb[:, c, :], ALU.add, ALU.mult)\
                       .then_inc(sem("lru_m2"), 1)
                    i_ = ii[:, c, :]
                    dve.tensor_tensor(i_, i_, xc[:, c, :], ALU.mult).then_inc(sem("lru_h"), 1)
                    dve.wait_ge(sem("lru_mult"), u + 1)
                    dve.wait_ge(sem("lru_h"), 3 * u + 1)
                    dve.tensor_tensor(i_, i_, tmpa[:, c, :], ALU.mult).then_inc(sem("lru_h"), 1)
                    dve.wait_ge(sem("lru_h"), 3 * u + 2)
                    dve.tensor_tensor_scan(xc[:, c, :], aa[:, c, :], i_, 0.0, ALU.mult, ALU.add)\
                       .then_inc(sem("lru_h"), 1)
                    dve.wait_ge(sem("lru_high"), u + 1)
                    dve.tensor_tensor(yl[:, u, :], xc[:, c, :], yh[:, u, :].bitcast(F32), ALU.subtract)\
                       .then_inc(sem("lru_low"), 1)
            products("gate1", False, "g1_ready", "g1_gate", "g1_prod")
            for t in range(KT):
                dve.sem_inc(sem("merged_ready"), 1)
            for t in range(KT):
                dve.wait_ge(sem("yh1_ready"), t + 1)
                dve.tensor_tensor(yl[:, t, :], merged[:, t, :], yh[:, t, :].bitcast(F32), ALU.subtract)\
                   .then_inc(sem("yl1_ready"), 1)
            residual(4, "out_ready", "out_read", 1)
            ffn(0, 1, "norm_ffn", 0)
            norm(2, "even_norm", 0)
            attend(("moba", 4, 0), ("diff", 4, 8))
            for h in range(4):
                y = yt[:, :, (4 + h) * P:(5 + h) * P]
                w = tmpa[:, 0, :].rearrange("p (b n) -> p b n", b=NB)
                step(dve.tensor_tensor(w, y, y, ALU.mult))
                step(dve.tensor_reduce(dss[:, :, h:h + 1], w, AX.X, ALU.add))
            dve.tensor_scalar(dss, dss, 1.0 / P, EPS, ALU.mult, ALU.add).then_inc(sem("diff_var"), 1)
            dve.wait_ge(sem("diff_std"), 1)
            step(dve.reciprocal(dss, dss))
            for h in range(4):
                y = yt[:, :, (4 + h) * P:(5 + h) * P]
                last = dve.tensor_tensor(y, y, dss[:, :, h:h + 1].to_broadcast([P, NB, P]), ALU.mult)
            last.then_inc(sem("y_token"), 1)
            turn(0)
            residual(4, "eo_ready", "eo_read", 1)
            ffn(1, 3, "ffn_norm", 0)
            norm(4, "odd_norm", 0)
            attend(("dil", 4, 16),)
            dve.wait_ge(sem("c_sum"), 3)
            for t in range(2):
                dve.tensor_scalar(tmpa[:, t, :], bank[6 + t][:, :], 1.0 / (2 * P, P)[t], EPS, ALU.mult, ALU.add)\
                   .then_inc(sem("c_var"), 1)
            for t in range(2):
                dve.wait_ge(sem("c_std"), t + 1)
                step(dve.reciprocal(tmpa[:, t, :], tmpa[:, t, :]))
            for t in range(3):
                c = qk[:, 8 + t, :]
                gain = col("mla_q_norm", t) if t < 2 else col("mla_kv_norm", 0)
                dve.scalar_tensor_tensor(c, c, gain, tmpa[:, t // 2, :], ALU.mult, ALU.mult)\
                   .then_inc(sem("c_normed"), 1)
            for t in range(3):
                dve.wait_ge(sem("ch_ready"), t + 1)
                dve.tensor_tensor(cl[:, t, :], qk[:, 8 + t, :], ch[:, t, :].bitcast(F32), ALU.subtract)\
                   .then_inc(sem("cl_ready"), 1)
            dve.wait_ge(sem("rope_landed"), 16)
            for n, t in enumerate((12, 13, 11)):
                x = qk[:, t, :]
                dve.wait_ge(sem("rotated"), n + 1)
                step(dve.tensor_tensor(tmpb[:, 0, :], bank[4 + n][:, :], rope[:, 1, :], ALU.mult))
                step(dve.tensor_tensor(x, x, rope[:, 0, :], ALU.mult))
                dve.tensor_tensor(x, x, tmpb[:, 0, :], ALU.add).then_inc(sem("roped"), 1)
                dve.wait_ge(sem("roped"), n + 1)
            attend(("mla", 2, 24),)
            dve.drain().then_inc(sem("y_token"), 1)
            turn(1)
            residual(4, "oo_ready", "oo_read", 1)
            ffn(2, 5, "ffn_norm", 8)
            norm(6, "final", 0)


def _chunk(w):
    k = w.shape[0] // P
    out = np.zeros((P, CHUNK), w.dtype)
    out[:, 0:k * w.shape[1]] = w.reshape(k, P, w.shape[1]).transpose(1, 0, 2).reshape(P, -1)
    return out


def _chunks(w):
    return [_chunk(w[:, c:c + 2 * P]) for c in range(0, w.shape[1], 2 * P)]


def _pairs(a, b):
    return [c for pair in zip(_chunks(a), _chunks(b)) for c in pair]


def _downs(w):
    return [w[h * DOWN:(h + 1) * DOWN, t * P:(t + 1) * P].reshape(HALF, P, P).transpose(1, 0, 2).reshape(P, DOWN)
            for t in range(KT) for h in range(2)]


def _columns(v):
    return np.asarray(v).reshape(-1, P).T


def _bucket(distance):
    n = np.maximum(distance, 0)
    f = np.maximum(n, 1).astype(np.float32)
    large = 16 + (np.log(f / np.float32(16)) / np.float32(math.log(1024 / 16)) * np.float32(16)).astype(np.int32)
    return np.where(n < 16, n, np.minimum(large, 31))


def _constants():
    p = np.arange(P)
    upper = (p[None, :] > p[:, None]).astype(np.float32)
    rot = np.zeros((P, P), np.float32)
    for h in (0, 64):
        for j in range(32):
            rot[h + 32 + j, h + j] = -1.0
            rot[h + j, h + 32 + j] = 1.0
    mats = np.stack([np.ones((P, P)), np.eye(P), -(p[:, None] >= p[None, :]).astype(np.float32),
                     -np.ones((P, P)), np.where(upper > 0, 0.0, NEG), upper, rot, np.tile(p == 15, (P, 1))], axis=1).astype(np.float32)
    freq = (np.float32(10000.0) ** (-np.arange(32, dtype=np.float32) / np.float32(32))).astype(np.float32)
    angle = (np.arange(S, dtype=np.float32)[None, :] * freq[:, None]).astype(np.float32)
    rope = np.stack([np.tile(np.cos(angle), (4, 1)), np.tile(np.sin(angle), (4, 1))], axis=1).astype(np.float32)
    distance = np.arange(TW) - (P - 1)
    onehot = ((_bucket(distance)[None, :] == np.arange(32)[:, None]) & (distance >= 0)).astype(np.float32)
    causal = np.where(distance >= 0, 0.0, NEG)
    count = (distance <= 128).astype(int) + (distance % 4 == 0) + (distance % 16 == 0)
    dilated = np.where((distance >= 0) & (count > 0), np.log(np.maximum(count, 1)), NEG)
    add = np.stack([causal] * 12 + [dilated] * 8 + [causal]).astype(np.float32)
    edge = np.ones((P, 64), np.float32)
    for g, w in enumerate(WINDOWS):
        edge[:, 16 * g:16 * g + 16] = w / np.minimum(np.arange(1, 17), w)
    return mats, rope, onehot, add, edge


def _layout(x, norm_mix, w_in, b_gate, w_pool, pool_scale, conv_w, conv_b, w_rg, b_rg, w_ig, b_ig, lru_lambda,
            q_norm, k_norm, w_branch, w_out, norm_ffn, w_ffn_gate, w_ffn_up, w_ffn_down, rel_bias_2, even_norm1_2,
            even_w_in_2, diff_lambda_2, diff_subln_2, even_w_out_2, odd_norm1_2, odd_w_in_2, mla_q_norm_2,
            mla_w_uq_2, mla_kv_norm_2, mla_w_ukv_2, odd_w_out_2, ffn_norm_2, ffn_w_in_2, ffn_conv_w_2,
            ffn_conv_b_2, ffn_w_out_2, final_norm_2):
    wi, wb = w_in[0], w_branch[0]
    ev, od = even_w_in_2[0], odd_w_in_2[0]
    gate = [wi[:, 5 * D + b * D:5 * D + (b + 1) * D] for b in range(3)]
    ffn = lambda l: _pairs(ffn_w_in_2[l][:, FF:], ffn_w_in_2[l][:, :FF])
    uq = mla_w_uq_2[0].reshape(2 * P, 4, 192)
    uq = np.concatenate([uq[:, :, :P].reshape(2 * P, -1), uq[:, :, P:].reshape(2 * P, -1)], axis=1)
    ukv = mla_w_ukv_2[0].reshape(P, 4, 2 * P)
    ukv = np.concatenate([ukv[:, :, :P].reshape(P, -1), ukv[:, :, P:].reshape(P, -1)], axis=1)
    wp = w_pool[0].reshape(4, 2, P, 2 * P).transpose(2, 0, 1, 3).reshape(P, 2, CHUNK // 2)
    wpool = [np.concatenate([wp[:, c], np.zeros_like(wp[:, c])], axis=1) for c in range(2)]
    ckv = np.concatenate([od[:, 1792:1920], od[:, 1920:1984], od[:, 1920:1984]], axis=1)
    main = (_chunks(wi[:, 2 * D:4 * D]) + _chunks(wi[:, 4 * D:5 * D]) + _pairs(gate[2], wb[2])
            + _chunks(wi[:, 0:D]) + wpool + _pairs(gate[0], wb[0]) + _chunks(wi[:, D:2 * D]) + _pairs(gate[1], wb[1])
            + _chunks(w_out[0]) + _pairs(w_ffn_gate[0], w_ffn_up[0])
            + _chunks(ev[:, 0:1024]) + _chunks(ev[:, 1536:2560])
            + _chunks(ev[:, 1024:1536]) + _chunks(ev[:, 2560:3072]) + _chunks(even_w_out_2[0]) + ffn(0)
            + _chunks(od[:, 0:1024]) + _chunks(od[:, 1536:1792]) + _chunks(ckv) + _chunks(od[:, 1024:1536])
            + [_chunk(uq), _chunk(ukv)] + _chunks(odd_w_out_2[0]) + ffn(1))
    assert len(main) == MAIN, (len(main), MAIN)
    downs = _downs(w_ffn_down[0]) + _downs(ffn_w_out_2[0]) + _downs(ffn_w_out_2[1])
    mats, rope, onehot, add, edge = _constants()
    one = np.ones((P, 1), np.float32)
    eighth = 0.125 * one
    cols = [_columns(v) for v in (norm_mix, b_gate, pool_scale, conv_w, conv_b, b_rg, b_ig, lru_lambda)]
    cols += [_columns(q_norm)] * 8 + [_columns(k_norm)] * 8
    cols += [_columns(v) for v in (norm_ffn, even_norm1_2, odd_norm1_2, mla_q_norm_2, mla_kv_norm_2, ffn_norm_2,
                                   final_norm_2, ffn_conv_b_2, ffn_conv_w_2)]
    cols += [one] * 4 + [_columns(diff_subln_2)] * 4
    cols += [one] * 16 + ([eighth] * 4 + [one] * 4) * 2 + [eighth] * 4 + [one] * 8
    cols += [one] * 4 + [(1.0 - LAM_INIT) * one] * 4 + [edge]
    cols = np.ascontiguousarray(np.concatenate(cols, axis=1), dtype=np.float32)
    assert cols.shape == (P, NCOL), (cols.shape, NCOL)
    rg = np.zeros((P, 16, P), np.float32)
    for k, w in enumerate((w_rg[0], w_ig[0])):
        for t in range(KT):
            rg[0:64, 8 * k + t, 0:64] = w[2 * t]
            rg[64:P, 8 * k + t, 64:P] = w[2 * t + 1]
    rel = np.zeros((32, ROWS + 3), np.float32)
    rel[:, 0:20] = rel_bias_2
    return {
        "wmain": np.stack(main), "wdown": np.stack(downs),
        "x": np.ascontiguousarray(x[0].T.reshape(KT, P, S).transpose(1, 0, 2)),
        "cols": cols, "mats": np.ascontiguousarray(mats), "rg": rg, "rope": np.ascontiguousarray(rope),
        "onehot": onehot, "add": add, "rel": rel,
        "lam": np.ascontiguousarray(np.broadcast_to(diff_lambda_2[0][None], (P, 4, 64))),
    }


def kernel(**inputs):
    import concourse.bacc as bacc
    from concourse.bass_utils import run_bass_kernel_spmd

    arrays = _layout(**{k: np.asarray(v) for k, v in inputs.items()})
    nc = bacc.Bacc("TRN2", target_bir_lowering=False, num_devices=1)
    args = [nc.dram_tensor(n, a.shape, F32, kind="ExternalInput").ap() for n, a in arrays.items()]
    out = nc.dram_tensor("out", (P, KT, S), F32, kind="ExternalOutput").ap()
    table = nc.dram_tensor("distance_table", (ROWS, TW), F32, kind="Internal").ap()
    program(nc, *args, out, table)
    r = run_bass_kernel_spmd(nc, [arrays], core_ids=[0])
    y = r.results[0]["out"]
    return np.ascontiguousarray(y.transpose(1, 0, 2).reshape(D, S).T)[None]
```

```python
from contextlib import ExitStack
import math

import numpy as np

import concourse.bass as bass
from concourse import mybir

F32 = mybir.dt.float32
F32R = mybir.dt.float32r
ALU = mybir.AluOpType
ACT = mybir.ActivationFunctionType
AX = mybir.AxisListType

P = 128
S = 512
D = 1024
KT = D // P
NB = S // P
FF = 2816
FT = FF // P
HALF = FT // 2
EPS = 1e-6
CHUNK = KT * 2 * P
DOWN = HALF * P
NEG = -1e30
TW = 640
WINDOWS = (2, 4, 8, 16)
LAM_INIT = 0.8 - 0.6 * math.exp(-0.3 * 0)
MASK_ROW = 20
ROWS = 21

STAGES = [("qk", 8, 0), ("v", 4, 0), ("gate2", 8, 0), ("pool", 4, 0), ("wpool", 2, 0), ("gate0", 8, 0),
          ("lru", 4, 0), ("gate1", 8, 0), ("out", 4, 0), ("ffn0", FT, 0), ("down0", 16, 1),
          ("eqk", 8, 0), ("ev", 4, 0), ("eout", 4, 0), ("ffn1", FT, 0), ("down1", 16, 1),
          ("oqk", 6, 0), ("ov", 2, 0), ("mla", 2, 0), ("oout", 4, 0), ("ffn2", FT, 0), ("down2", 16, 1)]
BASE, WHERE, COUNT = {}, {}, {name: count for name, count, _ in STAGES}
_n, _in = 0, [0, 0]
for _name, _count, _kind in STAGES:
    BASE[_name], WHERE[_name] = _n, _in[_kind]
    _n, _in[_kind] = _n + _count, _in[_kind] + _count
CHUNKS = _n
MAIN, DOWNS = _in

COLS = {}
_at = 0
for _name, _k in [("norm_mix", 8), ("b_gate", 24), ("pool_scale", 8), ("conv_w", 32), ("conv_b", 8), ("b_rg", 8),
                  ("b_ig", 8), ("lru_lambda", 8), ("qk_norm", 16), ("norm_ffn", 8), ("even_norm", 8),
                  ("odd_norm", 8), ("mla_q_norm", 2), ("mla_kv_norm", 1), ("ffn_norm", 16), ("final", 8),
                  ("ffn_b", 2 * FT), ("ffn_w", 6 * FT), ("subln", 8), ("one_scale", 16), ("even_scale", 16),
                  ("odd_scale", 12), ("subln_factor", 8), ("edge", 64)]:
    COLS[_name] = _at
    _at += _k
NCOL = _at


def program(nc, wmain, wdown, xin, cols_in, mats_in, rg_in, rope_in, onehot_in, add_in, rel_in, lam_in, out, table):
    base = nc.sbuf_base + 31 & ~31
    top = [base]

    def place(name, shape, dt=F32, at=None):
        size = int(np.prod(shape[1:])) * 4
        if at is None:
            at = top[0]
            top[0] += size + 31 & ~31
        return nc.alloc_sbuf_tensor_at(name, shape, dt, offset=at)

    raw = place("raw", [P, 2, CHUNK])
    wh = place("w_high", [P, 2, CHUNK], F32R)
    wl = place("w_low", [P, 2, CHUNK], F32R)
    xT = place("x_residual", [P, KT, S])
    xh = place("x_high", [P, KT, S], F32R)
    xl = place("x_low", [P, KT, S], F32R)
    cols = place("columns", [P, NCOL])
    mats = place("matrices", [P, 8, P])
    ones, ident, negtri, negones, negmask, mask01, small_rot, pick = (mats[:, j, :] for j in range(8))
    rstd = place("rstd_diagonals", [P, S])
    tmpa = place("temp_a", [P, 2, S])
    tmpb = place("temp_b", [P, 2, S])
    small = place("small", [P, 128])
    arena = top[0]
    T = S * 4

    def over(name, shape, tile, dt=F32):
        return place(name, shape, dt, at=arena + int(tile * T))

    ah = over("act_high", [P, FT, S], 0, F32R)
    al = over("act_low", [P, FT, S], FT, F32R)
    qk = over("qk", [P, 16, S], 0)
    vt = over("v_tokens", [P, NB, D], 16)
    yh = over("y_high", [P, KT, S], 8, F32R)
    yl = over("y_low", [P, KT, S], 16, F32R)
    merged = over("merged", [P, KT, S], 24)
    sq = over("squares", [P, 16, S], 24)
    sp = over("softplus", [P, 2, 3, S], 32)
    wz = over("sb_weights", [P, 3, S], 38)
    ks = over("k_stage", [P, S], 41)
    vs = over("v_stage", [P, NB, P], 42)
    sph = over("softplus_high", [P, 2, 3, S], 24, F32R)
    spl = over("softplus_low", [P, 2, 3, S], 32, F32R)
    exact = over("matrices_r", [P, 4, P], 43, F32R)
    ident_r, negtri_r, negones_r, negmask_r = (exact[:, j, :] for j in range(4))
    qkrstd = over("qk_rstd_parts", [16, 2, S], 40, F32R)
    pu = over("pool_u", [P, 2, 16 + S], 32)
    pa = over("pool_a", [P, 2, 16 + S], 35)
    rgw = over("rg_blocks", [P, 16, P], 38)
    rr = over("r_gate_decay", [P, KT, S], 0)
    ii = over("i_gate", [P, KT, S], 8)
    xc = over("conv_out", [P, KT, S], 16)
    tanh = over("tanh", [P, 4, S], 32)
    yt = over("y_tokens", [P, NB, D], 24)
    tq = over("probs", [P, NB, S], 32)
    pts = over("probs_t", [P, 2, S], 36)
    qs = over("q_stage", [P, 2, S], 38)
    bt = over("bias", [P, 2, S], 40)
    rope = over("rope", [P, 2, S], 42)
    ytr = over("y_tokens_r", [P, NB, D], 24, F32R)
    qkr = over("qk_r", [P, 16, S], 0, F32R)
    ch = [ytr[:, t, S:D] for t in range(3)]
    cl = [ytr[:, 3, S:D], qkr[:, 14, :], qkr[:, 15, :]]
    oh = over("onehot", [32, TW], 16)
    ad = over("table_add", [ROWS, TW], 18)
    tt = over("table", [ROWS, TW], 20)
    rb = over("rel_bias", [32, ROWS + 3], 22)
    lamb = over("lambda_rows", [P, 4, 64], 23)
    assert arena + 44 * T <= nc.sbuf_usable_end, (arena + 44 * T, nc.sbuf_usable_end)

    SPAN = ((0, 0), (1, 0), (2, 0), (1, 3 * P))

    nm = small[:, 0:8].rearrange("p (u q) -> p u q", u=2)
    rs = small[:, 8:16].rearrange("p (u q) -> p u q", u=2)
    rd = small[:, 16:24].rearrange("p (u q) -> p u q", u=2)
    dss = small[:, 24:40].rearrange("p (q h) -> p q h", q=NB)
    nlam = small[:, 40:41]
    decay8 = small[:, 48:56]
    ndecay8 = small[:, 56:64]
    t1, t2, t3, t4 = (small[:, 64 + 8 * j:72 + 8 * j] for j in range(4))
    lam2 = small[:, 96:98]
    token_rstd = small[:, 98:102]

    with ExitStack() as ctx:
        names = {}

        def sem(name):
            if name not in names:
                names[name] = ctx.enter_context(nc.semaphore(name))
            return names[name]

        bank = [ctx.enter_context(nc.psum_tensor(f"bank{b}", [P, S], F32)) for b in range(8)]

        raw_landed = [sem("raw_landed_0"), sem("raw_landed_1")]
        high_ready, low_ready = sem("high_ready"), sem("low_ready")
        x_landed = [sem("x_landed_0"), sem("x_landed_1")]
        params_landed, inputs_landed = sem("params_landed"), sem("inputs_landed")
        table_ready, table_stored = sem("table_ready"), sem("table_stored")
        out_stored = sem("out_stored")

        class Steps:

            def __init__(self, eng, semaphore):
                self.eng, self.semaphore, self.n, self.here = eng, semaphore, 0, 0

            def __call__(self, instruction):
                self.here += 1
                self.n = self.n + 1
                instruction.then_inc(self.semaphore, 1)
                self.eng.wait_ge(self.semaphore, self.n)

        def repeat(eng, rounds, steps=None, per=0):
            if rounds == 1:
                yield 0
                return
            first = steps.n if steps else 0
            with eng.Fori(0, rounds) as i:
                if steps:
                    steps.n, steps.here = i * per + first, 0
                yield i
                assert not steps or steps.here == per, (steps.here, per)
            if steps:
                steps.n = first + rounds * per

        def col(name, k, n=1):
            if type(k) is int:
                return cols[:, COLS[name] + k:COLS[name] + k + n]
            return cols[:, bass.ds(k + COLS[name], n)]

        def tile(t, k, n=1):
            if type(k) is int:
                return t[:, k, :]
            return t[:, bass.ds(k, 1), :].rearrange("p a s -> p (a s)")

        def in_pairs(eng, kinds, body, steps=None, per=()):
            for n, (kind, pairs, u0) in enumerate(kinds):
                for i in repeat(eng, pairs - 1, steps, per[n] if per else 0):
                    body((kind, u0, i, 0), (kind, u0, i, 1))
                    body((kind, u0, i, 1), (kind, u0, i + 1, 0))
                last = pairs - 1
                after = kinds[n + 1] if n + 1 < len(kinds) else None
                body((kind, u0, last, 0), (kind, u0, last, 1))
                body((kind, u0, last, 1), after and (after[0], after[2], 0, 0))

        def cut(k, n):
            return slice(k, k + n) if type(k) is int else bass.ds(k, n)

        block = ctx.enter_context(nc.Block())

        @block.sync
        def _(sp_):
            def stream(name, count, down):
                source, width = (wdown, DOWN) if down else (wmain, CHUNK)
                n0, at = BASE[name], WHERE[name]

                def load(i, c):
                    if n0 + c >= 2:
                        sp_.wait_ge(low_ready, i * 2 + (n0 + c - 1))
                    src = source[cut(i * 2 + (at + c), 1), :, :].rearrange("a p n -> (a p) n")
                    sp_.dma_start(raw[:, c, 0:width], src).then_inc(raw_landed[c], 16)

                rounds = count // 2
                if n0 == 0:
                    load(0, 0)
                    sp_.dma_start(mats[:, :, :], mats_in).then_inc(params_landed, 16)
                    sp_.dma_start(cols[:, :], cols_in).then_inc(params_landed, 16)
                    load(0, 1)
                    sp_.dma_start(oh[:, :], onehot_in).then_inc(inputs_landed, 16)
                    sp_.dma_start(ad[:, :], add_in).then_inc(inputs_landed, 16)
                    sp_.dma_start(rb[:, :], rel_in).then_inc(inputs_landed, 16)
                    sp_.dma_start(lamb[:, :, :], lam_in).then_inc(inputs_landed, 16)
                    n0, at, rounds = 2, at + 2, rounds - 1
                for i in repeat(sp_, rounds):
                    for c in range(2):
                        load(i, c)

            for n in range(2):
                half = slice(n * KT // 2, (n + 1) * KT // 2)
                sp_.dma_start(xT[:, half, :], xin[:, half, :]).then_inc(x_landed[n], 16)
            for name, count, down in STAGES:
                stream(name, count, down)
            for t in range(KT):
                sp_.wait_ge(sem("final_ready"), t + 1)
                sp_.dma_start(out[:, t, :], tile(qk, t)).then_inc(out_stored, 16)
            sp_.wait_ge(out_stored, 16 * KT)

        @block.tensor
        def _(pe):
            def products(target, stationary, moving, start=True, stop=True):
                n = len(stationary)
                for k, ((sh, sl), (mh, ml)) in enumerate(zip(stationary, moving)):
                    pe.matmul(target, sh, ml, start=start and k == 0, stop=False)
                    pe.matmul(target, sh, mh, start=False, stop=False)
                    last = pe.matmul(target, sl, mh, start=False, stop=stop and k == n - 1)
                return last

            def weights(c, j, kts=KT, width=2 * P, at=0):
                w = [slice(at + k * width + j * P, at + k * width + (j + 1) * P) for k in range(kts)]
                return [(wh[:, c, s], wl[:, c, s]) for s in w]

            def acts(h, l, first=0, kts=KT):
                return [(h[:, first + k, :], l[:, first + k, :]) for k in range(kts)]

            def chunk(i, n):
                pe.wait_ge(low_ready, i + (n + 1))

            def credit(name, n):
                pe.sem_inc(sem(name), n)

            pe.wait_ge(params_landed, 2 * 16)

            def norm_sum(v):
                pe.wait_ge(sem("squares_ready"), v + 1)
                for b in range(NB):
                    last = pe.matmul(bank[7][:, b:b + 1], tmpb[:, 0, b * P:(b + 1) * P], ones[:, 0:1],
                                     start=True, stop=True)
                last.then_inc(sem("token_sums"), 1)
                pe.wait_ge(sem("diagonals_ready"), v + 1)
                pe.matmul(bank[7][:, :], ones, rstd[:, :], start=True, stop=True).then_inc(sem("rstd_ready"), 1)

            def both_columns(c, x, read, target, ready, x_ready):
                for j in range(2):
                    pe.wait_ge(sem(read), j + 1)
                for k in range(KT):
                    pe.wait_ge(sem(x_ready[0]), x_ready[1] + k + 1)
                    for j in range(2):
                        last = products(bank[target + j][:, :], weights(c, j)[k:k + 1], x[k:k + 1],
                                        start=k == 0, stop=k == KT - 1)
                        if k == KT - 1:
                            last.then_inc(sem(ready), 1)

            def feature_major(name, chunks, x, ready, read, free_after, x_ready):
                for s, v in free_after:
                    pe.wait_ge(sem(s), v)
                credit(read, 4)
                n0 = BASE[name]

                def tiles(i, n, c, j):
                    pe.wait_ge(sem(read), i * 4 + (2 * n + j + 1))
                    products(bank[2 * c + j][:, :], weights(c, j), x).then_inc(sem(ready), 1)

                chunk(0, n0)
                both_columns(0, x, read, 0, ready, x_ready)
                chunk(0, n0 + 1)
                tiles(0, 1, 1, 0)
                tiles(0, 1, 1, 1)
                for i in repeat(pe, chunks // 2 - 1):
                    for c in range(2):
                        chunk(i * 2, n0 + 2 + c)
                        for j in range(2):
                            tiles(i, 2 + c, c, j)

            def token_major(name, chunks, x, ready, read, free_after):
                for s, v in free_after:
                    pe.wait_ge(sem(s), v)
                credit(read, 4)
                n0 = BASE[name]
                for i in repeat(pe, chunks // 2):
                    for c in range(2):
                        chunk(i * 2, n0 + c)
                        w = [(wh[:, c, k * 2 * P:(k + 1) * 2 * P], wl[:, c, k * 2 * P:(k + 1) * 2 * P])
                             for k in range(KT)]
                        for j in range(2):
                            pe.wait_ge(sem(read), i * 4 + (2 * c + j + 1))
                            for b in range(2):
                                tokens = slice((2 * j + b) * P, (2 * j + b + 1) * P)
                                last = products(bank[2 * c + j][:, b * 2 * P:(b + 1) * 2 * P],
                                                [(h[:, tokens], l[:, tokens]) for h, l in x], w)
                            last.then_inc(sem(ready), 1)

            def paired(name, chunks, x0, x1, ready, read0, read1, free_after, x0_ready=None, x1_ready=None):
                for s, v in free_after:
                    pe.wait_ge(sem(s), v)
                credit(read0, 2)
                credit(read1, 2)
                n0 = BASE[name]

                def part(i, n, c, x, read, x_ready=None):
                    chunk(i * 2, n0 + 2 * n + c)
                    if x_ready:
                        both_columns(c, x, read, 2 * c, ready, x_ready)
                        return
                    for j in range(2):
                        pe.wait_ge(sem(read), i * 2 + (2 * n + j + 1))
                        products(bank[2 * c + j][:, :], weights(c, j), x).then_inc(sem(ready), 1)

                part(0, 0, 0, x0, read0, x0_ready)
                part(0, 0, 1, x1, read1, x1_ready)
                for i in repeat(pe, chunks // 2 - 1):
                    part(i, 1, 0, x0, read0)
                    part(i, 1, 1, x1, read1)

            def down(name, x, ready, read, free_after, x_ready):
                for s, v in free_after:
                    pe.wait_ge(sem(s), v)
                credit(read, 2)
                n0 = BASE[name]
                for i in repeat(pe, 4):
                    for j in range(2):
                        pe.wait_ge(sem(read), i * 2 + (j + 1))
                        for c in range(2):
                            chunk(i * 4, n0 + 2 * j + c)
                            pe.wait_ge(sem(x_ready), (c + 1) * HALF)
                            products(bank[j][:, :], weights(c, 0, HALF, P), x[c * HALF:(c + 1) * HALF],
                                     start=c == 0, stop=c == 1).then_inc(sem(ready), 1)

            def turn(v, units, y_token):
                pe.wait_ge(sem("y_read"), units + 2)
                for t in range(KT):
                    if t >= 6:
                        pe.wait_ge(sem("turn_read"), KT * v + t - 5)
                    if t >= 4 and y_token:
                        pe.wait_ge(sem(y_token), t - 3)
                    for b in range(NB):
                        last = pe.transpose(bank[2 + t % 6][:, b * P:(b + 1) * P], yt[:, b, t * P:(t + 1) * P], ident)
                    last.then_inc(sem("turned"), 1)

            def attend(*kinds):
                if kinds[0][0] == "diff":
                    for name, n in (("s_ready", 8), ("s_read", 8), ("pt_even", 1), ("pt_odd", 1), ("pv_done", 2),
                                    ("t_ready", 4), ("y_read", 2)):
                        credit(name, n)

                def scores(unit, b):
                    kind, u0, i, u = unit
                    n = (b + 1) * P
                    q = slice(b * P, n)
                    if b == 0:
                        pe.wait_ge(sem("q_staged"), i * 2 + (u0 + u + 1))
                    pe.wait_ge(sem("s_read"), i * 8 + (4 * (u0 + u) + b + 5))
                    if kind == "mla":
                        half = slice(64 * u, 64 * u + 64)
                        pe.matmul(bank[b][:, 0:n], qs[:, u, q], qk[:, i * 2 + (4 + u), 0:n], start=True, stop=False)
                        last = pe.matmul(bank[b][:, 0:n], tmpa[half, i, q], qk[half, 11, 0:n],
                                         start=False, stop=True)
                    else:
                        k = {"moba": 4, "diff": 12, "dil": 4}[kind]
                        last = pe.matmul(bank[b][:, 0:n], qs[:, u, q], tile(qk, i + k)[:, 0:n],
                                         start=True, stop=True)
                    last.then_inc(sem("s_ready"), 1)

                def transposes(unit, b):
                    kind, u0, i, u = unit
                    pe.wait_ge(sem("p_ready"), i * 8 + (4 * (u0 + u) + b + 1))
                    pe.wait_ge(sem("pt_odd" if b % 2 else "pt_even"), i * 4 + (2 * (u0 + u) + b // 2 + 1))
                    for k in range(b + 1):
                        last = pe.transpose(bank[4 + b % 2][:, k * P:(k + 1) * P], tq[:, b, k * P:(k + 1) * P],
                                            ident)
                    last.then_inc(sem("t_ready"), 1)

                def values(unit, b):
                    kind, u0, i, u = unit
                    pe.wait_ge(sem("pt_odd" if b % 2 else "pt_even"), i * 4 + (2 * (u0 + u) + b // 2 + 2))
                    if b == 0:
                        pe.wait_ge(sem("y_read"), i * 2 + (u0 + u + 1))
                    dh, c = {"moba": (64, i * P + 64 * u), "dil": (64, i * P + 64 * u), "diff": (P, i * P + 4 * P),
                             "mla": (P, i * (2 * P) + (4 + u) * P)}[kind]
                    for k in range(b + 1):
                        last = pe.matmul(bank[6 + u][:, b * dh:(b + 1) * dh],
                                         pts[:, b % 2, k * P:(k + 1) * P], vt[:, k, cut(c, dh)],
                                         start=k == 0, stop=k == b)
                    last.then_inc(sem("pv_done"), 1)

                def body(unit, following):
                    for b in range(NB):
                        transposes(unit, b)
                        if following:
                            scores(following, b)
                        if b:
                            values(unit, b - 1)
                    values(unit, NB - 1)

                for b in range(NB):
                    scores((kinds[0][0], kinds[0][2], 0, 0), b)
                in_pairs(pe, kinds, body)

            norm_sum(0)
            feature_major("qk", 8, acts(xh, xl), "qk_ready", "qk_read", [], ("xl_ready", 0))
            pe.wait_ge(inputs_landed, 4 * 16)
            for j in range(2):
                last = pe.matmul(bank[5 + j][0:ROWS, 0:TW // 2], rb[:, 0:ROWS], oh[:, j * TW // 2:(j + 1) * TW // 2],
                                 start=True, stop=True)
            last.then_inc(sem("table_mm"), 1)
            for t in range(16):
                pe.wait_ge(sem("qk_read"), t + 5)
                last = pe.matmul(bank[4][0:16, :], pick[:, 15 - t:31 - t], sq[:, t, :], start=t == 0, stop=t == 15)
            last.then_inc(sem("qk_sum"), 1)
            token_major("v", 4, acts(xh, xl), "v_ready", "v_read", [])
            pe.wait_ge(sem("v_read"), 12)
            pe.wait_ge(sem("qk_rstd"), 1)
            pe.wait_ge(sem("exact_ready"), 1)
            for t in range(16):
                if t >= 4:
                    pe.wait_ge(sem("qk_normed"), t - 3)
                for part in range(2):
                    last = pe.matmul(bank[t % 4][:, :], ident_r[0:16, t:t + 1].to_broadcast([16, P]),
                                     qkrstd[:, part, :], start=part == 0, stop=part == 1)
                last.then_inc(sem("qk_spread"), 1)
            pe.wait_ge(sem("qk_normed"), 16)
            pe.sem_inc(sem("sy_read"), 2)

            def span(kb, jb):
                at = SPAN[kb][1]
                return slice(at + (jb - kb) * P, at + S - kb * P)

            def sb_scores(i, h):
                c = h % 2
                pe.wait_ge(sem("k_staged"), i + (h + 1))
                if h >= 2:
                    pe.wait_ge(sem("w_ready"), i * 3 + 3 * (h - 1))
                for j, kbs in enumerate(((0,), (1, 3), (2,))):
                    for kb in kbs:
                        last = pe.matmul(bank[3 * c + j][:, span(kb, kb)], ks[:, kb * P:(kb + 1) * P],
                                         tile(qk, i + h)[:, kb * P:S], start=kb < 3, stop=False,
                                         skip_group_check=True)
                    last.then_inc(sem("z_ready"), 1)

            def sb_sums(i, h):
                c = h % 2
                pe.wait_ge(sem("sp_ready"), i * 2 + 2 * (h + 1))
                for j, kbs in enumerate(((0,), (1, 3), (2,))):
                    for kb in kbs:
                        for jb in range(kb, NB):
                            for part in (sph, spl):
                                pe.matmul(bank[3 * c + j][:, span(kb, jb)], negtri_r if jb == kb else negones_r,
                                          part[:, c, SPAN[jb][0], span(jb, jb)], start=False, stop=False,
                                          skip_group_check=True)
                        at = SPAN[kb][1]
                        last = pe.matmul(bank[3 * c + j][:, at:at + P], ident_r, negmask_r, start=False, stop=True,
                                         skip_group_check=True)
                    last.then_inc(sem("z_done"), 1)

            def sb_values(i, h):
                pe.wait_ge(sem("v_staged"), i + (h + 1))
                pe.wait_ge(sem("w_ready"), i * 3 + 3 * (h + 1))
                pe.wait_ge(sem("sy_read"), i + (h + 1))
                for kb in range(NB):
                    last = pe.matmul(bank[6 + h % 2][:, kb * P:S], vs[:, kb, :], wz[:, SPAN[kb][0], span(kb, kb)],
                                     start=kb == 0, stop=kb == NB - 1)
                last.then_inc(sem("sy_ready"), 1)

            sb_scores(0, 0)
            sb_scores(0, 1)
            sb_sums(0, 0)
            for i in repeat(pe, 3):
                for h in (1, 2):
                    sb_scores(i * 2, h + 1)
                    sb_values(i * 2, h - 1)
                    sb_sums(i * 2, h)
            sb_values(0, 6)
            sb_sums(0, 7)
            sb_values(0, 7)
            paired("gate2", 8, acts(xh, xl), acts(yh, yl), "g2_ready", "g2_gate", "g2_prod", [("sy_read", 10)],
                   x1_ready=("yl0_ready", 0))
            feature_major("pool", 4, acts(xh, xl), "pool_ready", "pool_read", [("g2_gate", 10), ("g2_prod", 10)],
                          ("xl_ready", 0))
            pe.wait_ge(sem("pool_read"), 12)
            for c in range(2):
                chunk(0, BASE["wpool"] + c)
                for g in range(2):
                    pe.wait_ge(sem("p_low"), 4 * c + 2 * g + 2)
                    for j in range(2):
                        f = 4 * c + 2 * g
                        if c:
                            pe.wait_ge(sem("wpool_low"), 2 * g + j + 1)
                        products(bank[2 * g + j][:, :], weights(c, j, 2, at=g * 2 * 2 * P),
                                 acts(yh, yl, f, 2)).then_inc(sem("wpool_ready"), 1)
            pe.wait_ge(sem("wpool_low"), 8)
            paired("gate0", 8, acts(xh, xl), acts(yh, yl), "g0_ready", "g0_gate", "g0_prod", [])
            pe.wait_ge(sem("g0_gate"), 10)
            pe.wait_ge(sem("g0_prod"), 10)
            pe.wait_ge(sem("rg_landed"), 16)

            def lru_gates(t):
                pe.wait_ge(sem("lru_conv"), 3 * t + 3)
                if t >= 2:
                    pe.wait_ge(sem("lru_sigmoid"), 2 * (t - 2) + 2)
                pe.matmul(bank[4 + 2 * (t % 2)][:, :], rgw[:, t, :], xc[:, t, :], start=True, stop=True)
                pe.matmul(bank[5 + 2 * (t % 2)][:, :], rgw[:, 8 + t, :], xc[:, t, :], start=True,
                          stop=True).then_inc(sem("lru_gate"), 1)

            for t in range(KT):
                if t % 2 == 0:
                    chunk(0, BASE["lru"] + t // 2)
                if t >= 4:
                    pe.wait_ge(sem("lru_conv"), 3 * (t - 4) + 3)
                products(bank[t % 4][:, :], weights(t // 2 % 2, t % 2), acts(xh, xl)).then_inc(sem("lru_ready"), 1)
                if t:
                    lru_gates(t - 1)
            lru_gates(KT - 1)
            paired("gate1", 8, acts(xh, xl), acts(yh, yl), "g1_ready", "g1_gate", "g1_prod", [("lru_conv", 24)],
                   x1_ready=("lru_low", 0))
            feature_major("out", 4, acts(yh, yl), "out_ready", "out_read", [("g1_gate", 10), ("g1_prod", 10)],
                          ("yl1_ready", 0))

            def ffn(n, v):
                norm_sum(v)
                paired(f"ffn{n}", FT, acts(xh, xl), acts(xh, xl), f"f{n}_ready", f"f{n}_gate", f"f{n}_prod", [],
                       x0_ready=("xl_ready", KT * v))
                down(f"down{n}", acts(ah, al, 0, FT), f"d{n}_ready", f"d{n}_read", [(f"f{n}_gate", FT + 2)],
                     f"f{n}_low")

            ffn(0, 1)
            norm_sum(2)
            feature_major("eqk", 8, acts(xh, xl), "eqk_ready", "eqk_read", [("d0_read", 10)],
                          ("xl_ready", KT * 2))
            token_major("ev", 4, acts(xh, xl), "ev_ready", "ev_read", [("eqk_read", 20)])
            pe.wait_ge(sem("ev_read"), 12)
            attend(("diff", 4, 0), ("moba", 4, 8))
            turn(0, 16, "y_token")
            feature_major("eout", 4, acts(xh, xl), "eo_ready", "eo_read", [], ("turn_read", 0))
            ffn(1, 3)
            norm_sum(4)
            feature_major("oqk", 6, acts(xh, xl), "oqk_ready", "oqk_read", [("d1_read", 10)],
                          ("xl_ready", KT * 4))
            for t in range(3):
                pe.wait_ge(sem("c_square"), t + 1)
                pe.matmul(bank[6 + t // 2][:, :], ones, tile(tmpb, t % 2), start=t != 1,
                          stop=t != 0).then_inc(sem("c_sum"), 1)
            token_major("ov", 2, acts(xh, xl), "ov_ready", "ov_read", [("oqk_read", 16)])
            pe.wait_ge(sem("ov_read"), 8)
            pe.wait_ge(sem("c_var"), 2)
            attend(("dil", 4, 16),)
            pe.wait_ge(sem("s_read"), 8 + 4 * 24)
            pe.wait_ge(sem("y_read"), 26)
            pe.matmul(bank[4][:, :], small_rot, qk[:, 11, :], start=True, stop=True).then_inc(sem("rotated"), 1)
            pe.wait_ge(sem("cl_ready"), 3)
            cq = [(ch[t], cl[t]) for t in range(2)]
            chunk(0, BASE["mla"])
            for n, j in enumerate((4, 5, 0, 1, 2, 3)):
                if n >= 4:
                    pe.wait_ge(sem("mla_read"), n - 3)
                products(bank[n % 4][:, :], weights(0, j, 2, 6 * P), cq).then_inc(sem("mla_ready"), 1)
            for t in range(2):
                pe.wait_ge(sem("mla_read"), t + 1)
                pe.matmul(bank[5 + t][:, :], small_rot, qk[:, 12 + t, :], start=True, stop=True)\
                  .then_inc(sem("rotated"), 1)
            chunk(0, BASE["mla"] + 1)
            for j in range(4):
                pe.wait_ge(sem("mla_read"), j + 3)
                products(bank[(6 + j) % 4][:, :], weights(1, j, 1), [(ch[2], cl[2])]).then_inc(sem("mla_ready"), 1)
            for b in range(NB):
                tokens = slice(b * P, (b + 1) * P)
                pe.wait_ge(sem("mla_read"), b + 7)
                products(bank[(10 + b) % 4][:, :], [(ch[2][:, tokens], cl[2][:, tokens])],
                         [(wh[:, 1, 4 * P:8 * P], wl[:, 1, 4 * P:8 * P])]).then_inc(sem("mla_ready"), 1)
            pe.wait_ge(sem("mla_read"), 14)
            pe.wait_ge(sem("roped"), 3)
            attend(("mla", 2, 24),)
            turn(1, 28, None)
            feature_major("oout", 4, acts(xh, xl), "oo_ready", "oo_read", [], ("turn_read", KT))
            ffn(2, 5)
            norm_sum(6)

        @block.gpsimd
        def _(pool):
            def low(i, n, c):
                pool.wait_ge(high_ready, i + (n + 1))
                pool.tensor_tensor(wl[:, c, :], raw[:, c, :], wh[:, c, :].bitcast(F32),
                                   ALU.subtract).then_inc(low_ready, 1)

            def stage(name, count):
                n0 = BASE[name] + 2
                rounds = count // 2 - (1 if n0 + count > CHUNKS else 0)
                for i in repeat(pool, rounds):
                    for c in range(2):
                        low(i * 2, n0 + c, c)

            def query(kind, u0, i, n, u):
                g = u0 + 2 * n + u
                if g >= 2:
                    pool.wait_ge(sem("s_ready"), i * 8 + (4 * g + 4))
                if kind == "mla":
                    if u == 0:
                        pool.tensor_copy(tmpa[:, n, :], qk[:, n + 12, :])
                    pool.tensor_copy(qs[:, u, :], qk[:, 2 * n + u, :]).then_inc(sem("q_staged"), 1)
                else:
                    first = {"moba": 0, "diff": 8, "dil": 0}[kind] + n
                    half = slice(64 * u, 64 * u + 64)
                    q = qk[half, first:first + 1, :] if type(i) is int else qk[half, bass.ds(i + first, 1), :]
                    pool.tensor_copy(qs[half, u:u + 1, :], q).then_inc(sem("q_staged"), 1)
                pool.wait_ge(sem("q_staged"), i * 2 + (g + 1))
                if g >= 2:
                    pool.wait_ge(sem("s_read"), i * 8 + (4 * g + 4))
                row = {"moba": i * 2 + (2 * n + u), "diff": i + (8 + n), "dil": i * 2 + (12 + 2 * n + u),
                       "mla": MASK_ROW}[kind]
                pool.sem_inc(sem("bias_begun"), 1)
                one = table[cut(row, 1), 0:S]
                src = bass.AP(tensor=one.tensor, offset=one.offset, ap=[[1, P], [1, S]])
                pool.dma_start(bt[:, u, :], src).then_inc(sem(f"bias_landed_{u}"), 16)

            def begin(kind, u0, lows, ready, ready_at, free, zeroed):
                pool.wait_ge(low_ready, lows)
                pool.wait_ge(sem(free), 10)
                pool.wait_ge(sem(ready), ready_at)
                for u in range(2):
                    pool.memset(qs[64 - 64 * u:P - 64 * u, u, :], 0.0).then_inc(sem("qs_zero"), 1)
                    pool.wait_ge(sem("qs_zero"), zeroed + u + 1)
                for u in range(2):
                    query(kind, u0, 0, 0, u)

            def attend(*kinds):
                for k, (kind, pairs, u0) in enumerate(kinds):
                    n = 0 if k else 1
                    for i in repeat(pool, pairs - n):
                        for u in range(2):
                            query(kind, u0, i, n, u)

            for n in range(2):
                low(0, n, n)
            stage("qk", 8)
            pool.wait_ge(table_ready, 1)
            pool.dma_start(table[:, :], tt[:, :]).then_inc(table_stored, 16)
            pool.wait_ge(table_stored, 16)
            stage("v", 4)
            pool.wait_ge(sem("qk_normed"), 16)
            pool.wait_ge(sem("v_read"), 12)

            def stage_keys(i, h):
                if h:
                    pool.wait_ge(sem("z_ready"), i * 3 + 3 * h)
                pool.tensor_copy(ks[:, :], tile(qk, i + (h + 8))).then_inc(sem("k_staged"), 1)

            def stage_values(i, h):
                if h:
                    pool.wait_ge(sem("sy_ready"), i + h)
                pool.tensor_copy(vs[:, :, :], vt[:, :, cut(i * P + h * P, P)]).then_inc(sem("v_staged"), 1)

            stage_keys(0, 0)
            stage_values(0, 0)
            stage_keys(0, 1)
            for i in repeat(pool, 6):
                stage_keys(i, 2)
                stage_values(i, 1)
            stage_values(0, 7)
            pool.wait_ge(sem("sy_read"), 10)
            pool.dma_start(rgw[:, :, :], rg_in).then_inc(sem("rg_landed"), 16)
            stage("gate2", 8)
            for name in ("pool", "wpool", "gate0", "lru", "gate1", "out", "ffn0"):
                stage(name, COUNT[name])
            stage("down0", 16)
            stage("eqk", 8)
            begin("diff", 0, BASE["ev"] + 2, "eqk_read", 20, "d0_read", 0)
            stage("ev", 4)
            attend(("diff", 4, 0), ("moba", 4, 8))
            stage("eout", 4)
            stage("ffn1", FT)
            stage("down1", 16)
            pool.wait_ge(sem("d1_read"), 10)
            pool.dma_start(rope[:, :, :], rope_in).then_inc(sem("rope_landed"), 16)
            stage("oqk", 6)
            begin("dil", 16, BASE["ov"] + 2, "oqk_read", 16, "d1_read", 2)
            stage("ov", 2)
            attend(("dil", 4, 16),)
            pool.wait_ge(sem("mla_read"), 6)
            pool.wait_ge(sem("roped"), 3)
            for u in range(2):
                query("mla", 24, 0, 0, u)
            stage("mla", 2)
            attend(("mla", 2, 24),)
            stage("oout", 4)
            stage("ffn2", FT)
            stage("down2", 16)

        @block.scalar
        def _(act):
            step = Steps(act, sem("act_step"))

            def refill(c, n, i=0):
                if type(i) is not int:
                    act.wait_ge(raw_landed[c], i * 8 + 16 * (n // 2 + 1))
                else:
                    act.wait_ge(raw_landed[c], 16 * ((i + n) // 2 + 1))
                act.activation(wh[:, c, :], raw[:, c, :], ACT.Copy).then_inc(high_ready, 1)

            def norm(v):
                act.preload_act_table(ACT.Sqrt)
                act.wait_ge(sem("var_ready"), v + 1)
                act.activation(token_rstd, token_rstd, ACT.Sqrt).then_inc(sem("std_ready"), 1)
                if v == 0:
                    act.wait_ge(raw_landed[1], 16)
                    act.activation(wh[:, 1, :], raw[:, 1, :], ACT.Copy).then_inc(high_ready, 1)
                    act.wait_ge(params_landed, 2 * 16)
                if v < 6:
                    for t in range(KT):
                        act.wait_ge(sem("nx_ready"), KT * v + t + 1)
                        act.activation(xh[:, t, :], tmpa[:, t % 2, :], ACT.Copy).then_inc(sem("xh_ready"), 1)

            def copies(name, chunks, ready, read, scale, squares=False):
                n0 = BASE[name] + 2
                for i in repeat(act, chunks // 2):
                    for c in range(2):
                        for j in range(2):
                            act.wait_ge(sem(ready), i * 4 + (2 * c + j + 1))
                            if squares:
                                act.activation(tile(sq, i * 4 + (2 * c + j)), bank[2 * c + j][:, :], ACT.Square)
                            act.activation(tile(qk, i * 4 + (2 * c + j)), bank[2 * c + j][:, :], ACT.Copy,
                                           scale=col(scale, i * 4 + (2 * c + j))).then_inc(sem(read), 1)
                        refill(c, n0 + c, i * 2)

            def value_copies(name, chunks, ready, read):
                n0 = BASE[name] + 2
                for i in repeat(act, chunks // 2):
                    for c in range(2):
                        for j in range(2):
                            act.wait_ge(sem(ready), i * 4 + (2 * c + j + 1))
                            act.activation(vt[:, 2 * j:2 * j + 2, cut(i * S + c * 2 * P, 2 * P)],
                                           bank[2 * c + j][:, :].rearrange("p (b n) -> p b n", b=2),
                                           ACT.Copy).then_inc(sem(read), 1)
                        refill(c, n0 + c, i * 2)

            def gates(b, name, ready, gate, prod, refilled=False):
                n0 = BASE[name] + 2

                def round_(i, n):
                    for j in range(2):
                        act.wait_ge(sem(ready), i * 4 + (4 * n + j + 1))
                        act.wait_ge(sem(prod), i * 2 + (2 * n + j + 1))
                        act.activation(tmpa[:, j, :], bank[j][:, :], ACT.Sigmoid,
                                       bias=col("b_gate", i * 2 + (8 * b + 2 * n + j))).then_inc(sem(gate), 1)
                    if n or not refilled:
                        refill(0, n0 + 2 * n, i * 2)
                    act.wait_ge(sem(ready), i * 4 + (4 * n + 4))
                    refill(1, n0 + 2 * n + 1, i * 2)

                act.preload_act_table(ACT.Sigmoid)
                round_(0, 0)
                for i in repeat(act, 3):
                    round_(i, 1)

            def refills(name, chunks, ready, per, last=False):
                n0 = BASE[name] + 2
                for i in repeat(act, chunks // 2 - last):
                    for c in range(2):
                        act.wait_ge(sem(ready), i * (2 * per) + per * (c + 1))
                        refill(c, n0 + c, i * 2)

            def split(high, source, source_ready):
                for t in range(KT):
                    act.wait_ge(sem(source_ready[0]), source_ready[1] + t)
                    act.activation(yh[:, t, :], source[:, t, :], ACT.Copy).then_inc(sem(high), 1)

            def ffn(n, v):
                norm(v)
                name, ready, n0 = f"ffn{n}", f"f{n}_ready", BASE[f"ffn{n}"] + 2
                act.preload_act_table(ACT.Gelu if n else ACT.Silu)
                for i in repeat(act, FT // 2):
                    for j in range(2):
                        act.wait_ge(sem(ready), i * 4 + (j + 1))
                        if n == 0:
                            act.activation(tmpa[:, j, :], bank[j][:, :], ACT.Silu).then_inc(sem("f0_gate"), 1)
                        else:
                            k = (n - 1) * FT
                            act.activation(tmpa[:, j, :], bank[j][:, :], ACT.Identity,
                                           bias=col("ffn_b", i * 2 + (k + j)),
                                           scale=col("ffn_w", i * 2 + (3 * k + 2 * FT + j)))\
                               .then_inc(sem(f"f{n}_conv0"), 1)
                    refill(0, n0, i * 2)
                    if n:
                        for j in range(2):
                            act.wait_ge(sem(f"f{n}_gate"), i * 2 + (j + 3))
                            act.activation(tmpa[:, j, :], tmpa[:, j, :], ACT.Gelu).then_inc(sem(f"f{n}_gelu"), 1)
                    for j in range(2):
                        act.wait_ge(sem(f"f{n}_prod"), i * 2 + (j + 3))
                        act.activation(tile(ah, i * 2 + j), tmpb[:, j, :], ACT.Copy).then_inc(sem(f"f{n}_high"), 1)
                    refill(1, n0 + 1, i * 2)
                refills(f"down{n}", 16, f"d{n}_ready", 1, last=n == 2)

            def attend(*kinds):
                def exponent(unit, b):
                    _, u0, i, u = unit
                    n = (b + 1) * P
                    act.wait_ge(sem("s_read"), i * 8 + (4 * (u0 + u) + b + 9))
                    act.activation(tq[:, b, 0:n], tq[:, b, 0:n], ACT.Exp, bias=nm[:, u, b:b + 1], scale=-1.0,
                                   accum_out=rs[:, u, b:b + 1]).then_inc(sem("p_ready"), 1)

                def copy_even(unit, b):
                    _, u0, i, u = unit
                    q = 4 * (u0 + u) + b
                    act.wait_ge(sem("t_ready"), i * 8 + (q + 5))
                    act.wait_ge(sem("pv_done"), i * 8 + (q + 1))
                    act.activation(pts[:, 0, 0:(b + 1) * P], bank[4][:, 0:(b + 1) * P], ACT.Copy)\
                       .then_inc(sem("pt_even"), 1)

                def body(unit, following):
                    for b in (0, 2):
                        copy_even(unit, b)
                        if following:
                            exponent(following, b)
                            exponent(following, b + 1)

                act.preload_act_table(ACT.Exp)
                for b in range(NB):
                    exponent((kinds[0][0], kinds[0][2], 0, 0), b)
                in_pairs(act, kinds, body)

            def turn(v):
                for t in range(KT):
                    act.wait_ge(sem("turned"), KT * v + t + 1)
                    act.activation(xh[:, t, :], bank[2 + t % 6][:, :], ACT.Copy,
                                   scale=col("one_scale" if v else "subln", t)).then_inc(sem("turn_high"), 1)

            for t in range(KT):
                if t % 4 == 0:
                    act.wait_ge(x_landed[t // 4], 16)
                act.activation(qk[:, t, :], xT[:, t, :], ACT.Square).then_inc(sem("x_square"), 1)
            act.wait_ge(raw_landed[0], 16)
            act.activation(wh[:, 0, :], raw[:, 0, :], ACT.Copy).then_inc(high_ready, 1)
            norm(0)
            act.activation(exact[:, :, :], mats[:, 1:5, :], ACT.Copy).then_inc(sem("exact_ready"), 1)
            copies("qk", 8, "qk_ready", "qk_read", "one_scale", squares=True)
            act.wait_ge(sem("qk_var"), 1)
            act.activation(rstd[0:16, :], rstd[0:16, :], ACT.Sqrt).then_inc(sem("qk_std"), 1)
            act.wait_ge(sem("lambda_sums"), 2)
            act.activation(t1, col("lru_lambda", 0, 8), ACT.Abs).then_inc(sem("lambda_abs"), 1)
            act.wait_ge(sem("lambda_abs"), 1)
            act.activation(t1, t1, ACT.Exp, scale=-1.0).then_inc(sem("lambda_exp"), 1)
            act.activation(lam2, lam2, ACT.Exp).then_inc(sem("lambda_exp"), 1)
            act.wait_ge(table_stored, 16)
            value_copies("v", 4, "v_ready", "v_read")

            def softplus(i, h):
                c, at = h % 2, i * 6 + 6 * h
                tiles = [(sp[:, c, j, 0:w], bank[3 * c + j][:, 0:w]) for j, w in enumerate((S, S, 2 * P))]
                for j, (w, z) in enumerate(tiles):
                    act.wait_ge(sem("z_ready"), i * 3 + (3 * h + j + 1))
                    act.activation(w, z, ACT.Abs).then_inc(sem("sp_chain"), 1)
                for j, (w, z) in enumerate(tiles):
                    act.wait_ge(sem("sp_chain"), at + (j + 1))
                    act.activation(w, w, ACT.Exp, scale=-1.0).then_inc(sem("sp_chain"), 1)
                for j, (w, z) in enumerate(tiles):
                    act.wait_ge(sem("sp_chain"), at + (j + 4))
                    act.activation(w, w, ACT.Ln, bias=1.0).then_inc(sem("ln_ready"), 1)

            def sb_weights(i, h):
                for j, w in enumerate((S, S, 2 * P)):
                    act.wait_ge(sem("z_done"), i * 3 + (3 * h + j + 1))
                    act.activation(wz[:, j, 0:w], bank[3 * (h % 2) + j][:, 0:w], ACT.Exp)\
                       .then_inc(sem("w_ready"), 1)

            def sb_output(i, h):
                act.wait_ge(sem("sy_ready"), i + (h + 1))
                act.activation(tile(qk, i + h), bank[6 + h % 2][:, :], ACT.Copy).then_inc(sem("sy_read"), 1)

            act.preload_act_table_set("natural_log_exp_and_others")
            softplus(0, 0)
            softplus(0, 1)
            sb_weights(0, 0)
            for i in repeat(act, 3):
                for h in (1, 2):
                    softplus(i * 2, h + 1)
                    sb_output(i * 2, h - 1)
                    sb_weights(i * 2, h)
            sb_output(0, 6)
            sb_weights(0, 7)
            sb_output(0, 7)
            act.wait_ge(sem("sy_read"), 10)
            for t in range(KT):
                act.activation(yh[:, t, :], qk[:, t, :], ACT.Copy).then_inc(sem("yh0_ready"), 1)
            gates(2, "gate2", "g2_ready", "g2_gate", "g2_prod")
            for t in range(KT + 1):
                if t < KT:
                    act.wait_ge(sem("pool_ready"), t + 1)
                    if t >= 2:
                        act.wait_ge(sem("p_low"), t - 1)
                    else:
                        act.wait_ge(sem("pads_ready"), 4)
                    act.activation(pu[:, t % 2, 16:16 + S], bank[t % 4][:, :], ACT.Copy).then_inc(sem("pool_read"), 1)
                if t:
                    act.wait_ge(sem("p_ready_value"), t)
                    act.activation(yh[:, t - 1, :], tmpb[:, (t - 1) % 2, :], ACT.Copy).then_inc(sem("p_high"), 1)
                if t < KT and t % 2:
                    refill(t // 2 % 2, BASE["pool"] + t // 2 + 2)
            for c in range(2):
                for g in range(2):
                    for j in range(2):
                        f = 4 * c + 2 * g
                        act.wait_ge(sem("wpool_ready"), f + 2)
                        act.activation(yh[:, f + j, :], bank[2 * g + j][:, :], ACT.Copy,
                                       scale=col("pool_scale", f + j)).then_inc(sem("wpool_high"), 1)
                refill(c, BASE["wpool"] + c + 2)
            gates(0, "gate0", "g0_ready", "g0_gate", "g0_prod")
            def lru_base(t):
                act.wait_ge(sem("lru_ready"), t + 1)
                act.activation(xc[:, t, :], bank[t % 4][:, :], ACT.Identity, bias=col("conv_b", t),
                               scale=col("conv_w", 24 + t)).then_inc(sem("lru_base"), 1)
                if t % 2:
                    refill(t // 2 % 2, BASE["lru"] + t // 2 + 2)

            def lru_sigmoids(t):
                act.wait_ge(sem("lru_gate"), t + 1)
                act.activation(rr[:, t, :], bank[4 + 2 * (t % 2)][:, :], ACT.Sigmoid, bias=col("b_rg", t))\
                   .then_inc(sem("lru_sigmoid"), 1)
                act.activation(ii[:, t, :], bank[5 + 2 * (t % 2)][:, :], ACT.Sigmoid, bias=col("b_ig", t))\
                   .then_inc(sem("lru_sigmoid"), 1)
                act.wait_ge(sem("lru_sigmoid"), 2 * t + 2)
                if t >= 4:
                    act.wait_ge(sem("lru_h"), 3 * (t - 4) + 2)
                act.activation(tanh[:, t % 4, :], rr[:, t, :], ACT.Tanh, scale=decay8[:, t:t + 1])\
                   .then_inc(sem("lru_tanh"), 1)

            def lru_rest(tiles):
                for t in tiles:
                    act.wait_ge(sem("lru_tanh"), t + 1)
                    act.activation(rr[:, t, :], rr[:, t, :], ACT.Exp, scale=ndecay8[:, t:t + 1])\
                       .then_inc(sem("lru_a"), 1)
                if tiles[0] == 0:
                    lru_base(5)
                for t in tiles:
                    act.wait_ge(sem("lru_m2"), 2 * t + 2)
                    act.activation(tanh[:, t % 4, :], tanh[:, t % 4, :], ACT.Sqrt).then_inc(sem("lru_mult"), 1)

            def lru_highs(tiles):
                for t in tiles:
                    act.wait_ge(sem("lru_h"), 3 * t + 3)
                    act.activation(yh[:, t, :], xc[:, t, :], ACT.Copy).then_inc(sem("lru_high"), 1)

            for t in range(KT + 1):
                if t < KT and t != 5:
                    lru_base(t)
                if t == 6:
                    lru_highs((0, 1))
                if t:
                    lru_sigmoids(t - 1)
                if t in (4, 7, 8):
                    lru_rest({4: (0, 1, 2, 3), 7: (4, 5, 6), 8: (7,)}[t])
                if t >= 7:
                    lru_highs({7: (2, 3, 4, 5, 6), 8: (7,)}[t])
                if t == KT:
                    act.wait_ge(sem("g1_ready"), 2)
                    refill(0, BASE["gate1"] + 2)
            gates(1, "gate1", "g1_ready", "g1_gate", "g1_prod", refilled=True)
            for t in range(KT):
                act.wait_ge(sem("merged_ready"), t + 1)
                act.wait_ge(sem("g1_ready"), 16)
                act.activation(yh[:, t, :], merged[:, t, :], ACT.Copy).then_inc(sem("yh1_ready"), 1)
            refills("out", 4, "out_ready", 2)
            ffn(0, 1)
            norm(2)
            copies("eqk", 8, "eqk_ready", "eqk_read", "even_scale")
            value_copies("ev", 4, "ev_ready", "ev_read")
            attend(("diff", 4, 0), ("moba", 4, 8))
            act.wait_ge(sem("diff_var"), 1)
            act.activation(dss, dss, ACT.Sqrt).then_inc(sem("diff_std"), 1)
            turn(0)
            refills("eout", 4, "eo_ready", 2)
            ffn(1, 3)
            norm(4)
            copies("oqk", 6, "oqk_ready", "oqk_read", "odd_scale")
            act.wait_ge(sem("oqk_read"), 16)
            for t in range(3):
                if t == 2:
                    act.wait_ge(sem("c_sum"), 1)
                act.activation(tmpb[:, t % 2, :], qk[:, 8 + t, :], ACT.Square).then_inc(sem("c_square"), 1)
            for t in range(2):
                act.wait_ge(sem("c_var"), t + 1)
                act.activation(tmpa[:, t, :], tmpa[:, t, :], ACT.Sqrt).then_inc(sem("c_std"), 1)
            value_copies("ov", 2, "ov_ready", "ov_read")
            for t in range(3):
                act.wait_ge(sem("c_normed"), t + 1)
                act.activation(ch[t], qk[:, 8 + t, :], ACT.Copy).then_inc(sem("ch_ready"), 1)
            attend(("dil", 4, 16),)
            for n in range(14):
                act.wait_ge(sem("mla_ready"), n + 1)
                if n < 6:
                    act.activation(qk[:, 12 + n if n < 2 else n - 2, :], bank[n % 4][:, :], ACT.Copy,
                                   scale=192 ** -0.5).then_inc(sem("mla_read"), 1)
                elif n < 10:
                    act.activation(qk[:, n - 2, :], bank[n % 4][:, :], ACT.Copy).then_inc(sem("mla_read"), 1)
                else:
                    act.activation(vt[:, n - 10, S:2 * S], bank[n % 4][:, :], ACT.Copy).then_inc(sem("mla_read"), 1)
                if n in (5, 13):
                    refill(n // 13, BASE["mla"] + 2 + n // 13)
            attend(("mla", 2, 24),)
            turn(1)
            refills("oout", 4, "oo_ready", 2)
            ffn(2, 5)
            norm(6)

        @block.vector
        def _(dve):
            step = Steps(dve, sem("dve_step"))

            def norm(v, gain, g0):
                dve.wait_ge(sem("token_sums"), v + 1)
                dve.tensor_scalar(token_rstd, bank[7][:, 0:NB], 1.0 / D, EPS, ALU.mult, ALU.add)\
                   .then_inc(sem("var_ready"), 1)
                dve.wait_ge(sem("std_ready"), v + 1)
                step(dve.reciprocal(token_rstd, token_rstd))
                dve.tensor_tensor(rstd[:, :].rearrange("p (b n) -> p b n", b=NB),
                                  ident.unsqueeze(1).to_broadcast([P, NB, P]),
                                  token_rstd.unsqueeze(2).to_broadcast([P, NB, P]), ALU.mult)\
                   .then_inc(sem("diagonals_ready"), 1)
                dve.wait_ge(sem("rstd_ready"), v + 1)
                for t in range(KT + 1):
                    if t < KT:
                        target = qk[:, t, :] if v == 6 else tmpa[:, t % 2, :]
                        if t >= 2 and v < 6:
                            dve.wait_ge(sem("xl_ready"), KT * v + t - 1)
                        dve.scalar_tensor_tensor(target, xT[:, t, :], col(gain, g0 + t), bank[7][:, :], ALU.mult,
                                                 ALU.mult).then_inc(sem("final_ready" if v == 6 else "nx_ready"), 1)
                    if t and v < 6:
                        dve.wait_ge(sem("xh_ready"), KT * v + t)
                        dve.tensor_tensor(xl[:, t - 1, :], tmpa[:, (t - 1) % 2, :], xh[:, t - 1, :].bitcast(F32),
                                          ALU.subtract).then_inc(sem("xl_ready"), 1)

            def products(name, first, ready, gate, prod):
                for i in repeat(dve, 4, step, 0 if first else 2):
                    for j in range(2):
                        dve.wait_ge(sem(gate), i * 2 + (j + 3))
                        dve.wait_ge(sem(ready), i * 4 + (j + 3))
                        if first:
                            dve.tensor_tensor(tile(merged, i * 2 + j), bank[2 + j][:, :], tmpa[:, j, :], ALU.mult)\
                               .then_inc(sem(prod), 1)
                        else:
                            dve.tensor_tensor(tmpb[:, j, :], bank[2 + j][:, :], tmpa[:, j, :], ALU.mult)\
                               .then_inc(sem(prod), 1)
                            dve.wait_ge(sem(prod), i * 2 + (j + 3))
                            step(dve.tensor_tensor(tile(merged, i * 2 + j), tile(merged, i * 2 + j), tmpb[:, j, :],
                                                   ALU.add))

            def residual(chunks, ready, read, per):
                rounds, tiles = (chunks // 2, 4) if per == 1 else (4, 2)
                step(dve.memset(tmpb[:, 0, :], 0.0))
                for i in repeat(dve, rounds, step, 2 * tiles):
                    for j in range(tiles):
                        dve.wait_ge(sem(ready), i * (tiles * per) + per * (j + 1))
                        t = i * tiles + j
                        dve.tensor_tensor(tile(xT, t), tile(xT, t), bank[j][:, :], ALU.add).then_inc(sem(read), 1)
                        dve.wait_ge(sem(read), i * tiles + (j + 1 + (4 if per == 1 else 2)))
                        step(dve.tensor_tensor(tmpb[:, 1, :], tile(xT, t), tile(xT, t), ALU.mult))
                        step(dve.tensor_tensor(tmpb[:, 0, :], tmpb[:, 0, :], tmpb[:, 1, :], ALU.add))
                dve.sem_inc(sem("squares_ready"), 1)

            def ffn(n, v, gain, g0):
                norm(v, gain, g0)
                for i in repeat(dve, FT // 2, step, 2 if n else 0):
                    if n:
                        for j in range(2):
                            k = 3 * (n - 1) * FT
                            dve.wait_ge(sem(f"f{n}_conv0"), i * 2 + (j + 1))
                            a = tmpa[:, j, :]
                            step(dve.scalar_tensor_tensor(a[:, 1:S], bank[j][:, 0:S - 1],
                                                          col("ffn_w", i * 2 + (k + FT + j)), a[:, 1:S],
                                                          ALU.mult, ALU.add))
                            dve.scalar_tensor_tensor(a[:, 2:S], bank[j][:, 0:S - 2], col("ffn_w", i * 2 + (k + j)),
                                                     a[:, 2:S], ALU.mult, ALU.add).then_inc(sem(f"f{n}_gate"), 1)
                    for j in range(2):
                        dve.wait_ge(sem(f"f{n}_ready"), i * 4 + (j + 3))
                        dve.wait_ge(sem(f"f{n}_gelu" if n else "f0_gate"), i * 2 + (j + (1 if n else 3)))
                        dve.tensor_tensor(tmpb[:, j, :], tmpa[:, j, :], bank[2 + j][:, :], ALU.mult)\
                           .then_inc(sem(f"f{n}_prod"), 1)
                    for j in range(2):
                        dve.wait_ge(sem(f"f{n}_high"), i * 2 + (j + 1))
                        dve.tensor_tensor(tile(al, i * 2 + j), tmpb[:, j, :], tile(ah, i * 2 + j).bitcast(F32),
                                          ALU.subtract).then_inc(sem(f"f{n}_low"), 1)
                    dve.wait_ge(sem(f"f{n}_low"), i * 2 + 2)
                residual(16, f"d{n}_ready", f"d{n}_read", 2)

            def attend(*kinds):
                def shifted(unit, b):
                    _, u0, i, u = unit
                    q = 4 * (u0 + u) + b
                    n = (b + 1) * P
                    dve.wait_ge(sem(f"bias_landed_{u}"), i * 16 + 16 * (u0 // 2 + 1))
                    dve.wait_ge(sem("s_ready"), i * 8 + (q + 9))
                    dve.wait_ge(sem("t_ready"), i * 8 + (q + 1))
                    dve.sem_inc(sem("shift_begun"), 1)
                    dve.tensor_tensor_reduce(tq[:, b, 0:n], bank[b][:, 0:n], bt[:, u, 0:n][:, ::-1], -1.0,
                                             3.0e38, ALU.add, ALU.min, nm[:, u, b:b + 1])\
                       .then_inc(sem("s_read"), 1)

                def copy_odd(unit, b):
                    _, u0, i, u = unit
                    q = 4 * (u0 + u) + b
                    dve.wait_ge(sem("t_ready"), i * 8 + (q + 5))
                    dve.wait_ge(sem("pv_done"), i * 8 + (q + 1))
                    dve.tensor_copy(pts[:, 1, 0:(b + 1) * P], bank[5][:, 0:(b + 1) * P])\
                       .then_inc(sem("pt_odd"), 1)

                def normalised(unit):
                    kind, u0, i, u = unit
                    dve.wait_ge(sem("pv_done"), i * 8 + (4 * (u0 + u) + 6))
                    step(dve.reciprocal(rd[:, u, :], rs[:, u, :]))
                    if kind != "diff":
                        dh, c = (P, i * (2 * P) + (4 + u) * P) if kind == "mla" else (64, i * P + 64 * u)
                        dve.tensor_tensor(yt[:, :, cut(c, dh)],
                                          bank[6 + u][:, 0:NB * dh].rearrange("p (b n) -> p b n", b=NB),
                                          rd[:, u, :].unsqueeze(2).to_broadcast([P, NB, dh]), ALU.mult)\
                           .then_inc(sem("y_read"), 1)
                    elif u == 1:
                        step(dve.tensor_scalar(rd[:, 1, :], rd[:, 1, :], nlam, None, ALU.mult))
                        for k in range(2):
                            dve.tensor_tensor((tmpa, tmpb)[k][:, 0, :].rearrange("p (b n) -> p b n", b=NB),
                                              bank[6 + k][:, :].rearrange("p (b n) -> p b n", b=NB),
                                              rd[:, k, :].unsqueeze(2).to_broadcast([P, NB, P]), ALU.mult)\
                               .then_inc(sem("y_read"), 1)
                        dve.wait_ge(sem("y_read"), i * 2 + (u0 + 4))
                        y = yt[:, :, cut(i * P + 4 * P, P)]
                        step(dve.tensor_tensor(y, tmpa[:, 0, :].rearrange("p (b n) -> p b n", b=NB),
                                               tmpb[:, 0, :].rearrange("p (b n) -> p b n", b=NB), ALU.add))
                    if kind == "moba" and u == 1:
                        y = yt[:, :, cut(i * P + 4 * P, P)]
                        w = tmpa[:, 1, :].rearrange("p (b n) -> p b n", b=NB)
                        step(dve.tensor_tensor(w, y, y, ALU.mult))
                        step(dve.tensor_reduce(dss[:, :, cut(i, 1)], w, AX.X, ALU.add))

                def body(unit, following):
                    if following:
                        shifted(following, 0)
                    copy_odd(unit, 1)
                    if following:
                        shifted(following, 1)
                        shifted(following, 2)
                    copy_odd(unit, 3)
                    if following:
                        shifted(following, 3)
                    normalised(unit)

                for b in range(NB):
                    shifted((kinds[0][0], kinds[0][2], 0, 0), b)
                in_pairs(dve, kinds, body, step, [2 if kind in ("dil", "mla") else 4 for kind, _, _ in kinds])

            def turn(v):
                for t in range(KT):
                    dve.wait_ge(sem("turn_high"), KT * v + t + 1)
                    dve.scalar_tensor_tensor(xl[:, t, :], bank[2 + t % 6][:, :], col("one_scale" if v else "subln", t),
                                             xh[:, t, :].bitcast(F32), ALU.mult, ALU.subtract)\
                       .then_inc(sem("turn_read"), 1)

            for t in range(1, KT):
                dve.wait_ge(sem("x_square"), t + 1)
                step(dve.tensor_tensor(tmpb[:, 0, :], tmpb[:, 0, :] if t > 1 else qk[:, 0, :], qk[:, t, :], ALU.add))
            dve.sem_inc(sem("squares_ready"), 1)
            dve.wait_ge(params_landed, 2 * 16)
            norm(0, "norm_mix", 0)
            dve.wait_ge(sem("table_mm"), 1)
            dve.wait_ge(inputs_landed, 4 * 16)
            for j in range(2):
                c = slice(j * TW // 2, (j + 1) * TW // 2)
                dve.tensor_tensor(tt[:, c], bank[5 + j][0:ROWS, 0:TW // 2], ad[:, c], ALU.add)\
                   .then_inc(sem("table_read"), 1)
            dve.wait_ge(sem("table_read"), 2)
            dve.sem_inc(table_ready, 1)
            dve.wait_ge(sem("qk_sum"), 1)
            dve.tensor_scalar(rstd[0:16, :], bank[4][0:16, :], 1.0 / P, EPS, ALU.mult, ALU.add)\
               .then_inc(sem("qk_var"), 1)
            dve.wait_ge(sem("qk_std"), 1)
            step(dve.reciprocal(rstd[0:16, :], rstd[0:16, :]))
            step(dve.tensor_copy(qkrstd[:, 0, :], rstd[0:16, :]))
            dve.tensor_tensor(qkrstd[:, 1, :], rstd[0:16, :], qkrstd[:, 0, :].bitcast(F32), ALU.subtract)\
               .then_inc(sem("qk_rstd"), 1)
            lam_col = col("lru_lambda", 0, 8)
            for k in range(2):
                step(dve.tensor_tensor(tmpa[:, 0, 0:64], lamb[:, 2 * k, :], lamb[:, 2 * k + 1, :], ALU.mult))
                dve.tensor_reduce(lam2[:, k:k + 1], tmpa[:, 0, 0:64], AX.X, ALU.add).then_inc(sem("lambda_sums"), 1)
                dve.wait_ge(sem("lambda_sums"), k + 1)
            step(dve.tensor_scalar(col("qk_norm", 0, 8), col("qk_norm", 0, 8), 128 ** -0.5, None, ALU.mult))
            step(dve.tensor_tensor(col("subln", 0, 8), col("subln", 0, 8), col("subln_factor", 0, 8), ALU.mult))
            dve.wait_ge(sem("lambda_exp"), 2)
            step(dve.tensor_scalar(t2, t1, 2.0, None, ALU.add))
            step(dve.reciprocal(t2, t2))
            step(dve.tensor_tensor(t1, t1, t2, ALU.mult))
            step(dve.tensor_tensor(t2, t1, t1, ALU.mult))
            step(dve.tensor_scalar(t3, t2, 1.0 / 15, None, ALU.mult))
            for k in (13, 11, 9, 7, 5, 3):
                step(dve.scalar_tensor_tensor(t3, t3, 1.0 / k, t2, ALU.add, ALU.mult))
            step(dve.scalar_tensor_tensor(t3, t3, 1.0, t1, ALU.add, ALU.mult))
            step(dve.tensor_scalar(t4, lam_col, -1.0, 0.0, ALU.mult, ALU.max))
            step(dve.scalar_tensor_tensor(t3, t3, 2.0, t4, ALU.mult, ALU.add))
            step(dve.tensor_scalar(decay8, t3, 8.0, None, ALU.mult))
            step(dve.tensor_scalar(ndecay8, t3, -8.0, None, ALU.mult))
            step(dve.tensor_tensor(nlam, lam2[:, 1:2], lam2[:, 0:1], ALU.subtract))
            step(dve.tensor_scalar(nlam, nlam, -LAM_INIT, None, ALU.add))
            for t in range(16):
                dve.wait_ge(sem("qk_spread"), t + 1)
                dve.scalar_tensor_tensor(qk[:, t, :], qk[:, t, :], col("qk_norm", t), bank[t % 4][:, :], ALU.mult,
                                         ALU.mult).then_inc(sem("qk_normed"), 1)
            for i in repeat(dve, 4, step, 6):
                for c in range(2):
                    for j, w in enumerate((S, S, 2 * P)):
                        dve.wait_ge(sem("ln_ready"), i * 6 + (3 * c + j + 1))
                        last = dve.scalar_tensor_tensor(sp[:, c, j, 0:w], bank[3 * c + j][:, 0:w], 0.0,
                                                        sp[:, c, j, 0:w], ALU.max, ALU.add)
                    step(last)
                    for d in (sp[:, c, :, 0:P], sp[:, c, 1:2, 3 * P:S]):
                        last = dve.tensor_tensor(d, d, mask01.unsqueeze(1).to_broadcast([P, d.shape[1], P]),
                                                 ALU.mult)
                    step(last)
                    parts = [(t[:, c, 0:2, :], t[:, c, 2:3, 0:2 * P]) for t in (sp, sph, spl)]
                    for x, high, _ in zip(*parts):
                        last = dve.tensor_copy(high, x)
                    step(last)
                    for x, high, low in zip(*parts):
                        dve.tensor_tensor(low, x, high.bitcast(F32), ALU.subtract).then_inc(sem("sp_ready"), 1)
            for t in range(KT):
                dve.wait_ge(sem("yh0_ready"), t + 1)
                dve.tensor_tensor(yl[:, t, :], qk[:, t, :], yh[:, t, :].bitcast(F32), ALU.subtract)\
                   .then_inc(sem("yl0_ready"), 1)
            products("gate2", True, "g2_ready", "g2_gate", "g2_prod")
            for b in range(2):
                for t in (pu, pa):
                    dve.memset(t[:, b, 0:16], 0.0).then_inc(sem("pads_ready"), 1)
            dve.wait_ge(sem("pads_ready"), 4)
            for t in range(KT):
                g, b = t // 2, t % 2
                w = WINDOWS[g]
                dve.wait_ge(sem("pool_read"), t + 5)
                src, dst, shift = pu[:, b, :], pa[:, 0, :], 1
                for n in range(g + 1):
                    step(dve.tensor_tensor(dst[:, 16:16 + S], src[:, 16:16 + S], src[:, 16 - shift:16 + S - shift],
                                           ALU.add))
                    src, dst, shift = dst, pa[:, 1 - n % 2, :], shift * 2
                step(dve.tensor_tensor(src[:, 16:32], src[:, 16:32], col("edge", 16 * g, 16), ALU.mult))
                dve.scalar_tensor_tensor(tmpb[:, b, :], src[:, 16:16 + S], 1.0 / w, pu[:, b, 16:16 + S], ALU.mult,
                                         ALU.subtract).then_inc(sem("p_ready_value"), 1)
                dve.wait_ge(sem("p_high"), t + 1)
                dve.tensor_tensor(yl[:, t, :], tmpb[:, b, :], yh[:, t, :].bitcast(F32), ALU.subtract)\
                   .then_inc(sem("p_low"), 1)
            for t in range(KT):
                dve.wait_ge(sem("wpool_high"), t + 1)
                dve.scalar_tensor_tensor(yl[:, t, :], bank[t % 4][:, :], col("pool_scale", t),
                                         yh[:, t, :].bitcast(F32), ALU.mult, ALU.subtract)\
                   .then_inc(sem("wpool_low"), 1)
            dve.wait_ge(sem("g2_prod"), 10)
            products("gate0", False, "g0_ready", "g0_gate", "g0_prod")
            def lru_convolution(t):
                x = xc[:, t, :]
                dve.wait_ge(sem("lru_base"), t + 1)
                for k in (1, 2, 3):
                    dve.scalar_tensor_tensor(x[:, k:S], bank[t % 4][:, 0:S - k], col("conv_w", 8 * (3 - k) + t),
                                             x[:, k:S], ALU.mult, ALU.add).then_inc(sem("lru_conv"), 1)
                    dve.wait_ge(sem("lru_conv"), 3 * t + k)

            def lru_multipliers(tiles):
                for t in tiles:
                    dve.wait_ge(sem("lru_a"), t + 1)
                    dve.tensor_tensor(tmpa[:, t % 2, :], rr[:, t, :], rr[:, t, :], ALU.mult)\
                       .then_inc(sem("lru_m2"), 1)
                    dve.wait_ge(sem("lru_m2"), 2 * t + 1)
                    dve.scalar_tensor_tensor(tanh[:, t % 4, :], tmpa[:, t % 2, :], 1.0, tanh[:, t % 4, :], ALU.add,
                                             ALU.mult).then_inc(sem("lru_m2"), 1)

            def lru_lows(tiles):
                for t in tiles:
                    dve.wait_ge(sem("lru_high"), t + 1)
                    dve.tensor_tensor(yl[:, t, :], xc[:, t, :], yh[:, t, :].bitcast(F32), ALU.subtract)\
                       .then_inc(sem("lru_low"), 1)

            def lru_scans(tiles):
                for t in tiles:
                    x = ii[:, t, :]
                    dve.tensor_tensor(x, x, xc[:, t, :], ALU.mult).then_inc(sem("lru_h"), 1)
                    dve.wait_ge(sem("lru_mult"), t + 1)
                    dve.wait_ge(sem("lru_h"), 3 * t + 1)
                    dve.tensor_tensor(x, x, tanh[:, t % 4, :], ALU.mult).then_inc(sem("lru_h"), 1)
                    dve.wait_ge(sem("lru_h"), 3 * t + 2)
                    dve.tensor_tensor_scan(xc[:, t, :], rr[:, t, :], x, 0.0, ALU.mult, ALU.add)\
                       .then_inc(sem("lru_h"), 1)

            for t in range(KT):
                lru_convolution(t)
                if t == 4:
                    lru_multipliers((0, 1, 2, 3))
                if t == 5:
                    lru_scans((0, 1))
                if t == 6:
                    lru_lows((0, 1))
            lru_scans((2, 3))
            lru_multipliers((4, 5, 6))
            lru_scans((4, 5, 6))
            lru_lows((2, 3, 4, 5, 6))
            lru_multipliers((7,))
            lru_scans((7,))
            lru_lows((7,))
            products("gate1", False, "g1_ready", "g1_gate", "g1_prod")
            for t in range(KT):
                dve.sem_inc(sem("merged_ready"), 1)
            for t in range(KT):
                dve.wait_ge(sem("yh1_ready"), t + 1)
                dve.tensor_tensor(yl[:, t, :], merged[:, t, :], yh[:, t, :].bitcast(F32), ALU.subtract)\
                   .then_inc(sem("yl1_ready"), 1)
            residual(4, "out_ready", "out_read", 1)
            ffn(0, 1, "norm_ffn", 0)
            norm(2, "even_norm", 0)
            attend(("diff", 4, 0), ("moba", 4, 8))
            dve.tensor_scalar(dss, dss, 1.0 / P, EPS, ALU.mult, ALU.add).then_inc(sem("diff_var"), 1)
            dve.wait_ge(sem("diff_std"), 1)
            step(dve.reciprocal(dss, dss))
            for h in range(4):
                y = yt[:, :, (4 + h) * P:(5 + h) * P]
                dve.tensor_tensor(y, y, dss[:, :, h:h + 1].to_broadcast([P, NB, P]), ALU.mult)\
                   .then_inc(sem("y_token"), 1)
            turn(0)
            residual(4, "eo_ready", "eo_read", 1)
            ffn(1, 3, "ffn_norm", 0)
            norm(4, "odd_norm", 0)
            dve.wait_ge(sem("c_sum"), 3)
            for t in range(2):
                dve.tensor_scalar(tmpa[:, t, :], bank[6 + t][:, :], 1.0 / (2 * P, P)[t], EPS, ALU.mult, ALU.add)\
                   .then_inc(sem("c_var"), 1)
            for t in range(2):
                dve.wait_ge(sem("c_std"), t + 1)
                step(dve.reciprocal(tmpa[:, t, :], tmpa[:, t, :]))
            for t in range(3):
                c = qk[:, 8 + t, :]
                gain = col("mla_q_norm", t) if t < 2 else col("mla_kv_norm", 0)
                dve.scalar_tensor_tensor(c, c, gain, tmpa[:, t // 2, :], ALU.mult, ALU.mult)\
                   .then_inc(sem("c_normed"), 1)
            for t in range(3):
                dve.wait_ge(sem("ch_ready"), t + 1)
                dve.tensor_tensor(cl[t], qk[:, 8 + t, :], ch[t].bitcast(F32), ALU.subtract)\
                   .then_inc(sem("cl_ready"), 1)
            attend(("dil", 4, 16),)
            dve.wait_ge(sem("rope_landed"), 16)
            for n, t in enumerate((11, 12, 13)):
                x = qk[:, t, :]
                dve.wait_ge(sem("rotated"), n + 1)
                step(dve.tensor_tensor(tmpb[:, 0, :], bank[4 + n][:, :], rope[:, 1, :], ALU.mult))
                step(dve.tensor_tensor(x, x, rope[:, 0, :], ALU.mult))
                dve.tensor_tensor(x, x, tmpb[:, 0, :], ALU.add).then_inc(sem("roped"), 1)
                dve.wait_ge(sem("roped"), n + 1)
            attend(("mla", 2, 24),)
            turn(1)
            residual(4, "oo_ready", "oo_read", 1)
            ffn(2, 5, "ffn_norm", 8)
            norm(6, "final", 0)


def _chunk(w):
    k = w.shape[0] // P
    out = np.zeros((P, CHUNK), w.dtype)
    out[:, 0:k * w.shape[1]] = w.reshape(k, P, w.shape[1]).transpose(1, 0, 2).reshape(P, -1)
    return out


def _chunks(w):
    return [_chunk(w[:, c:c + 2 * P]) for c in range(0, w.shape[1], 2 * P)]


def _pairs(a, b):
    return [c for pair in zip(_chunks(a), _chunks(b)) for c in pair]


def _downs(w):
    return [w[h * DOWN:(h + 1) * DOWN, t * P:(t + 1) * P].reshape(HALF, P, P).transpose(1, 0, 2).reshape(P, DOWN)
            for t in range(KT) for h in range(2)]


def _columns(v):
    return np.asarray(v).reshape(-1, P).T


def _bucket(distance):
    n = np.maximum(distance, 0)
    f = np.maximum(n, 1).astype(np.float32)
    large = 16 + (np.log(f / np.float32(16)) / np.float32(math.log(1024 / 16)) * np.float32(16)).astype(np.int32)
    return np.where(n < 16, n, np.minimum(large, 31))


def _constants():
    p = np.arange(P)
    upper = (p[None, :] > p[:, None]).astype(np.float32)
    rot = np.zeros((P, P), np.float32)
    for h in (0, 64):
        for j in range(32):
            rot[h + 32 + j, h + j] = -1.0
            rot[h + j, h + 32 + j] = 1.0
    mats = np.stack([np.ones((P, P)), np.eye(P), -(p[:, None] >= p[None, :]).astype(np.float32),
                     -np.ones((P, P)), np.where(upper > 0, 0.0, NEG), upper, rot, np.tile(p == 15, (P, 1))], axis=1).astype(np.float32)
    freq = (np.float32(10000.0) ** (-np.arange(32, dtype=np.float32) / np.float32(32))).astype(np.float32)
    angle = (np.arange(S, dtype=np.float32)[None, :] * freq[:, None]).astype(np.float32)
    rope = np.stack([np.tile(np.cos(angle), (4, 1)), np.tile(np.sin(angle), (4, 1))], axis=1).astype(np.float32)
    distance = np.arange(TW) - (P - 1)
    onehot = ((_bucket(distance)[None, :] == np.arange(32)[:, None]) & (distance >= 0)).astype(np.float32)
    causal = np.where(distance >= 0, 0.0, NEG)
    count = (distance <= 128).astype(int) + (distance % 4 == 0) + (distance % 16 == 0)
    dilated = np.where((distance >= 0) & (count > 0), np.log(np.maximum(count, 1)), NEG)
    add = np.stack([causal] * 12 + [dilated] * 8 + [causal]).astype(np.float32)
    edge = np.ones((P, 64), np.float32)
    for g, w in enumerate(WINDOWS):
        edge[:, 16 * g:16 * g + 16] = w / np.minimum(np.arange(1, 17), w)
    return mats, rope, onehot, add, edge


def _layout(x, norm_mix, w_in, b_gate, w_pool, pool_scale, conv_w, conv_b, w_rg, b_rg, w_ig, b_ig, lru_lambda,
            q_norm, k_norm, w_branch, w_out, norm_ffn, w_ffn_gate, w_ffn_up, w_ffn_down, rel_bias_2, even_norm1_2,
            even_w_in_2, diff_lambda_2, diff_subln_2, even_w_out_2, odd_norm1_2, odd_w_in_2, mla_q_norm_2,
            mla_w_uq_2, mla_kv_norm_2, mla_w_ukv_2, odd_w_out_2, ffn_norm_2, ffn_w_in_2, ffn_conv_w_2,
            ffn_conv_b_2, ffn_w_out_2, final_norm_2):
    wi, wb = w_in[0], w_branch[0]
    ev, od = even_w_in_2[0], odd_w_in_2[0]
    gate = [wi[:, 5 * D + b * D:5 * D + (b + 1) * D] for b in range(3)]
    ffn = lambda l: _pairs(ffn_w_in_2[l][:, FF:], ffn_w_in_2[l][:, :FF])
    uq = mla_w_uq_2[0].reshape(2 * P, 4, 192)
    uq = np.concatenate([uq[:, :, :P].reshape(2 * P, -1), uq[:, :, P:].reshape(2 * P, -1)], axis=1)
    ukv = mla_w_ukv_2[0].reshape(P, 4, 2 * P)
    ukv = np.concatenate([ukv[:, :, :P].reshape(P, -1), ukv[:, :, P:].reshape(P, -1)], axis=1)
    wp = w_pool[0].reshape(4, 2, P, 2 * P).transpose(2, 0, 1, 3).reshape(P, 2, CHUNK // 2)
    wpool = [np.concatenate([wp[:, c], np.zeros_like(wp[:, c])], axis=1) for c in range(2)]
    ckv = np.concatenate([od[:, 1792:1920], od[:, 1920:1984], od[:, 1920:1984]], axis=1)
    main = (_chunks(wi[:, 2 * D:4 * D]) + _chunks(wi[:, 4 * D:5 * D]) + _pairs(gate[2], wb[2])
            + _chunks(wi[:, 0:D]) + wpool + _pairs(gate[0], wb[0]) + _chunks(wi[:, D:2 * D]) + _pairs(gate[1], wb[1])
            + _chunks(w_out[0]) + _pairs(w_ffn_gate[0], w_ffn_up[0])
            + _chunks(ev[:, 0:1024]) + _chunks(ev[:, 1536:2560])
            + _chunks(ev[:, 1024:1536]) + _chunks(ev[:, 2560:3072]) + _chunks(even_w_out_2[0]) + ffn(0)
            + _chunks(od[:, 0:1024]) + _chunks(od[:, 1536:1792]) + _chunks(ckv) + _chunks(od[:, 1024:1536])
            + [_chunk(uq), _chunk(ukv)] + _chunks(odd_w_out_2[0]) + ffn(1))
    assert len(main) == MAIN, (len(main), MAIN)
    downs = _downs(w_ffn_down[0]) + _downs(ffn_w_out_2[0]) + _downs(ffn_w_out_2[1])
    mats, rope, onehot, add, edge = _constants()
    one = np.ones((P, 1), np.float32)
    eighth = 0.125 * one
    cols = [_columns(v) for v in (norm_mix, b_gate, pool_scale, conv_w, conv_b, b_rg, b_ig, lru_lambda)]
    cols += [_columns(q_norm)] * 8 + [_columns(k_norm)] * 8
    cols += [_columns(v) for v in (norm_ffn, even_norm1_2, odd_norm1_2, mla_q_norm_2, mla_kv_norm_2, ffn_norm_2,
                                   final_norm_2, ffn_conv_b_2, ffn_conv_w_2)]
    cols += [one] * 4 + [_columns(diff_subln_2)] * 4
    cols += [one] * 16 + ([eighth] * 4 + [one] * 4) * 2 + [eighth] * 4 + [one] * 8
    cols += [one] * 4 + [(1.0 - LAM_INIT) * one] * 4 + [edge]
    cols = np.ascontiguousarray(np.concatenate(cols, axis=1), dtype=np.float32)
    assert cols.shape == (P, NCOL), (cols.shape, NCOL)
    rg = np.zeros((P, 16, P), np.float32)
    for k, w in enumerate((w_rg[0], w_ig[0])):
        for t in range(KT):
            rg[0:64, 8 * k + t, 0:64] = w[2 * t]
            rg[64:P, 8 * k + t, 64:P] = w[2 * t + 1]
    rel = np.zeros((32, ROWS + 3), np.float32)
    rel[:, 0:20] = rel_bias_2
    return {
        "wmain": np.stack(main), "wdown": np.stack(downs),
        "x": np.ascontiguousarray(x[0].T.reshape(KT, P, S).transpose(1, 0, 2)),
        "cols": cols, "mats": np.ascontiguousarray(mats), "rg": rg, "rope": np.ascontiguousarray(rope),
        "onehot": onehot, "add": add, "rel": rel,
        "lam": np.ascontiguousarray(np.broadcast_to(diff_lambda_2[0][None], (P, 4, 64))),
    }


def kernel(**inputs):
    import concourse.bacc as bacc
    from concourse.bass_utils import run_bass_kernel_spmd

    arrays = _layout(**{k: np.asarray(v) for k, v in inputs.items()})
    nc = bacc.Bacc("TRN2", target_bir_lowering=False, num_devices=1)
    args = [nc.dram_tensor(n, a.shape, F32, kind="ExternalInput").ap() for n, a in arrays.items()]
    out = nc.dram_tensor("out", (P, KT, S), F32, kind="ExternalOutput").ap()
    table = nc.dram_tensor("distance_table", (ROWS, TW), F32, kind="Internal").ap()
    program(nc, *args, out, table)
    r = run_bass_kernel_spmd(nc, [arrays], core_ids=[0])
    y = r.results[0]["out"]
    return np.ascontiguousarray(y.transpose(1, 0, 2).reshape(D, S).T)[None]
```
